# Optimizing a Trainium2 kernel written in Bass

```python
import jax, jax.numpy as jnp
from jax import lax
import numpy as np

D_MODEL = 1024
BATCH = 1
SEQ = 256
DEPTH = 2

N_BRANCH = 4
HEAD_DIM = 64
BRANCH_WIDTH = D_MODEL // N_BRANCH
N_HEADS = BRANCH_WIDTH // HEAD_DIM
NORM_EPS = 1e-6
RW_DECAY_LORA = 64
RW_AAA_LORA = 64
RW_GATE_LORA = 128
RW_DECAY_SCALE = 0.606531
RW_LN_EPS = 64e-5
SB_BLOCK = 128
RET_CHUNK = 128
RET_GN_EPS = 1e-5
ROPE_BASE = 10000.0
CONV_WIDTH = 31
CONV_LN_EPS = 1e-5
D_FF = 2816
N_EXPERTS = 8
TOP_K = 2
D_FF_EXPERT = 1408
MOE_BLOCK = 256

RW_IN = 3 * BRANCH_WIDTH + RW_DECAY_LORA + RW_AAA_LORA + RW_GATE_LORA
SB_IN = 3 * BRANCH_WIDTH
RET_IN = 4 * BRANCH_WIDTH
CONV_IN = 2 * BRANCH_WIDTH
N_IN = RW_IN + SB_IN + RET_IN + CONV_IN
MIX_SPLITS = [RW_IN, RW_IN + SB_IN, RW_IN + SB_IN + RET_IN]
RW_SPLITS = [BRANCH_WIDTH, 2 * BRANCH_WIDTH, 3 * BRANCH_WIDTH,
             3 * BRANCH_WIDTH + RW_DECAY_LORA, 3 * BRANCH_WIDTH + RW_DECAY_LORA + RW_AAA_LORA]


def _rmsnorm(x, gain, eps=NORM_EPS):
    x32 = x.astype(jnp.float32)
    y = x32 * lax.rsqrt(jnp.mean(x32 * x32, axis=-1, keepdims=True) + eps)
    return (y * gain).astype(x.dtype)

def _layernorm(x, gain, bias, eps):
    x32 = x.astype(jnp.float32)
    xc = x32 - jnp.mean(x32, axis=-1, keepdims=True)
    var = jnp.mean(xc * xc, axis=-1, keepdims=True)
    return (xc * lax.rsqrt(var + eps) * gain + bias).astype(x.dtype)

def _token_shift(x):
    return jnp.pad(x, ((0, 0), (1, 0), (0, 0)))[:, :-1]

def _split_heads(t):
    return t.reshape(t.shape[0], t.shape[1], N_HEADS, HEAD_DIM)

def _rwkv7_mixer(p, mu, w0, w2, a0, a2, g2, k_k, k_a, r_k, ln_w, ln_b):
    B, S, _ = p.shape
    p = p + (_token_shift(p) - p) * mu
    r, k, v, pw, pa, pg = jnp.split(p, RW_SPLITS, axis=-1)
    w = jnp.exp(-RW_DECAY_SCALE * jax.nn.sigmoid((w0 + jnp.tanh(pw) @ w2).astype(jnp.float32)))
    a = jax.nn.sigmoid(a0 + pa @ a2)
    g = jax.nn.sigmoid(pg) @ g2
    r, k, v, w, a = (_split_heads(t) for t in (r, k, v, w, a))
    kk32 = (k * k_k.reshape(N_HEADS, HEAD_DIM)).astype(jnp.float32)
    kk = kk32 / jnp.maximum(jnp.sqrt(jnp.sum(kk32 * kk32, axis=-1, keepdims=True)), 1e-12)
    k = k * (1.0 + (a - 1.0) * k_a.reshape(N_HEADS, HEAD_DIM))

    def step(state, inp):
        r_t, w_t, k_t, v_t, kk_t, a_t = inp
        sa = jnp.einsum('bhvk,bhk->bhv', state, -kk_t)
        state = (state * w_t[:, :, None, :] + sa[..., None] * (kk_t * a_t)[:, :, None, :]
                 + v_t[..., None] * k_t[:, :, None, :])
        return state, jnp.einsum('bhvk,bhk->bhv', state, r_t)

    seq_first = lambda t: jnp.moveaxis(t.astype(jnp.float32), 1, 0)
    state0 = jnp.zeros((B, N_HEADS, HEAD_DIM, HEAD_DIM), jnp.float32)
    _, y = lax.scan(step, state0, tuple(seq_first(t) for t in (r, w, k, v, kk, a)))
    y = jnp.moveaxis(y, 0, 1)
    y = _layernorm(y, ln_w.reshape(N_HEADS, HEAD_DIM), ln_b.reshape(N_HEADS, HEAD_DIM), RW_LN_EPS)
    y = y + jnp.sum(r * k * r_k, axis=-1, keepdims=True) * v
    return (y.reshape(B, S, BRANCH_WIDTH) * g).astype(p.dtype)

def _stick_breaking_mixer(p, q_norm, k_norm):
    B, S, _ = p.shape
    nb = S // SB_BLOCK
    blocks = lambda t: _split_heads(t).reshape(B, nb, SB_BLOCK, N_HEADS, HEAD_DIM).transpose(0, 3, 1, 2, 4)
    q, k, v = (blocks(t) for t in jnp.split(p, 3, axis=-1))
    q = _rmsnorm(q, q_norm) * (HEAD_DIM ** -0.5)
    k = _rmsnorm(k, k_norm)
    idx = jnp.arange(SB_BLOCK)
    rev_incl = (idx[:, None] >= idx[None, :]).astype(jnp.float32)
    diag_mask = idx[None, :] < idx[:, None]
    acc = jnp.zeros((B, N_HEADS, nb, SB_BLOCK), jnp.float32)
    o = jnp.zeros((B, N_HEADS, nb, SB_BLOCK, HEAD_DIM), jnp.float32)
    for d in range(nb):
        n = nb - d
        z = jnp.einsum('bhnqd,bhnkd->bhnqk', q[:, :, d:], k[:, :, :n]).astype(jnp.float32)
        ls = jax.nn.log_sigmoid(-z)
        if d == 0:
            ls = jnp.where(diag_mask, ls, 0.0)
        cum = jnp.einsum('bhnqk,kj->bhnqj', ls, rev_incl)
        log_a = z + cum + acc[:, :, d:, :, None]
        if d == 0:
            log_a = jnp.where(diag_mask, log_a, -jnp.inf)
        attn = jnp.exp(log_a)
        o = o.at[:, :, d:].add(jnp.einsum('bhnqk,bhnkd->bhnqd', attn.astype(v.dtype), v[:, :, :n]).astype(jnp.float32))
        acc = acc.at[:, :, d:].add(cum[..., 0])
    return o.transpose(0, 2, 3, 1, 4).reshape(B, S, BRANCH_WIDTH).astype(p.dtype)

def _rotary(t):
    S = t.shape[1]
    inv_freq = ROPE_BASE ** (-jnp.arange(0, HEAD_DIM, 2, dtype=jnp.float32) / HEAD_DIM)
    ang = jnp.arange(S, dtype=jnp.float32)[:, None] * inv_freq[None, :]
    cos = jnp.cos(ang)[None, :, None, :].astype(t.dtype)
    sin = jnp.sin(ang)[None, :, None, :].astype(t.dtype)
    t1, t2 = jnp.split(t, 2, axis=-1)
    return jnp.concatenate([t1 * cos - t2 * sin, t1 * sin + t2 * cos], axis=-1)

def _retention_mixer(p, gn_w):
    B, S, _ = p.shape
    dt = p.dtype
    q, k, v, gt = jnp.split(p, 4, axis=-1)
    q = _rotary(_split_heads(q))
    k = _rotary(_split_heads(k)) * (HEAD_DIM ** -0.5)
    v = _split_heads(v)
    nc = S // RET_CHUNK
    chunk = lambda t: t.reshape(B, nc, RET_CHUNK, N_HEADS, HEAD_DIM).transpose(0, 3, 1, 2, 4)
    qc, kc, vc = chunk(q), chunk(k), chunk(v)
    log_gamma = jnp.log(1.0 - 2.0 ** (-5.0 - jnp.arange(N_HEADS, dtype=jnp.float32)))
    idx = jnp.arange(RET_CHUNK, dtype=jnp.float32)
    rel = idx[:, None] - idx[None, :]
    intra_decay = jnp.where(rel >= 0, jnp.exp(jnp.maximum(rel, 0.0) * log_gamma[:, None, None]), 0.0)
    k_decay = jnp.exp((RET_CHUNK - 1 - idx)[None, :] * log_gamma[:, None])
    q_decay = jnp.exp((idx + 1.0)[None, :] * log_gamma[:, None])
    chunk_decay = jnp.exp(RET_CHUNK * log_gamma)
    scores = jnp.einsum('bhcqd,bhckd->bhcqk', qc, kc) * intra_decay[None, :, None].astype(dt)
    intra = jnp.einsum('bhcqk,bhckd->bhcqd', scores, vc)
    kv = jnp.einsum('bhckd,bhcke->cbhde', kc * k_decay[None, :, None, :, None].astype(dt), vc)

    def step(state, kv_c):
        return chunk_decay[None, :, None, None] * state + kv_c, state

    _, state_prev = lax.scan(step, jnp.zeros(kv.shape[1:], jnp.float32), kv.astype(jnp.float32))
    inter = jnp.einsum('bhcqd,cbhde->bhcqe', qc * q_decay[None, :, None, :, None].astype(dt),
                       state_prev.astype(dt))
    o = (intra + inter).transpose(0, 2, 3, 1, 4).reshape(B, S, N_HEADS, HEAD_DIM)
    o = _layernorm(o, gn_w.reshape(N_HEADS, HEAD_DIM), 0.0, RET_GN_EPS)
    return o.reshape(B, S, BRANCH_WIDTH) * jax.nn.silu(gt)

def _conformer_conv_mixer(p, dw, db, ln_w, ln_b):
    u_a, u_b = jnp.split(p, 2, axis=-1)
    u = u_a * jax.nn.sigmoid(u_b)
    u = lax.conv_general_dilated(u, dw[:, None, :].astype(u.dtype), window_strides=(1,),
                                 padding=[(CONV_WIDTH - 1, 0)],
                                 dimension_numbers=('NWC', 'WIO', 'NWC'),
                                 feature_group_count=BRANCH_WIDTH) + db
    return jax.nn.silu(_layernorm(u, ln_w, ln_b, CONV_LN_EPS))

def _swiglu(h, w1, w3, w2):
    return (jax.nn.silu(h @ w1) * (h @ w3)) @ w2

def _moe_ffn(h, router, w1, w3, w2):
    B, S, D = h.shape
    T = B * S
    xt = h.reshape(T, D)
    logits = (xt @ router).astype(jnp.float32)
    top_logit, top_idx = lax.top_k(logits, TOP_K)
    gates = jax.nn.softmax(top_logit, axis=-1)
    n_assign = T * TOP_K
    expert = top_idx.reshape(-1)
    token = jnp.arange(n_assign) // TOP_K
    order = jnp.argsort(expert)
    expert_s, token_s, weight_s = expert[order], token[order], gates.reshape(-1)[order]
    x_s = xt[token_s]
    counts = jnp.bincount(expert, length=N_EXPERTS)
    n_blk = n_assign // MOE_BLOCK
    seg_start = jnp.sort(jnp.concatenate([jnp.arange(n_blk) * MOE_BLOCK, jnp.cumsum(counts)[:-1]]))
    seg_end = jnp.concatenate([seg_start[1:], jnp.array([n_assign], seg_start.dtype)])
    seg_blk = jnp.minimum(seg_start // MOE_BLOCK, n_blk - 1)
    seg_exp = expert_s[jnp.minimum(seg_start, n_assign - 1)]

    def segment(args):
        start, end, blk, e = args
        rows = blk * MOE_BLOCK + jnp.arange(MOE_BLOCK)
        xb = lax.dynamic_slice_in_dim(x_s, blk * MOE_BLOCK, MOE_BLOCK, axis=0)
        yb = _swiglu(xb, w1[e], w3[e], w2[e])
        return jnp.where(((rows >= start) & (rows < end))[:, None], yb, 0.0)

    y_seg = lax.map(segment, (seg_start, seg_end, seg_blk, seg_exp))
    y_s = jax.ops.segment_sum(y_seg, seg_blk, num_segments=n_blk).reshape(n_assign, D)
    out = jax.ops.segment_sum(y_s * weight_s[:, None].astype(y_s.dtype), token_s, num_segments=T)
    return out.reshape(B, S, D)

def first_inputs(seed: int = 0) -> dict:
    key = jax.random.key(seed)
    ks = iter(jax.random.split(key, 40))
    nrm = lambda shape, scale: scale * jax.random.normal(next(ks), shape, jnp.float32)
    L, C = DEPTH, BRANCH_WIDTH
    nd, nm = (DEPTH + 1) // 2, DEPTH // 2
    return {
        "x": nrm((BATCH, SEQ, D_MODEL), 1.0),
        "norm_mix": 1.0 + nrm((L, D_MODEL), 0.1),
        "w_in": nrm((L, D_MODEL, N_IN), D_MODEL ** -0.5),
        "rw_mu": jax.random.uniform(next(ks), (L, RW_IN), jnp.float32),
        "rw_w0": -1.5 + nrm((L, C), 0.5),
        "rw_w2": nrm((L, RW_DECAY_LORA, C), 0.5 * RW_DECAY_LORA ** -0.5),
        "rw_a0": nrm((L, C), 0.5),
        "rw_a2": nrm((L, RW_AAA_LORA, C), RW_AAA_LORA ** -0.5),
        "rw_g2": nrm((L, RW_GATE_LORA, C), RW_GATE_LORA ** -0.5),
        "rw_k_k": 0.85 + nrm((L, C), 0.1),
        "rw_k_a": 1.0 + nrm((L, C), 0.1),
        "rw_r_k": nrm((L, N_HEADS, HEAD_DIM), 0.1),
        "rw_ln_w": 1.0 + nrm((L, C), 0.1),
        "rw_ln_b": nrm((L, C), 0.01),
        "sb_q_norm": 1.0 + nrm((L, HEAD_DIM), 0.1),
        "sb_k_norm": 1.0 + nrm((L, HEAD_DIM), 0.1),
        "ret_gn": 1.0 + nrm((L, C), 0.1),
        "conv_dw": nrm((L, CONV_WIDTH, C), CONV_WIDTH ** -0.5),
        "conv_b": nrm((L, C), 0.01),
        "conv_ln_w": 1.0 + nrm((L, C), 0.1),
        "conv_ln_b": nrm((L, C), 0.01),
        "w_gate": nrm((L, N_BRANCH, D_MODEL, D_MODEL), D_MODEL ** -0.5),
        "w_branch": nrm((L, N_BRANCH, C, D_MODEL), C ** -0.5),
        "w_out": nrm((L, D_MODEL, D_MODEL), 0.5 * D_MODEL ** -0.5),
        "norm_ffn": 1.0 + nrm((L, D_MODEL), 0.1),
        "ffn_w1": nrm((nd, D_MODEL, D_FF), D_MODEL ** -0.5),
        "ffn_w3": nrm((nd, D_MODEL, D_FF), D_MODEL ** -0.5),
        "ffn_w2": nrm((nd, D_FF, D_MODEL), 0.5 * D_FF ** -0.5),
        "router": nrm((nm, D_MODEL, N_EXPERTS), D_MODEL ** -0.5),
        "moe_w1": nrm((nm, N_EXPERTS, D_MODEL, D_FF_EXPERT), D_MODEL ** -0.5),
        "moe_w3": nrm((nm, N_EXPERTS, D_MODEL, D_FF_EXPERT), D_MODEL ** -0.5),
        "moe_w2": nrm((nm, N_EXPERTS, D_FF_EXPERT, D_MODEL), 0.5 * D_FF_EXPERT ** -0.5),
    }

def first_block(x, norm_mix, w_in, rw_mu, rw_w0, rw_w2, rw_a0, rw_a2, rw_g2, rw_k_k, rw_k_a, rw_r_k,
              rw_ln_w, rw_ln_b, sb_q_norm, sb_k_norm, ret_gn, conv_dw, conv_b, conv_ln_w, conv_ln_b,
              w_gate, w_branch, w_out, norm_ffn, ffn_w1, ffn_w3, ffn_w2, router, moe_w1, moe_w3, moe_w2):
    for l in range(DEPTH):
        h = _rmsnorm(x, norm_mix[l])
        p_rw, p_sb, p_ret, p_conv = jnp.split(h @ w_in[l], MIX_SPLITS, axis=-1)
        branches = (
            _rwkv7_mixer(p_rw, rw_mu[l], rw_w0[l], rw_w2[l], rw_a0[l], rw_a2[l], rw_g2[l],
                         rw_k_k[l], rw_k_a[l], rw_r_k[l], rw_ln_w[l], rw_ln_b[l]),
            _stick_breaking_mixer(p_sb, sb_q_norm[l], sb_k_norm[l]),
            _retention_mixer(p_ret, ret_gn[l]),
            _conformer_conv_mixer(p_conv, conv_dw[l], conv_b[l], conv_ln_w[l], conv_ln_b[l]),
        )
        merged = jax.nn.sigmoid(h @ w_gate[l, 0]) * (branches[0] @ w_branch[l, 0])
        for i in range(1, N_BRANCH):
            merged = merged + jax.nn.sigmoid(h @ w_gate[l, i]) * (branches[i] @ w_branch[l, i])
        x = x + merged @ w_out[l]
        h = _rmsnorm(x, norm_ffn[l])
        if l % 2 == 0:
            x = x + _swiglu(h, ffn_w1[l // 2], ffn_w3[l // 2], ffn_w2[l // 2])
        else:
            x = x + _moe_ffn(h, router[l // 2], moe_w1[l // 2], moe_w3[l // 2], moe_w2[l // 2])
    return x


N_A_LAYERS = DEPTH // 2
N_B_LAYERS = DEPTH - N_A_LAYERS
LRU_WIDTH = D_MODEL
LRU_HEADS = 8
LRU_BLOCK = LRU_WIDTH // LRU_HEADS
CONV_WIDTH_2 = 4
LRU_C = 8.0
N_HEADS_2 = D_MODEL // HEAD_DIM
N_KV_GROUPS = 4
HEADS_PER_GROUP = N_HEADS_2 // N_KV_GROUPS
CMP_BLOCK = 32
CMP_STRIDE = 16
CMP_HIDDEN = 256
SLC_BLOCK = 64
SLC_TOPK = 16
N_LOCAL_BLOCKS = 2
WINDOW = 512
Q_BLOCK = 128
ROPE_THETA = 10000.0
FFN_HIDDEN = ((8 * D_MODEL // 3 + 255) // 256) * 256
EPS = 1e-6
NEG = -1e30
FORCE = 1e30


def rmsnorm(x, g):
    xf = x.astype(jnp.float32)
    y = xf * lax.rsqrt(jnp.mean(xf * xf, axis=-1, keepdims=True) + EPS)
    return (y * g.astype(jnp.float32)).astype(x.dtype)

def rope(x, pos):
    half = HEAD_DIM // 2
    freqs = jnp.power(ROPE_THETA, -jnp.arange(half, dtype=jnp.float32) / half)
    ang = pos.astype(jnp.float32)[:, None] * freqs[None, :]
    cos = jnp.cos(ang)[:, None, :]
    sin = jnp.sin(ang)[:, None, :]
    xf = x.astype(jnp.float32)
    x1, x2 = xf[..., :half], xf[..., half:]
    return jnp.concatenate([x1 * cos - x2 * sin, x1 * sin + x2 * cos], axis=-1).astype(x.dtype)

def masked_softmax(s, mask):
    s = jnp.where(mask, s, NEG)
    return jax.nn.softmax(s, axis=-1) * mask

def causal_conv(x, w, b):
    S = x.shape[1]
    xp = jnp.pad(x, ((0, 0), (CONV_WIDTH_2 - 1, 0), (0, 0)))
    out = b
    for k in range(CONV_WIDTH_2):
        out = out + xp[:, k:k + S] * w[k]
    return out

def rg_lru(x, gate_w, gate_b, lam):
    B, S, R = x.shape
    xf = x.astype(jnp.float32)
    xh = xf.reshape(B, S, LRU_HEADS, LRU_BLOCK)
    gates = jnp.einsum('bshi,khij->kbshj', xh, gate_w.astype(jnp.float32)).reshape(2, B, S, R)
    gates = gates + gate_b.astype(jnp.float32)[:, None, None, :]
    r = jax.nn.sigmoid(gates[0])
    i = jax.nn.sigmoid(gates[1])
    log_a = -LRU_C * jax.nn.softplus(-lam.astype(jnp.float32)) * r
    a = jnp.exp(log_a)
    bterm = jnp.sqrt(-jnp.expm1(2.0 * log_a)) * (i * xf)

    def combine(e1, e2):
        a1, b1 = e1
        a2, b2 = e2
        return a1 * a2, a2 * b1 + b2

    _, h = lax.associative_scan(combine, (a, bterm), axis=1)
    return h.astype(x.dtype)

def recurrent_block(h, norm_g, w_in, conv_w, conv_b, gate_w, gate_b, lam, w_out):
    u = rmsnorm(h, norm_g)
    z = u @ w_in
    y = jax.nn.gelu(z[..., :LRU_WIDTH])
    xr = causal_conv(z[..., LRU_WIDTH:], conv_w, conv_b)
    hr = rg_lru(xr, gate_w, gate_b, lam)
    return (y * hr) @ w_out

def swiglu(h, norm_g, w_in, w_out):
    u = rmsnorm(h, norm_g)
    gu = u @ w_in
    return (jax.nn.silu(gu[..., :FFN_HIDDEN]) * gu[..., FFN_HIDDEN:]) @ w_out

def compress(t, pos_emb, w1, b1, w2, b2):
    B, S = t.shape[0], t.shape[1]
    n_cmp = (S - CMP_BLOCK) // CMP_STRIDE + 1
    idx = jnp.arange(n_cmp)[:, None] * CMP_STRIDE + jnp.arange(CMP_BLOCK)[None, :]
    blocks = t[:, idx] + pos_emb[:, None, :]
    blocks = blocks.transpose(0, 1, 3, 2, 4).reshape(B, n_cmp, N_KV_GROUPS, CMP_BLOCK * HEAD_DIM)
    return jax.nn.gelu(blocks @ w1 + b1) @ w2 + b2

def shared_kv(h, kv_norm, kv_w, k_norm, cmp_pos, cmp_w1, cmp_b1, cmp_w2, cmp_b2):
    B, S, _ = h.shape
    u = rmsnorm(h, kv_norm)
    kv = (u @ kv_w).reshape(B, S, 6, N_KV_GROUPS, HEAD_DIM)
    k_c, v_c, k_s, v_s, k_w, v_w = [kv[:, :, j] for j in range(6)]
    pos = jnp.arange(S)
    k_s = rope(rmsnorm(k_s, k_norm[1]), pos)
    k_w = rope(rmsnorm(k_w, k_norm[2]), pos)
    n_cmp = (S - CMP_BLOCK) // CMP_STRIDE + 1
    cmp_last = jnp.arange(n_cmp) * CMP_STRIDE + CMP_BLOCK - 1
    k_cmp = compress(k_c, cmp_pos[0], cmp_w1[0], cmp_b1[0], cmp_w2[0], cmp_b2[0])
    k_cmp = rope(rmsnorm(k_cmp, k_norm[0]), cmp_last)
    v_cmp = compress(v_c, cmp_pos[1], cmp_w1[1], cmp_b1[1], cmp_w2[1], cmp_b2[1])
    return (k_cmp, v_cmp, k_s, v_s, k_w, v_w)

def nsa_single(args):
    q, gate, k_cmp, v_cmp, k_slc, v_slc, k_win, v_win = args
    S = q.shape[0]
    G, Hg, dk = N_KV_GROUPS, HEADS_PER_GROUP, HEAD_DIM
    n_cmp = k_cmp.shape[0]
    n_slc = S // SLC_BLOCK
    top_n = min(SLC_TOPK, n_slc)
    scale = HEAD_DIM ** -0.5
    cmp_start = jnp.arange(n_cmp) * CMP_STRIDE
    cmp_last = cmp_start + CMP_BLOCK - 1
    slc_start = jnp.arange(n_slc) * SLC_BLOCK
    overlap = jnp.clip(jnp.minimum(cmp_start[:, None] + CMP_BLOCK, slc_start[None, :] + SLC_BLOCK)
                       - jnp.maximum(cmp_start[:, None], slc_start[None, :]), 0).astype(jnp.float32) / CMP_BLOCK
    kb = k_slc.reshape(n_slc, SLC_BLOCK, G, dk).transpose(2, 0, 1, 3)
    vb = v_slc.reshape(n_slc, SLC_BLOCK, G, dk).transpose(2, 0, 1, 3)
    kw_p = jnp.pad(k_win, ((WINDOW, 0), (0, 0), (0, 0)))
    vw_p = jnp.pad(v_win, ((WINDOW, 0), (0, 0), (0, 0)))
    qg = q.reshape(S, G, Hg, dk)
    blk = jnp.arange(n_slc)
    grp = jnp.arange(G)[None, :, None]

    def block(qb):
        s0 = qb * Q_BLOCK
        qt = lax.dynamic_slice_in_dim(qg, s0, Q_BLOCK, 0)
        gt = lax.dynamic_slice_in_dim(gate, s0, Q_BLOCK, 0).reshape(Q_BLOCK, 3, G, Hg)
        t = s0 + jnp.arange(Q_BLOCK)
        s = jnp.einsum('tghd,cgd->tghc', qt, k_cmp).astype(jnp.float32) * scale
        p_cmp = masked_softmax(s, (cmp_last[None, :] <= t[:, None])[:, None, None, :])
        o_cmp = jnp.einsum('tghc,cgd->tghd', p_cmp.astype(v_cmp.dtype), v_cmp)
        imp = jnp.einsum('tgc,cj->tgj', p_cmp.sum(axis=2), overlap)
        cur = (t // SLC_BLOCK)[:, None]
        causal_blk = blk[None, :] <= cur
        forced = (blk[None, :] == 0) | (causal_blk & (cur - blk[None, :] < N_LOCAL_BLOCKS))
        score = jnp.where(forced[:, None, :], FORCE, jnp.where(causal_blk[:, None, :], imp, NEG))
        _, idx = lax.top_k(score, top_n)
        ksel = kb[grp, idx].reshape(Q_BLOCK, G, top_n * SLC_BLOCK, dk)
        vsel = vb[grp, idx].reshape(Q_BLOCK, G, top_n * SLC_BLOCK, dk)
        kpos = (idx[..., None] * SLC_BLOCK + jnp.arange(SLC_BLOCK)).reshape(Q_BLOCK, G, top_n * SLC_BLOCK)
        s = jnp.einsum('tghd,tgkd->tghk', qt, ksel).astype(jnp.float32) * scale
        p = masked_softmax(s, (kpos <= t[:, None, None])[:, :, None, :])
        o_slc = jnp.einsum('tghk,tgkd->tghd', p.astype(vsel.dtype), vsel)
        kw = lax.dynamic_slice_in_dim(kw_p, s0, WINDOW + Q_BLOCK, 0)
        vw = lax.dynamic_slice_in_dim(vw_p, s0, WINDOW + Q_BLOCK, 0)
        kp = s0 - WINDOW + jnp.arange(WINDOW + Q_BLOCK)
        mw = (kp[None, :] <= t[:, None]) & (kp[None, :] > t[:, None] - WINDOW) & (kp[None, :] >= 0)
        s = jnp.einsum('tghd,kgd->tghk', qt, kw).astype(jnp.float32) * scale
        p = masked_softmax(s, mw[:, None, None, :])
        o_win = jnp.einsum('tghk,kgd->tghd', p.astype(vw.dtype), vw)
        o = gt[:, 0][..., None] * o_cmp + gt[:, 1][..., None] * o_slc + gt[:, 2][..., None] * o_win
        return o.reshape(Q_BLOCK, N_HEADS_2, dk)

    out = lax.map(block, jnp.arange(S // Q_BLOCK))
    return out.reshape(S, N_HEADS_2, dk)

def nsa_layer(h, norm_g, w_in, gate_b, q_norm_g, w_out, k_cmp, v_cmp, k_s, v_s, k_w, v_w):
    B, S, _ = h.shape
    u = rmsnorm(h, norm_g)
    z = u @ w_in
    q = z[..., :N_HEADS_2 * HEAD_DIM].reshape(B, S, N_HEADS_2, HEAD_DIM)
    q = rope(rmsnorm(q, q_norm_g), jnp.arange(S))
    gates = jax.nn.sigmoid(z[..., N_HEADS_2 * HEAD_DIM:] + gate_b).reshape(B, S, 3, N_HEADS_2)
    o = lax.map(nsa_single, (q, gates, k_cmp, v_cmp, k_s, v_s, k_w, v_w))
    return o.reshape(B, S, N_HEADS_2 * HEAD_DIM) @ w_out

def second_inputs(seed: int = 0) -> dict:
    key = jax.random.key(seed)
    ks = jax.random.split(key, 26)

    def nrm(k, shape, scale):
        return jax.random.normal(k, shape, jnp.float32) * scale

    def gain(k, shape):
        return 1.0 + 0.02 * jax.random.normal(k, shape, jnp.float32)

    R, NA, NB = LRU_WIDTH, N_A_LAYERS, N_B_LAYERS
    u = jax.random.uniform(ks[7], (NA, R), jnp.float32, minval=0.9, maxval=0.999)
    s = u ** (1.0 / LRU_C)
    a_lambda = jnp.log(s) - jnp.log1p(-s)
    nq = N_HEADS_2 * HEAD_DIM + 3 * N_HEADS_2
    return {
        "x": nrm(ks[0], (BATCH, SEQ, D_MODEL), 1.0),
        "a_norm": gain(ks[1], (NA, D_MODEL)),
        "a_w_in": nrm(ks[2], (NA, D_MODEL, 2 * R), D_MODEL ** -0.5),
        "a_conv_w": nrm(ks[3], (NA, CONV_WIDTH_2, R), CONV_WIDTH_2 ** -0.5),
        "a_conv_b": nrm(ks[4], (NA, R), 0.01),
        "a_gate_w": nrm(ks[5], (NA, 2, LRU_HEADS, LRU_BLOCK, LRU_BLOCK), LRU_BLOCK ** -0.5),
        "a_gate_b": nrm(ks[6], (NA, 2, R), 0.01),
        "a_lambda": a_lambda,
        "a_w_out": nrm(ks[8], (NA, R, D_MODEL), R ** -0.5),
        "kv_norm": gain(ks[9], (D_MODEL,)),
        "kv_w": nrm(ks[10], (D_MODEL, 6 * N_KV_GROUPS * HEAD_DIM), D_MODEL ** -0.5),
        "k_norm": gain(ks[11], (3, HEAD_DIM)),
        "cmp_pos": nrm(ks[12], (2, CMP_BLOCK, HEAD_DIM), 0.02),
        "cmp_w1": nrm(ks[13], (2, CMP_BLOCK * HEAD_DIM, CMP_HIDDEN), (CMP_BLOCK * HEAD_DIM) ** -0.5),
        "cmp_b1": nrm(ks[14], (2, CMP_HIDDEN), 0.01),
        "cmp_w2": nrm(ks[15], (2, CMP_HIDDEN, HEAD_DIM), CMP_HIDDEN ** -0.5),
        "cmp_b2": nrm(ks[16], (2, HEAD_DIM), 0.01),
        "b_norm": gain(ks[17], (NB, D_MODEL)),
        "b_w_in": nrm(ks[18], (NB, D_MODEL, nq), D_MODEL ** -0.5),
        "b_gate_b": nrm(ks[19], (NB, 3 * N_HEADS_2), 0.01),
        "q_norm": gain(ks[20], (NB, HEAD_DIM)),
        "b_w_out": nrm(ks[21], (NB, N_HEADS_2 * HEAD_DIM, D_MODEL), (N_HEADS_2 * HEAD_DIM) ** -0.5),
        "f_norm": gain(ks[22], (DEPTH, D_MODEL)),
        "f_w_in": nrm(ks[23], (DEPTH, D_MODEL, 2 * FFN_HIDDEN), D_MODEL ** -0.5),
        "f_w_out": nrm(ks[24], (DEPTH, FFN_HIDDEN, D_MODEL), FFN_HIDDEN ** -0.5),
    }

def second_block(x, a_norm, a_w_in, a_conv_w, a_conv_b, a_gate_w, a_gate_b, a_lambda, a_w_out,
              kv_norm, kv_w, k_norm, cmp_pos, cmp_w1, cmp_b1, cmp_w2, cmp_b2,
              b_norm, b_w_in, b_gate_b, q_norm, b_w_out,
              f_norm, f_w_in, f_w_out):
    h = x
    shared = None
    for layer in range(DEPTH):
        if layer < N_A_LAYERS:
            i = layer
            h = h + recurrent_block(h, a_norm[i], a_w_in[i], a_conv_w[i], a_conv_b[i],
                                    a_gate_w[i], a_gate_b[i], a_lambda[i], a_w_out[i])
        else:
            if layer == N_A_LAYERS:
                shared = shared_kv(h, kv_norm, kv_w, k_norm, cmp_pos, cmp_w1, cmp_b1, cmp_w2, cmp_b2)
            j = layer - N_A_LAYERS
            h = h + nsa_layer(h, b_norm[j], b_w_in[j], b_gate_b[j], q_norm[j], b_w_out[j], *shared)
        h = h + swiglu(h, f_norm[layer], f_w_in[layer], f_w_out[layer])
    return h


def setup_inputs(seed=0):
    out = dict(first_inputs(seed))
    for name, value in second_inputs(seed + 1).items():
        if name != "x":
            out[name + "_2"] = value
    return out


def reference(
    x, norm_mix, w_in, rw_mu, rw_w0, rw_w2, rw_a0, rw_a2, rw_g2, rw_k_k, rw_k_a, rw_r_k,
    rw_ln_w, rw_ln_b, sb_q_norm, sb_k_norm, ret_gn, conv_dw, conv_b, conv_ln_w, conv_ln_b,
    w_gate, w_branch, w_out, norm_ffn, ffn_w1, ffn_w3, ffn_w2, router, moe_w1, moe_w3, moe_w2,
    a_norm_2, a_w_in_2, a_conv_w_2, a_conv_b_2, a_gate_w_2, a_gate_b_2, a_lambda_2, a_w_out_2,
    kv_norm_2, kv_w_2, k_norm_2, cmp_pos_2, cmp_w1_2, cmp_b1_2, cmp_w2_2, cmp_b2_2, b_norm_2,
    b_w_in_2, b_gate_b_2, q_norm_2, b_w_out_2, f_norm_2, f_w_in_2, f_w_out_2,
):
    x = first_block(
        x, norm_mix, w_in, rw_mu, rw_w0, rw_w2, rw_a0, rw_a2, rw_g2, rw_k_k, rw_k_a, rw_r_k,
        rw_ln_w, rw_ln_b, sb_q_norm, sb_k_norm, ret_gn, conv_dw, conv_b, conv_ln_w, conv_ln_b,
        w_gate, w_branch, w_out, norm_ffn, ffn_w1, ffn_w3, ffn_w2, router, moe_w1, moe_w3,
        moe_w2,
    )
    return second_block(
        x, a_norm_2, a_w_in_2, a_conv_w_2, a_conv_b_2, a_gate_w_2, a_gate_b_2, a_lambda_2,
        a_w_out_2, kv_norm_2, kv_w_2, k_norm_2, cmp_pos_2, cmp_w1_2, cmp_b1_2, cmp_w2_2,
        cmp_b2_2, b_norm_2, b_w_in_2, b_gate_b_2, q_norm_2, b_w_out_2, f_norm_2, f_w_in_2,
        f_w_out_2,
    )


_drawn_inputs = setup_inputs


def setup_inputs(seed=0):
    import zlib

    import numpy as np

    out = dict(_drawn_inputs(seed))
    spreads = {}
    factors = {'rw_k_k': 3.069,
     'rw_ln_b': 8.0,
     'conv_b': 4.878,
     'conv_ln_b': 8.0,
     'a_norm_2': 5.052,
     'a_gate_b_2': 8.0,
     'kv_norm_2': 8.0,
     'k_norm_2': 8.0,
     'cmp_pos_2': 28.139,
     'cmp_b1_2': 51.428,
     'cmp_b2_2': 37.368,
     'b_norm_2': 8.0,
     'b_gate_b_2': 64.0,
     'q_norm_2': 8.0,
     'f_norm_2': 3.169}
    for name, (base, spread) in spreads.items():
        noise = np.random.default_rng([zlib.crc32(name.encode()), seed]).standard_normal(out[name].shape)
        drawn = base * np.exp(spread * noise) if base else spread * noise
        out[name] = __import__('jax').numpy.asarray(drawn.astype(out[name].dtype))
    for name, factor in factors.items():
        out[name] = (out[name] * factor).astype(out[name].dtype)
    return out
```

```python
from contextlib import ExitStack

import numpy as np

import concourse.bass as bass
from concourse import mybir

F32 = mybir.dt.float32
I32 = mybir.dt.int32
U32 = mybir.dt.uint32
ALU = mybir.AluOpType
ACT = mybir.ActivationFunctionType
AX = mybir.AxisListType.X

P = 128
T = 256
TT = T // P
D = 1024
KT = D // P
HD = 64
NH = 4
NHQ = 16
G = 4
LORA = 64
DECAY_SCALE = 0.606531
SHIFT = DECAY_SCALE * P / 2
EPS = 1e-6
RW_EPS = 64e-5
LN_EPS = 1e-5
TAPS = 31
TAPS2 = 4
NE = 8
FE = 1408
FT = FE // P
LRU_C = 8.0
CB, CS = 32, 16
NC = (T - CB) // CS + 1
HID = 256
NEG = -1e30
LEVELS = 7

SLAB = 4096
RING = 3
IN_SLABS, OUT_SLABS = 6, 3
EXPERT_SLABS = IN_SLABS + OUT_SLABS


def columns(widths):
    place, at = {}, 0
    for name, n in widths:
        place[name] = (at, n)
        at += n
    return place, at


CONSTS, N_CONSTS = columns([
    ("ident", P), ("head_sum", P), ("head_mean", P), ("ones", P), ("strict", P), ("causal", P),
    ("suffix", P), ("levels", LEVELS * P), ("swap", P), ("cos", T), ("sin", T), ("cos_cmp", NC),
    ("sin_cmp", NC), ("decay", NH * T), ("not_before", P), ("causal_add", T + P), ("cmp_add", TT * NC),
    ("cmp_keep", TT * NC), ("experts", NE), ("rms_eps", 1), ("rw_eps", 1), ("ln_eps", 1),
    ("shift", 1), ("minus_shift", 1), ("one", 1)])

LAYER_COLS = [
    ("norm_mix", KT), ("norm_ffn", KT), ("mu", KT), ("w0", 2), ("a0", 2), ("k_k", 2), ("k_a", 2),
    ("r_k", 2), ("ln_w", 2), ("ln_b", 2), ("sb_q", 1), ("sb_k", 1), ("gn", 2), ("dw", 2 * TAPS),
    ("db", 2), ("cln_w", 2), ("cln_b", 2), ("w2a2", 2 * P), ("g2", 2 * P)]
PARAMS, N_PARAMS = columns(
    [(f"{name}{l}", n) for l in range(2) for name, n in LAYER_COLS] + [
        ("router", KT * NE), ("a_norm", KT), ("a_conv_w", KT * TAPS2), ("a_conv_b", KT),
        ("a_gate_b", 2 * KT), ("a_lambda", KT), ("kv_norm", KT), ("k_norm", 3), ("cmp_pos", 2 * CB // 2),
        ("cmp_b1", 4), ("cmp_b2k", 1), ("cmp_b2v", HD), ("cmp_w2k", 2 * P), ("cmp_w2v", 2 * HD),
        ("b_norm", KT), ("gate_w", KT * 48), ("gate_b", 48), ("q_norm", 1), ("f_norm0", KT), ("f_norm1", KT)])


def constant_arrays():
    c = np.zeros((P, N_CONSTS), np.float32)

    def put(name, a):
        at, n = CONSTS[name]
        c[:, at:at + n] = np.asarray(a, np.float32).reshape(P, n)

    i = np.arange(P)
    row, col = i[:, None], i[None, :]
    same_head = (row // HD == col // HD).astype(np.float32)
    put("ident", np.eye(P))
    put("head_sum", same_head)
    put("head_mean", same_head / HD)
    put("ones", np.ones((P, P)))
    put("strict", row < col)
    put("causal", row <= col)
    put("suffix", row >= col)
    levels = []
    for n in range(LEVELS):
        b = 1 << n
        levels.append((row < col) & (row // (2 * b) == col // (2 * b)) & (row // b != col // b))
    put("levels", np.stack(levels, 1))
    swap = np.zeros((P, P), np.float32)
    for m in range(P):
        d = m % HD
        if d < HD // 2:
            swap[m + HD // 2, m] = -1.0
        else:
            swap[m - HD // 2, m] = 1.0
    put("swap", swap)
    freq = np.float32(10000.0) ** (-np.arange(0, HD, 2, dtype=np.float32) / np.float32(HD))
    freq = freq[i % (HD // 2)].astype(np.float32)[:, None]
    pos = np.arange(T, dtype=np.float32)[None, :]
    cmp_last = np.arange(NC) * CS + CB - 1
    put("cos", np.cos(pos * freq))
    put("sin", np.sin(pos * freq))
    put("cos_cmp", np.cos(cmp_last.astype(np.float32)[None, :] * freq))
    put("sin_cmp", np.sin(cmp_last.astype(np.float32)[None, :] * freq))
    gamma = np.log(1.0 - 2.0 ** (-5.0 - np.arange(NH)))
    rel = np.arange(T)[None, None, :] - i[:, None, None]
    decay = np.where(rel >= 0, np.exp(np.maximum(rel, 0) * gamma[None, :, None]) * HD ** -0.5, 0.0)
    put("decay", decay[:, [0, 2, 1, 3]])
    put("not_before", np.where(row < col, 0.0, NEG))
    put("causal_add", np.concatenate([np.zeros((P, P)), np.where(col <= row, 0.0, NEG), np.zeros((P, P))], 1))
    t = i[:, None, None] + P * np.arange(TT)[None, :, None]
    seen = cmp_last[None, None, :] <= t
    put("cmp_add", np.where(seen, 0.0, NEG))
    put("cmp_keep", seen)
    put("experts", np.broadcast_to(np.arange(NE), (P, NE)))
    for name, value in (("rms_eps", EPS), ("rw_eps", RW_EPS), ("ln_eps", LN_EPS), ("shift", SHIFT),
                        ("minus_shift", -SHIFT), ("one", 1.0)):
        put(name, np.full((P, 1), value))
    return c


def parameter_array(a):
    c = np.zeros((P, N_PARAMS), np.float32)

    def put(name, v, rows=slice(0, P)):
        at, n = PARAMS[name]
        c[rows, at:at + n] = v

    def column(v):
        return v.reshape(-1, P).T

    for l in range(2):
        for name, key in (("norm_mix", "norm_mix"), ("norm_ffn", "norm_ffn"), ("mu", "rw_mu"), ("w0", "rw_w0"),
                          ("a0", "rw_a0"), ("k_k", "rw_k_k"), ("k_a", "rw_k_a"), ("ln_w", "rw_ln_w"),
                          ("ln_b", "rw_ln_b"), ("gn", "ret_gn"), ("db", "conv_b"), ("cln_w", "conv_ln_w"),
                          ("cln_b", "conv_ln_b")):
            put(f"{name}{l}", column(a[key][l]))
        put(f"r_k{l}", column(a["rw_r_k"][l].reshape(-1)))
        put(f"sb_q{l}", np.concatenate([a["sb_q_norm"][l]] * 2)[:, None])
        put(f"sb_k{l}", np.concatenate([a["sb_k_norm"][l]] * 2)[:, None])
        put(f"dw{l}", a["conv_dw"][l].reshape(TAPS, 2, P).transpose(2, 1, 0).reshape(P, -1))
        put(f"w2a2{l}", np.concatenate([a["rw_w2"][l], a["rw_a2"][l]], 0))
        put(f"g2{l}", a["rw_g2"][l])
    put("router", a["router"][0].reshape(KT, P, NE).transpose(1, 0, 2).reshape(P, -1))
    put("a_norm", column(a["a_norm_2"][0]))
    put("a_conv_w", a["a_conv_w_2"][0].reshape(TAPS2, KT, P).transpose(2, 1, 0).reshape(P, -1))
    put("a_conv_b", column(a["a_conv_b_2"][0]))
    put("a_gate_b", column(a["a_gate_b_2"][0].reshape(-1)))
    put("a_lambda", column(a["a_lambda_2"][0]))
    put("kv_norm", column(a["kv_norm_2"]))
    put("k_norm", np.concatenate([a["k_norm_2"]] * 2, 1).T)
    put("cmp_pos", a["cmp_pos_2"].reshape(2, CB // 2, 2 * HD).transpose(2, 0, 1).reshape(P, -1))
    put("cmp_b1", column(a["cmp_b1_2"].reshape(-1)))
    put("cmp_b2k", np.concatenate([a["cmp_b2_2"][0]] * 2)[:, None])
    put("cmp_b2v", a["cmp_b2_2"][1][None, :], slice(0, 1))
    w2 = a["cmp_w2_2"].reshape(2, 2, P, HD)
    put("cmp_w2k", np.concatenate([w2[0]] * 2, 2).transpose(1, 0, 2).reshape(P, -1))
    put("cmp_w2v", w2[1].transpose(1, 0, 2).reshape(P, -1))
    put("b_norm", column(a["b_norm_2"][0]))
    put("gate_w", a["b_w_in_2"][0][:, D:].reshape(KT, P, 48).transpose(1, 0, 2).reshape(P, -1))
    put("gate_b", a["b_gate_b_2"][0][None, :], slice(0, 1))
    put("q_norm", np.concatenate([a["q_norm_2"][0]] * 2)[:, None])
    put("f_norm0", column(a["f_norm_2"][0]))
    put("f_norm1", column(a["f_norm_2"][1]))
    return c


def weight_stream(a):
    slabs = []

    def add(w):
        w = w.reshape(P, -1)
        slab = np.zeros((P, SLAB), np.float32)
        slab[:, :w.shape[1]] = w
        slabs.append(slab)

    def rows(w):
        return w.reshape(-1, P, w.shape[-1]).transpose(1, 0, 2)

    def wide(w):
        for n in range(0, w.shape[1], 512):
            cut = w[:, n:n + 512]
            if cut.shape[1] < 512:
                cut = np.concatenate([cut, np.zeros((cut.shape[0], 512 - cut.shape[1]), np.float32)], 1)
            add(rows(cut))

    def expert(w1, w3, w2):
        for f in range(0, FE, 2 * P):
            pad = np.zeros((D, max(0, f + 2 * P - FE)), np.float32)
            add(rows(np.concatenate([w1[:, f:f + 2 * P], pad, w3[:, f:f + 2 * P], pad], 1)))
        for f in range(0, FE, 4 * P):
            add(rows(w2[f:f + 4 * P]))

    for l in range(2):
        w = a["w_in"][l]
        rw, sb, ret = 1024, 1792, 2816
        order = [w[:, 0:rw], w[:, rw:rw + 512], w[:, sb:sb + 512],
                 w[:, rw + 512:sb], w[:, sb + 512:sb + 768], w[:, sb + 768:ret], w[:, ret:]]
        wide(np.concatenate(order, 1))
        for i in range(4):
            wide(a["w_gate"][l, i])
        for i in range(0, 4, 2):
            add(rows(a["w_branch"][l, i:i + 2].reshape(512, D)))
        wide(a["w_out"][l])
        if l == 0:
            for h in range(2):
                s = slice(h * FE, h * FE + FE)
                expert(a["ffn_w1"][0][:, s], a["ffn_w3"][0][:, s], a["ffn_w2"][0][s])
        else:
            for e in range(NE):
                expert(a["moe_w1"][0, e], a["moe_w3"][0, e], a["moe_w2"][0, e])

    def ffn(l):
        for h in range(2):
            s = slice(h * FE, h * FE + FE)
            w = a["f_w_in_2"][l]
            expert(w[:, :2 * FE][:, s], w[:, 2 * FE:][:, s], a["f_w_out_2"][l][s])

    wide(a["a_w_in_2"][0])
    add(a["a_gate_w_2"][0].transpose(2, 0, 1, 3))
    wide(a["a_w_out_2"][0])
    ffn(0)
    kv = a["kv_w_2"]
    wide(np.concatenate([kv[:, 0:768], kv[:, 1024:1280], kv[:, 768:1024], kv[:, 1280:1536]], 1))
    for v in range(2):
        add(rows(a["cmp_w1_2"][v]))
    wide(a["b_w_in_2"][0][:, :D])
    wide(a["b_w_out_2"][0])
    ffn(1)
    return np.stack(slabs)


class Steps:

    def __init__(self, sem, *names):
        self.sem, self.names, self.count = sem, names, 0

    def at(self, name, rnd=0):
        return rnd * len(self.names) + self.names.index(name) + 1

    def mark(self, ins, name, rnd=0):
        self.count += 1
        assert self.count == self.at(name, rnd), (name, rnd, self.count)
        ins.then_inc(self.sem, 1)
        return self.count


class Chain:

    def __init__(self, eng, sem):
        self.eng, self.sem, self.count = eng, sem, 0

    def to(self, ins, sem, value):
        ins.then_inc(sem, 1)
        self.eng.wait_ge(sem, value)

    def run(self, ins, steps=None, name=None, rnd=0):
        if steps is None:
            self.count += 1
            ins.then_inc(self.sem, 1)
            self.eng.wait_ge(self.sem, self.count)
        else:
            self.eng.wait_ge(steps.sem, steps.mark(ins, name, rnd))


def build(nc, stream, consts_in, params_in, x_in, out):
    n_slabs = stream.shape[0]
    assert n_slabs % RING == 0
    with ExitStack() as ctx:
        def sb(name, shape, dt=F32):
            return ctx.enter_context(nc.sbuf_tensor(name, shape, dt))

        def sem(name):
            return ctx.enter_context(nc.semaphore(name))

        x = sb("x", [P, TT, D])
        hT = sb("hT", [P, KT, T])
        scr = sb("scr", [P, 2048])
        ring = sb("ring", [P, RING, SLAB])
        consts = sb("consts", [P, N_CONSTS])
        params = sb("params", [P, N_PARAMS])
        small = sb("small", [P, 256])
        router_gates = sb("router_gates", [P, TT, NE])
        ones_gates = sb("ones_gates", [P, TT, NE])
        top_index = sb("top_index", [P, TT, 8], U32)
        glu = sb("glu", [P, 2, T])
        work = sb("work", [P, 27136])
        banks = ctx.enter_context(nc.psum_tensor("banks", [P, 8, 512], F32))

        def const(name, *index):
            at, n = CONSTS[name]
            return consts[:, at:at + n]

        def par(name, i=0, n=1, rows=slice(0, P)):
            at, _ = PARAMS[name]
            return params[rows, at + i:at + i + n]

        def w(at, *dims, rows=slice(0, P)):
            n = 1
            for d in dims:
                n *= d
            ap = work[rows, at:at + n]
            return ap if len(dims) == 1 else ap.rearrange(
                "p (a b) -> p a b" if len(dims) == 2 else "p (a b c) -> p a b c", **dict(zip("abc", dims)))

        def bank(b, n=1, rows=slice(0, P)):
            return banks[rows, b:b + n, :].rearrange("p a b -> p (a b)")

        def grid(ap, a):
            return ap.rearrange("p (a b) -> p a b", a=a)

        PAIR = 2 * T + 2 * P

        def pairs(b):
            return grid(bank(b, 4), 2)[:, :, 0:PAIR]

        def diagonals(at):
            s = w(at, 2, PAIR)
            return (s[:, :, 0:2 * T].rearrange("p r (t s) -> p r t s", t=2)[:, :, :, 0:P],
                    s[:, :, 2 * T:PAIR].rearrange("p r (t s) -> p r t s", t=2))

        def matrix(h, c):
            return (h % 2) * 4 + 2 * c + h // 2

        def half(r):
            return slice(HD * r, HD * r + HD)

        PT, VT, BR, SIG, MATS, INV, MX = 0, 5632, 6656, 8704, 16896, 20992, 25088
        LEVEL_AT = (INV + 3072, MX + 1024)
        pT = w(PT, 22, T)
        vt = w(VT, TT, 512)
        br = w(BR, KT, T)
        sig = w(SIG, 4 * KT, T)

        loaded = sem("loaded")
        landed = [sem(f"landed{i}") for i in range(RING)]
        slab_used = sem("slab_used")
        stored = sem("stored")
        v_chain, a_chain = sem("v_chain"), sem("a_chain")
        NORM_V = Steps(sem("norm_vector"), "rows", "hT")
        NORM_A = Steps(sem("norm_scalar"), "root")
        NORM_P = Steps(sem("norm_transposed"), "done")
        win_full, win_out = sem("win_full"), sem("win_out")
        gate_full, gate_out = sem("gate_full"), sem("gate_out")
        br_full, br_out = sem("branch_full"), sem("branch_merged")
        RW_P = Steps(sem("rw_products"), "lora", "squares", "bonus", "mats0", "mats1",
                     *[f"{s}{n}" for n in range(LEVELS) for s in ("T", "X")],
                     "w0", "u0", "state", "w1", "u1", "y", "mean", "var")
        RW_V = Steps(sem("rw_vector"), "mixed", "k_squared", "decays", "operands", "bonus_used", "mats0", "mats1",
                     *[f"X{n}" for n in range(LEVELS)], "state", "y", "centred", "done")
        RW_A = Steps(sem("rw_scalar"), "lora", "sigmoids", "norm", "exps", "rows", *[f"T{n}" for n in range(LEVELS)],
                     "w0", "u0", "w1", "u1", "dev")
        RW_G = Steps(sem("rw_masks"), "zeroed", *[f"M{n}" for n in range(LEVELS)])
        SB_P = Steps(sem("sb_products"), "squares", "scores", "suffix", "out")
        SB_V = Steps(sem("sb_vector"), "squares", "qk", "softplus", "logs", "done")
        SB_A = Steps(sem("sb_scalar"), "norm", "scores", "ln", "weights")
        RET_P = Steps(sem("ret_products"), "rotated", "scores", "out", "mean", "var")
        RET_V = Steps(sem("ret_vector"), "qk", "scores", "y", "centred", "done")
        RET_A = Steps(sem("ret_scalar"), "silu", "dev")
        CV_P = Steps(sem("conv_products"), "mean", "var")
        CV_V = Steps(sem("conv_vector"), "conv", "centred", "affine")
        CV_A = Steps(sem("conv_scalar"), "sigmoid", "dev", "done")
        proj_full, proj_added = sem("proj_full"), sem("proj_added")
        glu_full, glu_silu, glu_done = sem("glu_full"), sem("glu_silu"), sem("glu_done")
        ffn_full, ffn_added = sem("ffn_full"), sem("ffn_added")
        RT_P = Steps(sem("router_products"), "logits")
        RT_V = Steps(sem("router_vector"), "gap", "gates")
        RT_A = Steps(sem("router_scalar"), "exp")
        ain_full, ain_out = sem("ain_full"), sem("ain_out")
        ag_full, ag_out = sem("lru_gate_full"), sem("lru_gate_out")
        LR_V = Steps(sem("lru_vector"), "conv", "log_a", "square", "done")
        LR_A = Steps(sem("lru_scalar"), "lambda", "exps", "root")
        kv_full, kv_out = sem("kv_full"), sem("kv_out")
        KV_V = Steps(sem("kv_vector"), "windows", "cmp_squares", "cmp_normed", "cmp_rope", "v_cmp", "k_squares",
                     "k_normed", "k_rope")
        KV_P = Steps(sem("kv_products"), "hidden0", "hidden1", "k_cmp", "cmp_mean", "cmp_rot", "v_cmp", "k_mean", "k_rot")
        KV_A = Steps(sem("kv_scalar"), "hidden0", "hidden1", "k_cmp", "cmp_norm", "k_norm", "k_copies")
        Q_P = Steps(sem("q_products"), "full0", "full1", "full2", "full3", "gates", "mean", "rot")
        Q_A = Steps(sem("q_scalar"), "out0", "out1", "out2", "out3", "gates", "norm")
        Q_V = Steps(sem("q_vector"), "squares", "normed", "rope")
        AT_P = Steps(sem("at_products"), "scores", "turned", "out")
        AT_V = Steps(sem("at_vector"), "masked", "probs")
        AT_A = Steps(sem("at_scalar"), "exps", "turned", "out")

        FIRST_EXPERT = {"dense": 0, "moe": 2, "f0": 2 + NE, "f1": 4 + NE}
        N_PARTS = {"dense": 2, "moe": NE, "f0": 2, "f1": 2}

        block = ctx.enter_context(nc.Block())

        @block.sync
        def _(sp):
            sp.dma_start(x[:, :, :], x_in.rearrange("o (a p) d -> p (o a) d", p=P)).then_inc(loaded, 16)
            sp.dma_start(consts[:, :], consts_in).then_inc(loaded, 16)
            sp.dma_start(params[:, :], params_in).then_inc(loaded, 16)
            for n in range(RING):
                sp.dma_start(ring[:, n, :], stream[n]).then_inc(landed[n], 16)
            with sp.Fori(1, n_slabs // RING) as i:
                for n in range(RING):
                    sp.wait_ge(slab_used, i * RING + (n + 1 - RING))
                    sp.dma_start(ring[:, n, :], stream[i * RING + n]).then_inc(landed[n], 16)
            sp.wait_ge(ffn_added, 4 * (FIRST_EXPERT["f1"] + 2) + 1)
            sp.dma_start(out.rearrange("o (a p) d -> p (o a) d", p=P), x[:, :, :]).then_inc(stored, 16)
            sp.wait_ge(stored, 16)

        @block.gpsimd
        def _(pool):
            for l in range(2):
                if l:
                    pool.wait_ge(NORM_V.sem, NORM_V.at("rows", 2 * l))
                RW_G.mark(pool.memset(w(MATS, 4096), 0.0), "zeroed", l)
                pool.wait_ge(RW_V.sem, RW_V.at("mats1", l))
                for n in range(LEVELS):
                    if n >= 2:
                        pool.wait_ge(RW_P.sem, RW_P.at(f"T{n - 2}", l))
                    at, _ = CONSTS["levels"]
                    mask = consts[:, at + n * P:at + n * P + P].unsqueeze(1).to_broadcast([P, 8, P])
                    RW_G.mark(pool.tensor_tensor(w(LEVEL_AT[n % 2], 8, P), w(MATS, 8, P), mask, ALU.mult),
                              f"M{n}", l)

        @block.scalar
        def _(act):
            chain = Chain(act, a_chain)
            run = chain.run

            def f(out_, in_, func, **kw):
                return act.activation(out_, in_, func, **kw)

            def norm(n):
                if n == 0:
                    act.wait_ge(loaded, 48)
                elif n in (1, 3):
                    act.wait_ge(proj_added, 2 * (n // 2 + 1))
                elif n == 2:
                    act.wait_ge(ffn_added, 4 * FIRST_EXPERT["moe"] + 1)
                elif n == 4:
                    act.wait_ge(ffn_added, 4 * FIRST_EXPERT["f0"] + 1)
                elif n == 5:
                    act.wait_ge(proj_added, 6)
                elif n == 6:
                    act.wait_ge(ffn_added, 4 * FIRST_EXPERT["f1"] + 1)
                elif n == 7:
                    act.wait_ge(NORM_P.sem, NORM_P.at("done", 6))
                elif n == 8:
                    act.wait_ge(proj_added, 8)
                for a in range(TT):
                    run(f(scr[:, a * D:a * D + D], x[:, a, :], ACT.Square, accum_out=small[:, a:a + 1]))
                run(f(small[:, 2:4], small[:, 0:2], ACT.Sqrt, scale=1.0 / D, bias=const("rms_eps")), NORM_A, "root", n)

            def win(l):
                for q in range(13):
                    act.wait_ge(win_full, 13 * l + q + 1)
                    src = banks[:, 4 + q % 4, :]
                    if q < 8:
                        dst = w(PT + 512 * q, 512)
                    elif q < 10:
                        dst = vt[:, q - 8, :]
                    else:
                        dst = w(PT + 512 * (q - 2), 512)
                    chain.to(f(dst, src, ACT.Copy), win_out, 13 * l + q + 1)

            def gates(l, slabs):
                for s in slabs:
                    for q in range(2):
                        n = 2 * s + q
                        act.wait_ge(gate_full, 16 * l + n + 1)
                        f(w(SIG + 512 * n, 512), banks[:, 6 + q, :], ACT.Sigmoid).then_inc(gate_out, 1)

            def rwkv_front(l):
                act.wait_ge(RW_V.sem, RW_V.at("mixed", l))
                run(f(w(INV + 3584, T, rows=half(0)), w(MX + 6 * T, T, rows=half(0)), ACT.Tanh))
                run(f(w(INV + 3840, T), w(MX + 7 * T, T), ACT.Sigmoid), RW_A, "lora", l)
                act.wait_ge(RW_P.sem, RW_P.at("lora", l))
                for j in range(2):
                    run(f(w(INV + 1536 + j * T, T), bank(0)[:, j * T:j * T + T], ACT.Sigmoid, bias=par(f"w0{l}", j)))
                    run(f(w(MX + (6 + j) * T, T), bank(1)[:, j * T:j * T + T], ACT.Sigmoid, bias=par(f"a0{l}", j)))
                run(f(scr[:, 0:512], bank(2), ACT.Copy), RW_A, "sigmoids", l)
                act.wait_ge(RW_P.sem, RW_P.at("squares", l))
                run(f(w(INV + 1024, 512), bank(3), ACT.Sqrt), RW_A, "norm", l)
                act.wait_ge(RW_V.sem, RW_V.at("decays", l))
                run(f(w(PT, 512), w(INV + 2560, 512), ACT.Exp, bias=const("shift")))
                run(f(w(INV + 3072, 512), w(INV + 2048, 512), ACT.Exp, scale=-1.0, bias=const("minus_shift")))
                run(f(w(PT + 1536, 512), w(INV + 2048, 512), ACT.Exp, bias=const("shift")))
                run(f(small[:, 8:10], w(INV + 2048, 2, T)[:, :, P - 1], ACT.Exp), RW_A, "exps", l)
                act.wait_ge(RW_P.sem, RW_P.at("bonus", l))
                run(f(scr[:, 1024:2048], bank(4, 2), ACT.Copy), RW_A, "rows", l)

            def rwkv_level(l, n):
                act.wait_ge(RW_P.sem, RW_P.at(f"T{n}", l))
                run(f(w(INV + 2048, 1024), bank(0, 2), ACT.Copy), RW_A, f"T{n}", l)

            def rwkv_back(l):
                for name, at in (("w0", 0), ("u0", 256), ("w1", 0), ("u1", 512)):
                    act.wait_ge(RW_P.sem, RW_P.at(name, l))
                    if at:
                        run(f(w(MX + at, 256), bank(2)[:, 0:256], ACT.Copy), RW_A, name, l)
                    else:
                        run(f(w(MX, 2, P), grid(bank(0, 2), 2)[:, :, 0:P], ACT.Copy), RW_A, name, l)
                act.wait_ge(RW_P.sem, RW_P.at("var", l))
                run(f(w(INV + 1536, 512), bank(5), ACT.Sqrt, bias=const("rw_eps")), RW_A, "dev", l)

            def stick(l):
                act.wait_ge(SB_P.sem, SB_P.at("squares", l))
                run(f(w(MATS, 1024), bank(0, 2), ACT.Sqrt, bias=const("rms_eps")), SB_A, "norm", l)
                act.wait_ge(SB_P.sem, SB_P.at("scores", l))
                run(f(w(MATS + 2048, 2, PAIR), pairs(0), ACT.Copy), SB_A, "scores", l)
                run(f(w(INV, 1536), w(MATS + 2048, 1536), ACT.Abs))
                run(f(w(INV, 1536), w(INV, 1536), ACT.Exp, scale=-1.0))
                run(f(w(INV, 1536), w(INV, 1536), ACT.Ln, bias=const("one")), SB_A, "ln", l)
                act.wait_ge(SB_V.sem, SB_V.at("logs", l))
                run(f(w(INV, 1536), w(INV, 1536), ACT.Exp), SB_A, "weights", l)

            def retention(l):
                run(f(w(MX, 512), w(PT + 16 * T, 512), ACT.Silu), RET_A, "silu", l)
                act.wait_ge(RET_P.sem, RET_P.at("var", l))
                run(f(w(INV + 1536, 512), bank(1), ACT.Sqrt, bias=const("ln_eps")), RET_A, "dev", l)

            def conv_front(l):
                run(f(w(MX + 1536, 512), w(PT + 20 * T, 512), ACT.Sigmoid), CV_A, "sigmoid", l)

            def conv_back(l):
                act.wait_ge(CV_P.sem, CV_P.at("var", l))
                run(f(w(MX + 1024, T), bank(1)[:, 0:T], ACT.Sqrt, bias=const("ln_eps")), CV_A, "dev", l)
                act.wait_ge(CV_V.sem, CV_V.at("affine", l))
                run(f(w(BR + 6 * T, 512), w(INV, 512), ACT.Silu), CV_A, "done", l)

            def ffn(name):
                first = FIRST_EXPERT[name]
                with act.Fori(0, N_PARTS[name]) as e:
                    for t in range(FT):
                        act.wait_ge(glu_full, (e + first) * FT + t + 1)
                        act.wait_ge(glu_done, (e + first) * FT + (t if t >= 2 else 1))
                        f(glu[:, t % 2, :], banks[:, 4 + t % 4, 0:T], ACT.Silu).then_inc(glu_silu, 1)

            def lru():
                run(f(small[:, 16:24], par("a_lambda", 0, KT), ACT.Abs))
                run(f(small[:, 16:24], small[:, 16:24], ACT.Exp, scale=-1.0), LR_A, "lambda")
                for q in range(8):
                    act.wait_ge(ain_full, q + 1)
                    src = banks[:, 4 + q % 4, :]
                    if q < 4:
                        ins = f(w(512 * q, 512), src, ACT.Gelu_apprx_tanh)
                    else:
                        dst = w(2048, KT, T + 4)[:, 2 * (q - 4):2 * (q - 4) + 2, 3:3 + T]
                        ins = f(dst, grid(src, 2), ACT.Copy)
                    chain.to(ins, ain_out, q + 1)
                for h in range(KT):
                    act.wait_ge(ag_full, h + 1)
                    src = banks[:, 4 + h % 4, :]
                    run(f(w(8192 + h * T, T), src[:, 0:T], ACT.Sigmoid, bias=par("a_gate_b", h)))
                    chain.to(f(w(10240 + h * T, T), src[:, T:2 * T], ACT.Sigmoid, bias=par("a_gate_b", KT + h)),
                             ag_out, h + 1)
                act.wait_ge(LR_V.sem, LR_V.at("log_a"))
                run(f(w(12288, 2048), w(8192, 2048), ACT.Exp))
                run(f(w(14336, 2048), w(8192, 2048), ACT.Tanh, scale=-1.0), LR_A, "exps")
                act.wait_ge(LR_V.sem, LR_V.at("square"))
                run(f(w(14336, 2048), w(14336, 2048), ACT.Sqrt), LR_A, "root")

            KC, EXW, HIDN, KR, KD, VSW, QR, GA, KCM, VCM = 0, 2048, 3968, 4224, 6272, 8320, 9344, 11392, 11520, 11584

            def kv():
                for n in range(2):
                    act.wait_ge(kv_full, n + 1)
                    src = grid(banks[:, 4 + n, :], 2)
                    dst = w(KC + 1024 * n, G, T)
                    for r in range(2):
                        run(f(dst[0:HD, r::2, :], src[half(r), :, :], ACT.Copy))
                        ins = f(dst[HD:P, r::2, 0:T - 1], src[half(r), :, 1:T], ACT.Copy)
                        if r:
                            chain.to(ins, kv_out, n + 1)
                        else:
                            run(ins)
                for n in range(2):
                    act.wait_ge(kv_full, n + 3)
                    chain.to(f(w(KR + 512 * n, 512), banks[:, 6 + n, :], ACT.Copy), kv_out, n + 3)
                for n in range(2):
                    act.wait_ge(kv_full, n + 5)
                    chain.to(f(w(VSW + 512 * n, 512), banks[:, 4 + n, :], ACT.Copy), kv_out, n + 5)
                for v in range(2):
                    act.wait_ge(KV_P.sem, KV_P.at(f"hidden{v}"))
                    for m in range(2):
                        ins = f(w(HIDN + 128 * v + 64 * m, G * NC), bank(v)[:, 64 * m:64 * m + G * NC],
                                ACT.Gelu_apprx_tanh, bias=par("cmp_b1", 2 * v + m))
                        if m:
                            run(ins, KV_A, f"hidden{v}")
                        else:
                            run(ins)
                act.wait_ge(KV_P.sem, KV_P.at("k_cmp"))
                run(f(w(KCM, G * NC), bank(2)[:, 0:G * NC], ACT.Identity, bias=par("cmp_b2k")), KV_A, "k_cmp")
                act.wait_ge(KV_P.sem, KV_P.at("cmp_mean"))
                run(f(w(EXW, G * NC), bank(3)[:, 0:G * NC], ACT.Sqrt, bias=const("rms_eps")), KV_A, "cmp_norm")
                act.wait_ge(KV_P.sem, KV_P.at("k_mean"))
                run(f(w(EXW + 64, 1024), bank(0, 2), ACT.Sqrt, bias=const("rms_eps")), KV_A, "k_norm")
                act.wait_ge(KV_V.sem, KV_V.at("k_rope"))
                for b in range(2):
                    for d in range(2):
                        for r in range(2):
                            ins = f(w(KD + 1024 * b, G, T)[half(d), r::2, :], w(KR + 512 * b, 2, T)[half(r), :, :], ACT.Copy)
                            if (b, d, r) == (1, 1, 1):
                                run(ins, KV_A, "k_copies")
                            else:
                                run(ins)

            def queries():
                for q in range(4):
                    act.wait_ge(Q_P.sem, Q_P.at(f"full{q}"))
                    run(f(w(QR + 512 * q, 512), banks[:, 4 + q, :], ACT.Copy), Q_A, f"out{q}")
                act.wait_ge(Q_P.sem, Q_P.at("gates"))
                run(f(w(GA, 96), bank(0)[:, 0:96], ACT.Sigmoid), Q_A, "gates")
                act.wait_ge(Q_P.sem, Q_P.at("mean"))
                run(f(w(16896, 2048), bank(0, 4), ACT.Sqrt, bias=const("rms_eps")), Q_A, "norm")

            def attend(u):
                a = u % TT
                n = P * (a + 1)
                act.wait_ge(AT_V.sem, AT_V.at("masked", u))
                for b in range(2):
                    for h in range(4):
                        s = w(16896 + 1024 * b + h * n, n)
                        run(f(s, s, ACT.Exp, bias=small[:, 32 + 4 * b + h:33 + 4 * b + h],
                              accum_out=small[:, 48 + 4 * b + h:49 + 4 * b + h]))
                for h in range(4):
                    s = w(18944 + h * NC, NC)
                    ins = f(s, s, ACT.Exp, bias=small[:, 40 + h:41 + h], accum_out=small[:, 56 + h:57 + h])
                    if h == 3:
                        run(ins, AT_A, "exps", u)
                    else:
                        run(ins)
                act.wait_ge(AT_P.sem, AT_P.at("turned", u))
                run(f(w(19456, 2048)[:, 0:4 * n], bank(0, 2)[:, 0:4 * n], ACT.Copy))
                run(f(w(20480, 2048)[:, 0:4 * n], bank(2, 2)[:, 0:4 * n], ACT.Copy))
                run(f(w(21504, 512, rows=slice(0, NC)), bank(5, rows=slice(0, NC)), ACT.Copy), AT_A, "turned", u)
                act.wait_ge(AT_P.sem, AT_P.at("out", u))
                g = u // TT
                run(f(w(22016, KT, T)[:, 2 * g:2 * g + 2, a * P:a * P + P], grid(bank(6)[:, 0:2 * P], 2), ACT.Copy),
                    AT_A, "out", u)

            for l in range(2):
                norm(2 * l)
                win(l)
                rwkv_front(l)
                for n in range(LEVELS):
                    gates(l, [n])
                    rwkv_level(l, n)
                gates(l, [7])
                rwkv_back(l)
                stick(l)
                retention(l)
                conv_front(l)
                conv_back(l)
                norm(2 * l + 1)
                if l == 0:
                    ffn("dense")
                else:
                    act.wait_ge(RT_V.sem, RT_V.at("gap"))
                    run(f(small[:, 4:6], small[:, 6:8], ACT.Exp), RT_A, "exp")
                    ffn("moe")
            norm(4)
            lru()
            norm(5)
            ffn("f0")
            norm(6)
            kv()
            norm(7)
            queries()
            for u in range(2 * G):
                attend(u)
            norm(8)
            ffn("f1")

        @block.tensor
        def _(pe):
            slab = [0]

            def take(n=None):
                n = slab[0]
                pe.wait_ge(landed[n % RING], 16 * (n // RING + 1))
                slab[0] += 1
                return ring[:, n % RING, :]

            def mm(out_, lhsT, rhs, start=True, stop=True, **kw):
                return pe.matmul(out_, lhsT, rhs, start=start, stop=stop, **kw)

            def used():
                pe.sem_inc(slab_used, 1)

            def feature_tile(out_, cols, width=512):
                for k in range(KT):
                    ins = mm(out_, cols(k), hT[:, k, :], k == 0, k == KT - 1)
                return ins

            def norm(n):
                pe.wait_ge(NORM_V.sem, NORM_V.at("rows", n))
                for k in range(KT):
                    for a in range(TT):
                        at = (k % 2) * T + a * P
                        ins = pe.transpose(bank(k // 2)[:, at:at + P], scr[:, a * D + k * P:a * D + k * P + P],
                                           const("ident"))
                NORM_P.mark(ins, "done", n)
                pe.wait_ge(NORM_V.sem, NORM_V.at("hT", n))

            def two_tiles(s, q, out_):
                for j in range(2):
                    c = (2 * q + j) * P
                    ins = feature_tile(out_[:, j * T:j * T + T], lambda k: s[:, k * 512 + c:k * 512 + c + P])
                return ins

            def token_tile(s, a, out_, lhs):
                for k in range(KT):
                    ins = mm(out_, lhs[:, k, a * P:a * P + P], s[:, k * 512:k * 512 + 512], k == 0, k == KT - 1)
                return ins

            def fill(s, q, tile, full, out_sem, base, n, last):
                if n >= 4:
                    pe.wait_ge(out_sem, base + n - 3)
                two_tiles(s, q, banks[:, 4 + n % 4, :]).then_inc(full, 1)
                if last:
                    pe.wait_ge(full, base + n + 1)
                    used()

            def win(l):
                base = 13 * l
                n = 0
                for c in range(7):
                    s = take()
                    for q in range(1 if c == 6 else 2):
                        if c == 4:
                            pe.wait_ge(win_out, base + n - 3)
                            token_tile(s, q, banks[:, 4 + n % 4, :], hT).then_inc(win_full, 1)
                            if q == 1:
                                pe.wait_ge(win_full, base + n + 1)
                                used()
                        else:
                            fill(s, q, None, win_full, win_out, base, n, q == 1 or c == 6)
                        n += 1

            def gates(l, slabs):
                for c in slabs:
                    s = take()
                    for q in range(2):
                        n = 2 * c + q
                        if n >= 2:
                            pe.wait_ge(gate_out, 16 * l + n - 1)
                        else:
                            pe.wait_ge(win_out, 13 * l + 13)
                        two_tiles(s, q, banks[:, 6 + q, :]).then_inc(gate_full, 1)
                    pe.wait_ge(gate_full, 16 * l + 2 * c + 2)
                    used()

            def mat(q, m):
                return w(MATS + 1024 * q + P * m, P)

            def chunk(at, h, c):
                return w(at + (h // 2) * T + c * P, P, rows=half(h % 2))

            AT_, BT_, KT_, RT_ = PT, PT + 512, PT + 1024, PT + 1536

            def rwkv_front(l):
                pe.wait_ge(RW_A.sem, RW_A.at("lora", l))
                for j in range(2):
                    mm(bank(0)[:, j * T:j * T + T], par(f"w2a2{l}", j * P, P, half(0)), w(INV + 3584, T, rows=half(0)))
                for j in range(2):
                    mm(bank(1)[:, j * T:j * T + T], par(f"w2a2{l}", j * P, P, half(1)), w(MX + 6 * T, T, rows=half(1)))
                for j in range(2):
                    ins = mm(bank(2)[:, j * T:j * T + T], par(f"g2{l}", j * P, P), w(INV + 3840, T))
                RW_P.mark(ins, "lora", l)
                pe.wait_ge(RW_V.sem, RW_V.at("k_squared", l))
                RW_P.mark(mm(bank(3), const("head_sum"), w(INV + 512, 512)), "squares", l)
                pe.wait_ge(RW_V.sem, RW_V.at("operands", l))
                mm(bank(3), const("head_sum"), w(MX, 512))
                for c in range(2):
                    for j in range(2):
                        pe.transpose(bank(4)[:, c * T + j * P:c * T + j * P + P],
                                     w(MX + (4 + j) * T + c * P, P), const("ident"))
                for i, at in enumerate((BT_, KT_)):
                    for j in range(2):
                        ins = pe.transpose(bank(5)[:, i * T + j * P:i * T + j * P + P],
                                           w(at + j * T, P), const("ident"))
                RW_P.mark(ins, "bonus", l)
                pe.wait_ge(RW_V.sem, RW_V.at("bonus_used", l))
                for i, pairs in enumerate((((BT_, AT_), (KT_, AT_)), ((BT_, RT_), (KT_, RT_)))):
                    if i:
                        pe.wait_ge(RW_V.sem, RW_V.at("mats0", l))
                    for q, (lhs, rhs) in enumerate(pairs):
                        for c in range(2):
                            for h in range(NH):
                                at = matrix(h, c) * P
                                ins = mm(bank(2 * q, 2)[:, at:at + P], chunk(lhs, h, c), chunk(rhs, h, c))
                    RW_P.mark(ins, f"mats{i}", l)
                pe.wait_ge(RW_V.sem, RW_V.at("mats1", l))

            def rwkv_level(l, n):
                X, XT, TM, LM = INV, INV + 1024, INV + 2048, LEVEL_AT[n % 2]
                pe.wait_ge(RW_G.sem, RW_G.at(f"M{n}", l))
                if n:
                    pe.wait_ge(RW_V.sem, RW_V.at(f"X{n - 1}", l))
                for m in range(8):
                    ins = mm(bank(0, 2)[:, m * P:m * P + P], w(LM + m * P, P), w(X + m * P, P))
                RW_P.mark(ins, f"T{n}", l)
                pe.wait_ge(RW_A.sem, RW_A.at(f"T{n}", l))
                for m in range(8):
                    ins = mm(bank(2, 2)[:, m * P:m * P + P], w(TM + m * P, P), w(XT + m * P, P))
                if n < LEVELS - 1:
                    for m in range(8):
                        ins = mm(bank(4, 2)[:, m * P:m * P + P], w(XT + m * P, P), w(TM + m * P, P))
                RW_P.mark(ins, f"X{n}", l)

            def rwkv_back(l):
                pe.wait_ge(RW_V.sem, RW_V.at(f"X{LEVELS - 1}", l))
                vrow, brow, krow = 1024, 1536, 1792
                for c in range(2):
                    for h in range(NH):
                        o = bank(h % 2)[:, (h // 2) * HD:(h // 2) * HD + HD]
                        ins = mm(o, mat(1, matrix(h, c)), scr[:, vrow + c * T + h * HD:vrow + c * T + h * HD + HD],
                                 True, c == 0)
                        if c:
                            ins = mm(o, chunk(AT_, h, 1), w(MX + 768 + (h // 2) * HD, HD, rows=half(h % 2)),
                                     False, True)
                    RW_P.mark(ins, f"w{c}", l)
                    pe.wait_ge(RW_A.sem, RW_A.at(f"w{c}", l))
                    for h in range(NH):
                        ins = mm(bank(2)[:, h * HD:h * HD + HD], w(INV + 1024 + matrix(h, c) * P, P),
                                 w(MX + (h % 2) * 2 * HD + (h // 2) * HD, HD))
                    RW_P.mark(ins, f"u{c}", l)
                    pe.wait_ge(RW_A.sem, RW_A.at(f"u{c}", l))
                    if c == 0:
                        for h in range(NH):
                            o = bank(4, rows=half(h % 2))[:, (h // 2) * HD:(h // 2) * HD + HD]
                            mm(o, scr[:, krow + h * HD:krow + h * HD + HD], scr[:, vrow + h * HD:vrow + h * HD + HD],
                               True, False)
                            ins = mm(o, scr[:, brow + h * HD:brow + h * HD + HD], w(MX + 256 + h * HD, HD),
                                     False, True)
                        RW_P.mark(ins, "state", l)
                        pe.wait_ge(RW_V.sem, RW_V.at("state", l))
                for h in range(NH):
                    for c in range(2):
                        o = bank(3, rows=half(h % 2))[:, (h // 2) * T + c * P:(h // 2) * T + c * P + P]
                        mm(o, w(MX + 256 + 256 * c + h * HD, HD), mat(2, matrix(h, c)), True, False)
                        ins = mm(o, scr[:, vrow + c * T + h * HD:vrow + c * T + h * HD + HD], mat(3, matrix(h, c)),
                                 False, c == 0)
                        if c:
                            ins = mm(o, w(MX + 768 + (h // 2) * HD, HD, rows=half(h % 2)), chunk(RT_, h, 1),
                                     False, True)
                RW_P.mark(ins, "y", l)
                pe.wait_ge(RW_V.sem, RW_V.at("y", l))
                RW_P.mark(mm(bank(4), const("head_mean"), w(INV, 512)), "mean", l)
                pe.wait_ge(RW_V.sem, RW_V.at("centred", l))
                RW_P.mark(mm(bank(5), const("head_mean"), w(INV + 1024, 512)), "var", l)

            def scores(q, k, b):
                for t in range(2):
                    for r in range(2):
                        mm(bank(b + 2 * r)[:, t * T:t * T + T], w(k + t * T, P, rows=half(r)), w(q + t * T, T, rows=half(r)))
                for t in range(2):
                    for r in range(2):
                        ins = mm(bank(b + 2 * r + 1)[:, t * P:t * P + P], w(k + t * T + P, P, rows=half(r)),
                                 w(q + t * T + P, P, rows=half(r)))
                return ins

            def weighted(b, v0, at):
                for h in range(NH):
                    r, t = h % 2, h // 2
                    o = bank(b, rows=half(r))[:, t * T:t * T + T]
                    mm(o, vt[:, 0, v0 + h * HD:v0 + h * HD + HD], w(at + r * PAIR + t * T, T), True, False)
                    ins = mm(o[:, P:T], vt[:, 1, v0 + h * HD:v0 + h * HD + HD], w(at + r * PAIR + 2 * T + t * P, P),
                             False, True)
                return ins

            def stick(l):
                pe.wait_ge(SB_V.sem, SB_V.at("squares", l))
                for j in range(2):
                    ins = mm(bank(j), const("head_mean"), w(MATS + 512 * j, 512))
                SB_P.mark(ins, "squares", l)
                pe.wait_ge(SB_V.sem, SB_V.at("qk", l))
                SB_P.mark(scores(PT + 8 * T, PT + 10 * T, 0), "scores", l)
                pe.wait_ge(SB_V.sem, SB_V.at("softplus", l))
                for r in range(2):
                    first, second = MATS + r * PAIR, MATS + r * PAIR + 2 * T
                    mm(bank(2 * r), const("suffix"), w(first, 2 * T), True, False)
                    for t in range(2):
                        mm(bank(2 * r)[:, t * T + P:t * T + T], const("ones"), w(second + t * P, P), False, t == 1)
                    ins = mm(bank(2 * r + 1)[:, 0:2 * P], const("suffix"), w(second, 2 * P))
                SB_P.mark(ins, "suffix", l)
                pe.wait_ge(SB_A.sem, SB_A.at("weights", l))
                SB_P.mark(weighted(4, 0, INV), "out", l)

            def retention(l):
                pe.wait_ge(SB_V.sem, SB_V.at("done", l))
                for j in range(2):
                    ins = mm(bank(j), const("swap"), w(PT + 12 * T + 512 * j, 512))
                RET_P.mark(ins, "rotated", l)
                pe.wait_ge(RET_V.sem, RET_V.at("qk", l))
                RET_P.mark(scores(PT + 12 * T, PT + 14 * T, 0), "scores", l)
                pe.wait_ge(RET_V.sem, RET_V.at("scores", l))
                RET_P.mark(weighted(5, 256, MATS), "out", l)
                pe.wait_ge(RET_V.sem, RET_V.at("y", l))
                RET_P.mark(mm(bank(0), const("head_mean"), w(INV, 512)), "mean", l)
                pe.wait_ge(RET_V.sem, RET_V.at("centred", l))
                RET_P.mark(mm(bank(1), const("head_mean"), w(INV + 1024, 512)), "var", l)

            def conv(l):
                pe.wait_ge(CV_V.sem, CV_V.at("conv", l))
                for j in range(2):
                    ins = mm(bank(0)[:, 0:T], const("ones"), w(MX + 512 + j * T, T), j == 0, j == 1)
                CV_P.mark(ins, "mean", l)
                pe.wait_ge(CV_V.sem, CV_V.at("centred", l))
                for j in range(2):
                    ins = mm(bank(1)[:, 0:T], const("ones"), w(INV + 1024 + j * T, T), j == 0, j == 1)
                CV_P.mark(ins, "var", l)

            def branches(l):
                pe.wait_ge(RET_V.sem, RET_V.at("done", l))
                for c in range(2):
                    if c:
                        pe.wait_ge(CV_A.sem, CV_A.at("done", l))
                    s = take()
                    for i in range(2):
                        for q in range(4):
                            n = 8 * c + 4 * i + q
                            if n >= 4:
                                pe.wait_ge(br_out, 16 * l + n - 3)
                            else:
                                pe.wait_ge(gate_out, 16 * l + 16)
                            for j in range(2):
                                for k in range(2):
                                    at = (2 * i + k) * D + (2 * q + j) * P
                                    ins = mm(banks[:, 4 + n % 4, j * T:j * T + T], s[:, at:at + P],
                                             br[:, 2 * (2 * c + i) + k, :], k == 0, k == 1)
                            ins.then_inc(br_full, 1)
                    pe.wait_ge(br_full, 16 * l + 8 * c + 8)
                    used()

            def project(r, lhs):
                for c in range(2):
                    s = take()
                    for a in range(TT):
                        ins = token_tile(s, a, banks[:, 2 * c + a, :], lhs)
                    ins.then_inc(proj_full, 1)
                    pe.wait_ge(proj_full, 2 * r + c + 1)
                    used()

            def ffn(name):
                first, slab0 = FIRST_EXPERT[name], slab[0]
                with pe.Fori(0, N_PARTS[name]) as e:
                    def taken(j):
                        n = slab0 + j
                        pe.wait_ge(landed[n % RING], e * (16 * EXPERT_SLABS // RING) + 16 * (n // RING + 1))
                        return ring[:, n % RING, :]

                    for j in range(IN_SLABS):
                        s = taken(j)
                        for t in range(2 * j, min(2 * j + 2, FT)):
                            if t >= 4:
                                pe.wait_ge(glu_done, (e + first) * FT + t - 2)
                            for m in range(2):
                                c = m * 2 * P + (t % 2) * P
                                ins = feature_tile(banks[:, 4 + t % 4, m * T:m * T + T],
                                                   lambda k: s[:, k * 512 + c:k * 512 + c + P])
                            ins.then_inc(glu_full, 1)
                        pe.wait_ge(glu_full, (e + first) * FT + min(2 * j + 2, FT))
                        used()
                    pe.wait_ge(ffn_added, (e + first) * 4 + 1)
                    for k in range(FT):
                        if k % 4 == 0:
                            s = taken(IN_SLABS + k // 4)
                        pe.wait_ge(glu_done, (e + first) * FT + k + 2)
                        for b in range(4):
                            at = (k % 4) * D + (b % 2) * 512
                            ins = mm(banks[:, b, :], w(k * T + (b // 2) * P, P), s[:, at:at + 512],
                                     k == 0, k == FT - 1)
                        if k % 4 == 3:
                            ins.then_inc(slab_used, 1)
                    ins.then_inc(ffn_full, 1)
                    pe.wait_ge(ffn_full, e + first + 1)
                    used()
                slab[0] += EXPERT_SLABS * N_PARTS[name]

            def lru():
                for c in range(4):
                    s = take()
                    for q in range(2):
                        fill(s, q, None, ain_full, ain_out, 0, 2 * c + q, q == 1)
                s = take()
                pe.wait_ge(LR_V.sem, LR_V.at("conv"))
                for h in range(KT):
                    if h < 4:
                        pe.wait_ge(ain_out, 5 + h)
                    else:
                        pe.wait_ge(ag_out, h - 3)
                    for g in range(2):
                        ins = mm(banks[:, 4 + h % 4, g * T:g * T + T], s[:, g * D + h * P:g * D + h * P + P],
                                 w(6144 + h * T, T))
                    ins.then_inc(ag_full, 1)
                pe.wait_ge(ag_full, KT)
                used()
                pe.wait_ge(LR_V.sem, LR_V.at("done"))
                project(2, w(6144, KT, T))

            KC, EXW, HIDN, KR, KD, VSW, QR, GA, KCM, VCM = 0, 2048, 3968, 4224, 6272, 8320, 9344, 11392, 11520, 11584

            def kv():
                for c in range(2):
                    s = take()
                    for q in range(2):
                        two_tiles(s, q, banks[:, 4 + 2 * c + q, :]).then_inc(kv_full, 1)
                    pe.wait_ge(kv_full, 2 * c + 2)
                    used()
                s = take()
                for a in range(TT):
                    pe.wait_ge(kv_out, a + 1)
                    token_tile(s, a, banks[:, 4 + a, :], hT).then_inc(kv_full, 1)
                pe.wait_ge(kv_full, 6)
                used()
                pe.wait_ge(KV_V.sem, KV_V.at("windows"))
                for v in range(2):
                    s = take()
                    for m in range(2):
                        for j in range(CB // 2):
                            ins = mm(bank(v)[:, 64 * m:64 * m + G * NC], s[:, j * HID + m * P:j * HID + m * P + P],
                                     w(EXW + 960 * v + j * G * NC, G * NC), j == 0, j == CB // 2 - 1)
                    KV_P.mark(ins, f"hidden{v}")
                    pe.wait_ge(KV_P.sem, KV_P.at(f"hidden{v}"))
                    used()
                pe.wait_ge(KV_A.sem, KV_A.at("hidden1"))
                for m in range(2):
                    ins = mm(bank(2)[:, 0:G * NC], par("cmp_w2k", m * P, P), w(HIDN + 64 * m, G * NC), m == 0, m == 1)
                KV_P.mark(ins, "k_cmp")
                pe.wait_ge(KV_V.sem, KV_V.at("cmp_squares"))
                KV_P.mark(mm(bank(3)[:, 0:G * NC], const("head_mean"), w(EXW, G * NC)), "cmp_mean")
                pe.wait_ge(KV_V.sem, KV_V.at("cmp_normed"))
                KV_P.mark(mm(bank(2)[:, 0:G * NC], const("swap"), w(KCM, G * NC)), "cmp_rot")
                r = slice(0, NC)
                for g in range(G):
                    o = bank(3, rows=r)[:, g * HD:g * HD + HD]
                    for m in range(2):
                        mm(o, w(HIDN + 128 + 64 * m + g * NC, NC), par("cmp_w2v", m * HD, HD), m == 0, False)
                    at, _ = CONSTS["ones"]
                    ins = mm(o, consts[0:1, at:at + NC], par("cmp_b2v", 0, HD, slice(0, 1)), False, True)
                KV_P.mark(ins, "v_cmp")
                pe.wait_ge(KV_V.sem, KV_V.at("k_squares"))
                for j in range(2):
                    ins = mm(bank(j), const("head_mean"), w(EXW + 64 + 512 * j, 512))
                KV_P.mark(ins, "k_mean")
                pe.wait_ge(KV_V.sem, KV_V.at("k_normed"))
                for j in range(2):
                    ins = mm(bank(j), const("swap"), w(KR + 512 * j, 512))
                KV_P.mark(ins, "k_rot")

            def queries():
                for c in range(2):
                    s = take()
                    for q in range(2):
                        Q_P.mark(two_tiles(s, q, banks[:, 4 + 2 * c + q, :]), f"full{2 * c + q}")
                    pe.wait_ge(Q_P.sem, Q_P.at(f"full{2 * c + 1}"))
                    used()
                for a in range(TT):
                    o = bank(0)[:, a * 48:a * 48 + 48]
                    for k in range(KT):
                        mm(o, hT[:, k, a * P:a * P + P], par("gate_w", k * 48, 48), k == 0, False)
                    at, _ = CONSTS["ones"]
                    ins = mm(o, consts[0:1, at:at + P], par("gate_b", 0, 48, slice(0, 1)), False, True)
                Q_P.mark(ins, "gates")
                pe.wait_ge(Q_A.sem, Q_A.at("gates"))
                pe.wait_ge(Q_V.sem, Q_V.at("squares"))
                for j in range(4):
                    ins = mm(bank(j), const("head_mean"), w(16896 + 512 * j, 512))
                Q_P.mark(ins, "mean")
                pe.wait_ge(Q_V.sem, Q_V.at("normed"))
                for j in range(4):
                    ins = mm(bank(j), const("swap"), w(QR + 512 * j, 512))
                Q_P.mark(ins, "rot")
                pe.wait_ge(Q_V.sem, Q_V.at("rope"))
                pe.wait_ge(KV_A.sem, KV_A.at("k_copies"))
                pe.wait_ge(KV_V.sem, KV_V.at("v_cmp"))

            def attend(u):
                g, a = u // TT, u % TT
                n = P * (a + 1)
                if u:
                    pe.wait_ge(AT_A.sem, AT_A.at("out", u - 1))
                for b in range(2):
                    for t in range(2):
                        for r in range(2):
                            mm(bank(2 * b + r)[:, t * n:t * n + n], w(QR + (2 * g + t) * T + a * P, P, rows=half(r)),
                               w(KD + 1024 * b + g * T, n, rows=half(r)))
                for t in range(2):
                    for r in range(2):
                        ins = mm(bank(4 + r)[:, t * NC:t * NC + NC], w(QR + (2 * g + t) * T + a * P, P, rows=half(r)),
                                 w(KCM + g * NC, NC, rows=half(r)))
                AT_P.mark(ins, "scores", u)
                pe.wait_ge(AT_V.sem, AT_V.at("probs", u))
                for b in range(2):
                    for i in range(4):
                        for c in range(a + 1):
                            pe.transpose(bank(2 * b, 2)[:, i * n + c * P:i * n + c * P + P],
                                         w(16896 + 1024 * b + i * n + c * P, P), const("ident"))
                for i in range(4):
                    ins = pe.transpose(bank(5, rows=slice(0, NC))[:, i * P:i * P + P], w(18944 + i * NC, NC),
                                       const("ident"))
                AT_P.mark(ins, "turned", u)
                pe.wait_ge(AT_A.sem, AT_A.at("turned", u))
                for i in range(4):
                    o = bank(6, rows=half(i // 2))[:, (i % 2) * P:(i % 2) * P + P]
                    mm(o, w(VCM + g * HD, HD, rows=slice(0, NC)), w(21504 + i * P, P, rows=slice(0, NC)), True, False)
                    for b in range(2):
                        for c in range(a + 1):
                            ins = mm(o, w(VSW + 512 * c + 256 * b + g * HD, HD),
                                     w(19456 + 1024 * b + i * n + c * P, P), False, b == 1 and c == a)
                AT_P.mark(ins, "out", u)

            for l in range(2):
                norm(2 * l)
                win(l)
                rwkv_front(l)
                for n in range(LEVELS):
                    gates(l, [n])
                    rwkv_level(l, n)
                gates(l, [7])
                rwkv_back(l)
                stick(l)
                retention(l)
                conv(l)
                branches(l)
                pe.wait_ge(br_out, 16 * l + 16)
                project(l, scr[:, :].rearrange("p (k t) -> p k t", k=KT))
                norm(2 * l + 1)
                if l == 0:
                    ffn("dense")
                else:
                    for a in range(TT):
                        for k in range(KT):
                            ins = mm(bank(0)[:, a * NE:a * NE + NE], hT[:, k, a * P:a * P + P],
                                     par("router", k * NE, NE), k == 0, k == KT - 1)
                    RT_P.mark(ins, "logits")
                    ffn("moe")
            norm(4)
            lru()
            norm(5)
            ffn("f0")
            norm(6)
            kv()
            norm(7)
            queries()
            for u in range(2 * G):
                attend(u)
            pe.wait_ge(AT_A.sem, AT_A.at("out", 2 * G - 1))
            project(3, w(22016, KT, T))
            norm(8)
            ffn("f1")
            assert slab[0] == n_slabs

        @block.vector
        def _(dve):
            chain = Chain(dve, v_chain)
            run = chain.run
            tt, ts, stt = dve.tensor_tensor, dve.tensor_scalar, dve.scalar_tensor_tensor
            MUL, ADD, SUB, MAX = ALU.mult, ALU.add, ALU.subtract, ALU.max

            def bc(ap, n):
                return ap.unsqueeze(1).to_broadcast([ap.shape[0], n, ap.shape[1]])

            def bc22(ap):
                return ap.unsqueeze(1).unsqueeze(1).to_broadcast([P, 2, 2, P])

            chain.to(dve.memset(ones_gates[:, 0, :], 1.0), glu_done, 1)
            chain.to(dve.memset(ones_gates[:, 1, :], 1.0), ffn_added, 1)

            def norm(n, gain):
                dve.wait_ge(NORM_A.sem, NORM_A.at("root", n))
                run(dve.reciprocal(small[:, 0:2], small[:, 2:4]))
                for a in range(TT):
                    ins = ts(scr[:, a * D:a * D + D], x[:, a, :], small[:, a:a + 1], None, MUL)
                    if a:
                        run(ins, NORM_V, "rows", n)
                    else:
                        run(ins)
                dve.wait_ge(NORM_P.sem, NORM_P.at("done", n))
                for k in range(KT):
                    ins = ts(hT[:, k, :], bank(k // 2)[:, (k % 2) * T:(k % 2) * T + T], par(gain, k), None, MUL)
                    if k == KT - 1:
                        run(ins, NORM_V, "hT", n)
                    else:
                        run(ins)

            def rwkv_front(l):
                dve.wait_ge(win_out, 13 * l + 4)
                p, d = w(PT, 8, T), w(INV, 8, T)
                run(tt(d[:, :, 1:T], p[:, :, 0:T - 1], p[:, :, 1:T], SUB))
                run(ts(d[:, :, 0:1], p[:, :, 0:1], -1.0, None, MUL))
                m = w(MX, 8, T)
                for j in range(8):
                    ins = stt(m[:, j, :], d[:, j, :], par(f"mu{l}", j), p[:, j, :], MUL, ADD)
                    if j == 7:
                        run(ins, RW_V, "mixed", l)
                    else:
                        run(ins)
                r, k, v, a = (w(MX + 512 * i, 512) for i in range(4))
                kk, sq, rinv = w(INV, 512), w(INV + 512, 512), w(INV + 1024, 512)
                sw, c, cex = w(INV + 1536, 512), w(INV + 2048, 512), w(INV + 2560, 512)
                e1, e2, e3 = w(PT, 512), w(INV + 3072, 512), w(PT + 1536, 512)
                at_, bt_, kt_, rt_ = (w(PT + 512 * i, 512) for i in range(4))
                for j in range(2):
                    run(ts(kk[:, j * T:j * T + T], k[:, j * T:j * T + T], par(f"k_k{l}", j), None, MUL))
                run(tt(sq, kk, kk, MUL), RW_V, "k_squared", l)
                dve.wait_ge(RW_A.sem, RW_A.at("sigmoids", l))
                run(ts(sw, sw, -DECAY_SCALE, None, MUL))
                for j in range(4):
                    s = slice(j * P, j * P + P)
                    run(dve.tensor_tensor_scan(c[:, s], const("ones"), sw[:, s], 0.0, MUL, ADD))
                run(tt(cex, c, sw, SUB), RW_V, "decays", l)
                dve.wait_ge(RW_A.sem, RW_A.at("norm", l))
                run(ts(rinv, rinv, 1e-12, None, MAX))
                run(dve.reciprocal(rinv, rinv))
                run(tt(kk, kk, rinv, MUL))
                for j in range(2):
                    s = slice(j * T, j * T + T)
                    run(ts(sq[:, s], a[:, s], 1.0, par(f"k_a{l}", j), SUB, MUL))
                run(stt(k, sq, 1.0, k, ADD, MUL))
                run(tt(sw, kk, a, MUL))
                dve.wait_ge(RW_A.sem, RW_A.at("exps", l))
                run(stt(at_, kk, -1.0, e1, MUL, MUL))
                run(tt(bt_, sw, e2, MUL))
                run(tt(kt_, k, e2, MUL))
                run(tt(rt_, r, e3, MUL))
                for j in range(2):
                    s = slice(j * T, j * T + T)
                    ins = stt(r[:, s], r[:, s], par(f"r_k{l}", j), k[:, s], MUL, MUL)
                    if j:
                        run(ins, RW_V, "operands", l)
                    else:
                        run(ins)
                dve.wait_ge(RW_P.sem, RW_P.at("bonus", l))
                run(tt(scr[:, 512:1024], bank(3), v, MUL), RW_V, "bonus_used", l)
                dve.wait_ge(RW_G.sem, RW_G.at("zeroed", l))
                for i in range(2):
                    dve.wait_ge(RW_P.sem, RW_P.at(f"mats{i}", l))
                    mask = bc(const("causal" if i else "strict").bitcast(I32), 8)
                    for q in range(2):
                        ins = dve.copy_predicated(w(MATS + 1024 * (2 * i + q), 8, P), mask, grid(bank(2 * q, 2), 8))
                        if q:
                            run(ins, RW_V, f"mats{i}", l)
                        else:
                            run(ins)
                    if i == 0:
                        for at in (INV, INV + 1024):
                            run(dve.tensor_copy(w(at, 8, P), bc(const("ident"), 8)))

            def rwkv_level(l, n):
                dve.wait_ge(RW_P.sem, RW_P.at(f"X{n}", l))
                xt = w(INV + 1024, 1024)
                if n < LEVELS - 1:
                    run(tt(w(INV, 1024), w(INV, 1024), bank(4, 2), ADD))
                run(tt(xt, xt, bank(2, 2), ADD), RW_V, f"X{n}", l)

            def head_norm(b_mean, P_, V_, A_, y, xc, sq, dev, l):
                dve.wait_ge(P_.sem, P_.at("mean", l))
                run(tt(xc, y, bank(b_mean), SUB))
                run(tt(sq, xc, xc, MUL), V_, "centred", l)
                dve.wait_ge(A_.sem, A_.at("dev", l))
                run(dve.reciprocal(dev, dev))
                run(tt(y, xc, dev, MUL))

            def rwkv_back(l):
                dve.wait_ge(RW_P.sem, RW_P.at("state", l))
                for j in range(2):
                    ins = ts(w(MX + 768 + j * HD, HD), bank(4)[:, j * HD:j * HD + HD], small[:, 8 + j:9 + j], None, MUL)
                    if j:
                        run(ins, RW_V, "state", l)
                    else:
                        run(ins)
                dve.wait_ge(RW_P.sem, RW_P.at("y", l))
                y, xc, sq, dev = (w(INV + 512 * i, 512) for i in range(4))
                run(dve.tensor_copy(y, bank(3)), RW_V, "y", l)
                head_norm(4, RW_P, RW_V, RW_A, y, xc, sq, dev, l)
                for j in range(2):
                    s = slice(j * T, j * T + T)
                    run(ts(y[:, s], y[:, s], par(f"ln_w{l}", j), par(f"ln_b{l}", j), MUL, ADD))
                run(tt(y, y, scr[:, 512:1024], ADD))
                run(tt(w(BR, 512), y, scr[:, 0:512], MUL), RW_V, "done", l)

            def stick(l):
                qk, sq = w(PT + 8 * T, 1024), w(MATS, 1024)
                run(tt(sq, qk, qk, MUL), SB_V, "squares", l)
                dve.wait_ge(SB_A.sem, SB_A.at("norm", l))
                run(dve.reciprocal(sq, sq))
                run(tt(qk, qk, sq, MUL))
                run(ts(qk[:, 0:512], qk[:, 0:512], par(f"sb_q{l}"), HD ** -0.5, MUL, MUL))
                run(ts(qk[:, 512:1024], qk[:, 512:1024], par(f"sb_k{l}"), None, MUL), SB_V, "qk", l)
                z, ln, sp_ = w(MATS + 2048, 1536), w(INV, 1536), w(MATS, 1536)
                dve.wait_ge(SB_A.sem, SB_A.at("ln", l))
                run(stt(sp_, z, 0.0, ln, MAX, ADD))
                first, second = diagonals(MATS)
                run(tt(first, first, bc22(const("strict")), MUL))
                run(tt(second, second, bc22(const("strict")), MUL), SB_V, "softplus", l)
                dve.wait_ge(SB_P.sem, SB_P.at("suffix", l))
                run(tt(w(INV, 2, PAIR), w(MATS + 2048, 2, PAIR), pairs(0), SUB))
                first, second = diagonals(INV)
                run(tt(first, first, bc22(const("not_before")), ADD))
                run(tt(second, second, bc22(const("not_before")), ADD), SB_V, "logs", l)
                dve.wait_ge(SB_P.sem, SB_P.at("out", l))
                run(dve.tensor_copy(w(BR + 512, 512), bank(4)), SB_V, "done", l)

            def rotate(dst, rot, cos, sin, tmp, groups, steps, name, rnd=0):
                run(tt(tmp, rot, bc(sin, groups), MUL))
                run(tt(dst, dst, bc(cos, groups), MUL))
                run(tt(dst, dst, tmp, ADD), steps, name, rnd)

            def retention(l):
                dve.wait_ge(RET_P.sem, RET_P.at("rotated", l))
                rotate(w(PT + 12 * T, 4, T), grid(bank(0, 2), 4), const("cos"), const("sin"), w(MATS, 4, T), 4,
                       RET_V, "qk", l)
                dve.wait_ge(RET_P.sem, RET_P.at("scores", l))
                dec = grid(const("decay"), 2)
                s = pairs(0)
                run(tt(w(MATS, 2, PAIR)[:, :, 0:2 * T], s[:, :, 0:2 * T], dec, MUL))
                dec = dec.rearrange("p r (t s) -> p r t s", t=2)[:, :, :, 0:P]
                run(tt(diagonals(MATS)[1], s[:, :, 2 * T:PAIR].rearrange("p r (t s) -> p r t s", t=2), dec, MUL),
                    RET_V, "scores", l)
                dve.wait_ge(RET_P.sem, RET_P.at("out", l))
                y, xc, sq, dev = (w(INV + 512 * i, 512) for i in range(4))
                run(dve.tensor_copy(y, bank(5)), RET_V, "y", l)
                head_norm(0, RET_P, RET_V, RET_A, y, xc, sq, dev, l)
                dve.wait_ge(RET_A.sem, RET_A.at("silu", l))
                for j in range(2):
                    ins = stt(w(BR + 1024 + j * T, T), y[:, j * T:j * T + T], par(f"gn{l}", j),
                              w(MX + j * T, T), MUL, MUL)
                    if j:
                        run(ins, RET_V, "done", l)
                    else:
                        run(ins)

            def conv(l):
                dve.wait_ge(CV_A.sem, CV_A.at("sigmoid", l))
                pad = TAPS - 1
                u = w(MATS, 2, pad + T)
                run(dve.memset(u[:, :, 0:pad], 0.0))
                run(tt(u[:, :, pad:pad + T], w(PT + 18 * T, 2, T), w(MX + 1536, 2, T), MUL))
                acc = [w(MX + 512 + j * T, T) for j in range(2)]
                for i in range(TAPS):
                    for j in range(2):
                        if i == 0:
                            ins = ts(acc[j], u[:, j, i:i + T], par(f"dw{l}", j * TAPS + i), par(f"db{l}", j), MUL, ADD)
                        else:
                            ins = stt(acc[j], u[:, j, i:i + T], par(f"dw{l}", j * TAPS + i), acc[j], MUL, ADD)
                        if i == TAPS - 1 and j == 1:
                            run(ins, CV_V, "conv", l)
                        else:
                            run(ins)
                y, xc, sq, dev = w(MX + 512, 2, T), w(INV + 512, 2, T), w(INV + 1024, 2, T), w(MX + 1024, T)
                dve.wait_ge(CV_P.sem, CV_P.at("mean", l))
                run(stt(xc, bc(bank(0)[:, 0:T], 2), -1.0 / 256, y, MUL, ADD))
                run(stt(sq, xc, 1.0 / 256, xc, MUL, MUL), CV_V, "centred", l)
                dve.wait_ge(CV_A.sem, CV_A.at("dev", l))
                run(dve.reciprocal(dev, dev))
                run(tt(xc, xc, bc(dev, 2), MUL))
                for j in range(2):
                    ins = ts(w(INV + j * T, T), xc[:, j, :], par(f"cln_w{l}", j), par(f"cln_b{l}", j), MUL, ADD)
                    if j:
                        run(ins, CV_V, "affine", l)
                    else:
                        run(ins)

            def merge(l):
                dve.wait_ge(gate_out, 16 * l + 16)
                for n in range(16):
                    dve.wait_ge(br_full, 16 * l + n + 1)
                    q = n % 4
                    b = banks[:, 4 + n % 4, :]
                    dst = scr[:, 512 * q:512 * q + 512]
                    if n < 4:
                        ins = tt(dst, w(SIG + 512 * n, 512), b, MUL)
                    else:
                        s = w(SIG + 512 * n, 512)
                        run(tt(s, s, b, MUL))
                        ins = tt(dst, dst, s, ADD)
                    chain.to(ins, br_out, 16 * l + n + 1)

            def project(r):
                for c in range(2):
                    dve.wait_ge(proj_full, 2 * r + c + 1)
                    for a in range(TT):
                        xs = x[:, a, 512 * c:512 * c + 512]
                        ins = tt(xs, xs, banks[:, 2 * c + a, :], ADD)
                        if a:
                            chain.to(ins, proj_added, 2 * r + c + 1)
                        else:
                            run(ins)

            def route():
                dve.wait_ge(RT_P.sem, RT_P.at("logits"))
                lg = small[:, 64:64 + TT * NE].rearrange("p (a e) -> p a e", a=TT)
                top = small[:, 96:96 + TT * 8].rearrange("p (a e) -> p a e", a=TT)
                idx = small[:, 128:128 + TT * 8].rearrange("p (a e) -> p a e", a=TT)
                run(dve.tensor_copy(lg, bank(0)[:, 0:TT * NE].rearrange("p (a e) -> p a e", a=TT)))
                for a in range(TT):
                    run(dve.max(top[:, a, :], lg[:, a, :]))
                    run(dve.max_index(top_index[:, a, :], top[:, a, :], lg[:, a, :]))
                run(dve.tensor_copy(idx, top_index[:, :, :]))
                run(tt(small[:, 6:8], top[:, :, 1], top[:, :, 0], SUB), RT_V, "gap")
                dve.wait_ge(RT_A.sem, RT_A.at("exp"))
                run(ts(small[:, 8:10], small[:, 4:6], 1.0, None, ADD))
                run(dve.reciprocal(small[:, 8:10], small[:, 8:10]))
                run(tt(small[:, 10:12], small[:, 8:10], small[:, 4:6], MUL))
                for a in range(TT):
                    tmp = small[:, 160:160 + NE]
                    run(ts(router_gates[:, a, :], const("experts"), idx[:, a, 0:1], small[:, 8 + a:9 + a],
                           ALU.is_equal, MUL))
                    run(ts(tmp, const("experts"), idx[:, a, 1:2], small[:, 10 + a:11 + a], ALU.is_equal, MUL))
                    ins = tt(router_gates[:, a, :], router_gates[:, a, :], tmp, ADD)
                    if a:
                        run(ins, RT_V, "gates")
                    else:
                        run(ins)

            def ffn(name, gates_):
                first = FIRST_EXPERT[name]
                with dve.Fori(0, N_PARTS[name]) as e:
                    for t in range(FT):
                        dve.wait_ge(glu_silu, (e + first) * FT + t + 1)
                        tt(w(t * T, T), glu[:, t % 2, :], banks[:, 4 + t % 4, T:2 * T], MUL).then_inc(glu_done, 1)
                    dve.wait_ge(ffn_full, e + first + 1)
                    dve.wait_ge(ffn_added, (e + first) * 4 + 1)
                    for b in range(4):
                        xs = x[:, b // 2, (b % 2) * 512:(b % 2) * 512 + 512]
                        stt(xs, banks[:, b, :], gates_[:, b // 2, bass.ds(e, 1)], xs, MUL, ADD).then_inc(ffn_added, 1)
                dve.wait_ge(ffn_added, 4 * (first + N_PARTS[name]) + 1)

            def lru():
                lam = par("a_lambda", 0, KT)
                e, s, s2, acc, cl = (small[:, 16 + 8 * i:24 + 8 * i] for i in range(5))
                dve.wait_ge(LR_A.sem, LR_A.at("lambda"))
                run(ts(s, e, 2.0, None, ADD))
                run(dve.reciprocal(s, s))
                run(tt(s, s, e, MUL))
                run(tt(s2, s, s, MUL))
                run(ts(acc, s2, 1.0 / 17, 1.0 / 15, MUL, ADD))
                for n in (13, 11, 9, 7, 5, 3, 1):
                    run(tt(acc, acc, s2, MUL))
                    run(ts(acc, acc, 1.0 / n, None, ADD))
                run(tt(acc, acc, s, MUL))
                run(ts(cl, lam, -1.0, 0.0, MUL, MAX))
                run(stt(cl, acc, 2.0, cl, MUL, ADD))
                run(ts(cl, cl, -LRU_C, None, MUL))
                z = w(2048, KT, T + 4)
                xr = w(6144, KT, T)
                run(dve.memset(z[:, :, 0:3], 0.0))
                for q in range(4):
                    dve.wait_ge(ain_out, 5 + q)
                    for i in range(TAPS2):
                        for k in range(2 * q, 2 * q + 2):
                            wk = par("a_conv_w", k * TAPS2 + i)
                            if i == 0:
                                ins = ts(xr[:, k, :], z[:, k, i:i + T], wk, par("a_conv_b", k), MUL, ADD)
                            else:
                                ins = stt(xr[:, k, :], z[:, k, i:i + T], wk, xr[:, k, :], MUL, ADD)
                            if (q, i, k) == (3, TAPS2 - 1, KT - 1):
                                run(ins, LR_V, "conv")
                            else:
                                run(ins)
                la, gi, a, th = w(8192, KT, T), w(10240, 2048), w(12288, 2048), w(14336, 2048)
                for h in range(KT):
                    dve.wait_ge(ag_out, h + 1)
                    ins = ts(la[:, h, :], la[:, h, :], cl[:, h:h + 1], None, MUL)
                    if h == KT - 1:
                        run(ins, LR_V, "log_a")
                    else:
                        run(ins)
                run(tt(gi, gi, w(6144, 2048), MUL))
                dve.wait_ge(LR_A.sem, LR_A.at("exps"))
                run(tt(w(8192, 2048), a, a, MUL))
                run(stt(th, w(8192, 2048), 1.0, th, ADD, MUL), LR_V, "square")
                dve.wait_ge(LR_A.sem, LR_A.at("root"))
                run(tt(gi, gi, th, MUL))
                for h in range(KT):
                    s_ = slice(h * T, h * T + T)
                    run(dve.tensor_tensor_scan(w(8192, 2048)[:, s_], a[:, s_], gi[:, s_], 0.0, MUL, ADD))
                run(tt(w(6144, 2048), w(8192, 2048), w(0, 2048), MUL), LR_V, "done")

            KC, EXW, HIDN, KR, KD, VSW, QR, GA, KCM, VCM = 0, 2048, 3968, 4224, 6272, 8320, 9344, 11392, 11520, 11584

            def kv():
                dve.wait_ge(kv_out, 2)
                for v in range(2):
                    src = w(KC + 1024 * v, G, T).rearrange("p g (n s) -> p s g n", s=CS)
                    for j in range(2):
                        pos = par("cmp_pos", 16 * v + 8 * j, 8).unsqueeze(2).unsqueeze(3).to_broadcast([P, 8, G, NC])
                        ins = tt(w(EXW + 960 * v + 480 * j, 8, G, NC), src[:, 0::2, :, j:j + NC], pos, ADD)
                        if v and j:
                            run(ins, KV_V, "windows")
                        else:
                            run(ins)

            def keys():
                dve.wait_ge(kv_out, 4)
                dve.wait_ge(KV_P.sem, KV_P.at("hidden1"))
                k, sq = w(KR, 1024), w(EXW + 64, 1024)
                run(tt(sq, k, k, MUL), KV_V, "k_squares")
                dve.wait_ge(KV_A.sem, KV_A.at("k_norm"))
                run(dve.reciprocal(sq, sq))
                run(tt(k, k, sq, MUL))
                run(ts(k[:, 0:512], k[:, 0:512], par("k_norm", 1), None, MUL))
                run(ts(k[:, 512:1024], k[:, 512:1024], par("k_norm", 2), None, MUL), KV_V, "k_normed")
                dve.wait_ge(KV_P.sem, KV_P.at("k_rot"))
                rotate(w(KR, 4, T), grid(bank(0, 2), 4), const("cos"), const("sin"), w(EXW + 64, 4, T), 4,
                       KV_V, "k_rope")

            def kv_cmp():
                dve.wait_ge(KV_A.sem, KV_A.at("k_cmp"))
                k, sq = w(KCM, G * NC), w(EXW, G * NC)
                run(tt(sq, k, k, MUL), KV_V, "cmp_squares")
                dve.wait_ge(KV_A.sem, KV_A.at("cmp_norm"))
                run(dve.reciprocal(sq, sq))
                run(tt(k, k, sq, MUL))
                run(ts(k, k, par("k_norm", 0), None, MUL), KV_V, "cmp_normed")
                dve.wait_ge(KV_P.sem, KV_P.at("cmp_rot"))
                rotate(w(KCM, G, NC), grid(bank(2)[:, 0:G * NC], G), const("cos_cmp"), const("sin_cmp"),
                       w(EXW, G, NC), G, KV_V, "cmp_rope")
                dve.wait_ge(KV_P.sem, KV_P.at("v_cmp"))
                r = slice(0, NC)
                run(dve.tensor_copy(w(VCM, G * HD, rows=r), bank(3, rows=r)[:, 0:G * HD]), KV_V, "v_cmp")

            def queries():
                dve.wait_ge(Q_A.sem, Q_A.at("out3"))
                q, sq = w(QR, 2048), w(16896, 2048)
                run(tt(sq, q, q, MUL), Q_V, "squares")
                dve.wait_ge(Q_A.sem, Q_A.at("norm"))
                run(dve.reciprocal(sq, sq))
                run(tt(q, q, sq, MUL))
                run(ts(q, q, par("q_norm"), None, MUL), Q_V, "normed")
                dve.wait_ge(Q_P.sem, Q_P.at("rot"))
                rotate(w(QR, KT, T), grid(bank(0, 4), KT), const("cos"), const("sin"), w(16896, KT, T), KT,
                       Q_V, "rope")

            def attend(u):
                g, a = u // TT, u % TT
                n = P * (a + 1)
                at, _ = CONSTS["causal_add"]
                mask = consts[:, at + (1 - a) * P:at + 2 * P]
                dve.wait_ge(AT_P.sem, AT_P.at("scores", u))
                for b in range(2):
                    s = w(16896 + 1024 * b, 4, n)
                    for r in range(2):
                        run(stt(s[:, 2 * r:2 * r + 2, :], grid(bank(2 * b + r)[:, 0:2 * n], 2), HD ** -0.5, bc(mask, 2),
                                MUL, ADD))
                    run(dve.tensor_reduce(small[:, 32 + 4 * b:36 + 4 * b], s, AX, MAX, negate=True))
                s = w(18944, 4, NC)
                at, _ = CONSTS["cmp_add"]
                for r in range(2):
                    run(stt(s[:, 2 * r:2 * r + 2, :], grid(bank(4 + r)[:, 0:2 * NC], 2), HD ** -0.5,
                            bc(consts[:, at + a * NC:at + a * NC + NC], 2), MUL, ADD))
                run(dve.tensor_reduce(small[:, 40:44], s, AX, MAX, negate=True), AT_V, "masked", u)
                dve.wait_ge(AT_A.sem, AT_A.at("exps", u))
                run(dve.reciprocal(small[:, 48:60], small[:, 48:60]))
                ga = w(GA + 48 * a, 3, 16)[:, :, 4 * g:4 * g + 4].rearrange("p c (t r) -> p c r t", t=2)
                for b, c in ((0, 1), (1, 2), (2, 0)):
                    wt = grid(small[:, 48 + 4 * b:52 + 4 * b], 2)
                    run(tt(wt, wt, ga[:, c, :, :], MUL))
                at, _ = CONSTS["cmp_keep"]
                run(tt(s, s, bc(consts[:, at + a * NC:at + a * NC + NC], 4), MUL))
                run(tt(s, s, small[:, 56:60].unsqueeze(2).to_broadcast([P, 4, NC]), MUL))
                for b in range(2):
                    s = w(16896 + 1024 * b, 4, n)
                    ins = tt(s, s, small[:, 48 + 4 * b:52 + 4 * b].unsqueeze(2).to_broadcast([P, 4, n]), MUL)
                    if b:
                        run(ins, AT_V, "probs", u)
                    else:
                        run(ins)

            for l in range(2):
                norm(2 * l, f"norm_mix{l}")
                rwkv_front(l)
                for n in range(LEVELS):
                    rwkv_level(l, n)
                rwkv_back(l)
                stick(l)
                retention(l)
                conv(l)
                merge(l)
                project(l)
                norm(2 * l + 1, f"norm_ffn{l}")
                if l == 0:
                    ffn("dense", ones_gates)
                else:
                    route()
                    ffn("moe", router_gates)
            norm(4, "a_norm")
            lru()
            project(2)
            norm(5, "f_norm0")
            ffn("f0", ones_gates)
            norm(6, "kv_norm")
            kv()
            kv_cmp()
            keys()
            norm(7, "b_norm")
            queries()
            for u in range(2 * G):
                attend(u)
            project(3)
            norm(8, "f_norm1")
            ffn("f1", ones_gates)


def kernel(**inputs):
    import concourse.bacc as bacc
    from concourse.bass_utils import run_bass_kernel_spmd

    a = {name: np.asarray(v) for name, v in inputs.items()}
    arrays = {"weights_in": weight_stream(a), "consts_in": constant_arrays(), "params_in": parameter_array(a),
              "x_in": np.ascontiguousarray(a["x"])}
    nc = bacc.Bacc("TRN2", target_bir_lowering=False, num_devices=1)
    aps = [nc.dram_tensor(name, v.shape, F32, kind="ExternalInput").ap() for name, v in arrays.items()]
    out = nc.dram_tensor("out", (1, T, D), F32, kind="ExternalOutput").ap()
    build(nc, *aps, out)
    return run_bass_kernel_spmd(nc, [arrays], core_ids=[0]).results[0]["out"]
```

```python
from contextlib import ExitStack

import numpy as np

import concourse.bass as bass
from concourse import mybir

F32 = mybir.dt.float32
F32R = mybir.dt.float32r
I32 = mybir.dt.int32
U32 = mybir.dt.uint32
ALU = mybir.AluOpType
ACT = mybir.ActivationFunctionType
AX = mybir.AxisListType.X

P = 128
T = 256
TT = T // P
D = 1024
KT = D // P
HD = 64
NH = 4
NHQ = 16
G = 4
LORA = 64
DECAY_SCALE = 0.606531
SHIFT = DECAY_SCALE * P / 2
EPS = 1e-6
RW_EPS = 64e-5
LN_EPS = 1e-5
TAPS = 31
TAPS2 = 4
NE = 8
FE = 1408
FT = FE // P
CAP = 96
LRU_C = 8.0
CB, CS = 32, 16
NC = (T - CB) // CS + 1
HID = 256
NEG = -1e30
LEVELS = 7

SLAB = 4096
RING = 3
IN_SLABS, OUT_SLABS = 6, 3
EXPERT_SLABS = IN_SLABS + OUT_SLABS
HALF_SLAB = SLAB // 2
OUT_UNIT = 2 * IN_SLABS
OUT_UNITS = 2 * OUT_SLABS
UNITS = [*range(FT), *range(OUT_UNIT, OUT_UNIT + OUT_UNITS)]
SPLIT_BUFS = 3
assert 2 * EXPERT_SLABS % SPLIT_BUFS == 0


def columns(widths):
    place, at = {}, 0
    for name, n in widths:
        place[name] = (at, n)
        at += n
    return place, at


CONSTS, N_CONSTS = columns([
    ("ident", P), ("head_sum", P), ("head_mean", P), ("ones", P), ("strict", P), ("causal", P),
    ("suffix", P), ("levels", LEVELS * P), ("swap", P), ("cos", T), ("sin", T), ("cos_cmp", NC),
    ("sin_cmp", NC), ("decay", NH * T), ("not_before", P), ("causal_add", T + P), ("cmp_add", TT * NC),
    ("cmp_keep", TT * NC), ("experts", NE), ("slots", CAP), ("rms_eps", 1), ("rw_eps", 1), ("ln_eps", 1),
    ("shift", 1), ("minus_shift", 1), ("one", 1)])

LAYER_COLS = [
    ("norm_mix", KT), ("norm_ffn", KT), ("mu", KT), ("w0", 2), ("a0", 2), ("k_k", 2), ("k_a", 2),
    ("r_k", 2), ("ln_w", 2), ("ln_b", 2), ("sb_q", 1), ("sb_k", 1), ("gn", 2), ("dw", 2 * TAPS),
    ("db", 2), ("cln_w", 2), ("cln_b", 2), ("w2a2", 2 * P), ("g2", 2 * P)]
PARAMS, N_PARAMS = columns(
    [(f"{name}{l}", n) for l in range(2) for name, n in LAYER_COLS] + [
        ("router", KT * NE), ("a_norm", KT), ("a_conv_w", KT * TAPS2), ("a_conv_b", KT),
        ("a_gate_b", 2 * KT), ("a_lambda", KT), ("kv_norm", KT), ("k_norm", 3), ("cmp_pos", 2 * CB // 2),
        ("cmp_b1", 4), ("cmp_b2k", 1), ("cmp_b2v", HD), ("cmp_w2k", 2 * P), ("cmp_w2v", 2 * HD),
        ("b_norm", KT), ("gate_w", KT * 48), ("gate_b", 48), ("q_norm", 1), ("f_norm0", KT), ("f_norm1", KT)])


def constant_arrays():
    c = np.zeros((P, N_CONSTS), np.float32)

    def put(name, a):
        at, n = CONSTS[name]
        c[:, at:at + n] = np.asarray(a, np.float32).reshape(P, n)

    i = np.arange(P)
    row, col = i[:, None], i[None, :]
    same_head = (row // HD == col // HD).astype(np.float32)
    put("ident", np.eye(P))
    put("head_sum", same_head)
    put("head_mean", same_head / HD)
    put("ones", np.ones((P, P)))
    put("strict", row < col)
    put("causal", row <= col)
    put("suffix", row >= col)
    levels = []
    for n in range(LEVELS):
        b = 1 << n
        levels.append((row < col) & (row // (2 * b) == col // (2 * b)) & (row // b != col // b))
    put("levels", np.stack(levels, 1))
    swap = np.zeros((P, P), np.float32)
    for m in range(P):
        d = m % HD
        if d < HD // 2:
            swap[m + HD // 2, m] = -1.0
        else:
            swap[m - HD // 2, m] = 1.0
    put("swap", swap)
    freq = np.float32(10000.0) ** (-np.arange(0, HD, 2, dtype=np.float32) / np.float32(HD))
    freq = freq[i % (HD // 2)].astype(np.float32)[:, None]
    pos = np.arange(T, dtype=np.float32)[None, :]
    cmp_last = np.arange(NC) * CS + CB - 1
    put("cos", np.cos(pos * freq))
    put("sin", np.sin(pos * freq))
    put("cos_cmp", np.cos(cmp_last.astype(np.float32)[None, :] * freq))
    put("sin_cmp", np.sin(cmp_last.astype(np.float32)[None, :] * freq))
    gamma = np.log(1.0 - 2.0 ** (-5.0 - np.arange(NH)))
    rel = np.arange(T)[None, None, :] - i[:, None, None]
    decay = np.where(rel >= 0, np.exp(np.maximum(rel, 0) * gamma[None, :, None]) * HD ** -0.5, 0.0)
    put("decay", decay[:, [0, 2, 1, 3]])
    put("not_before", np.where(row < col, 0.0, NEG))
    put("causal_add", np.concatenate([np.zeros((P, P)), np.where(col <= row, 0.0, NEG), np.zeros((P, P))], 1))
    t = i[:, None, None] + P * np.arange(TT)[None, :, None]
    seen = cmp_last[None, None, :] <= t
    put("cmp_add", np.where(seen, 0.0, NEG))
    put("cmp_keep", seen)
    put("experts", np.broadcast_to(np.arange(NE), (P, NE)))
    put("slots", np.broadcast_to(np.arange(CAP), (P, CAP)))
    for name, value in (("rms_eps", EPS), ("rw_eps", RW_EPS), ("ln_eps", LN_EPS), ("shift", SHIFT),
                        ("minus_shift", -SHIFT), ("one", 1.0)):
        put(name, np.full((P, 1), value))
    return c


def parameter_array(a):
    c = np.zeros((P, N_PARAMS), np.float32)

    def put(name, v, rows=slice(0, P)):
        at, n = PARAMS[name]
        c[rows, at:at + n] = v

    def column(v):
        return v.reshape(-1, P).T

    for l in range(2):
        for name, key in (("norm_mix", "norm_mix"), ("norm_ffn", "norm_ffn"), ("mu", "rw_mu"), ("w0", "rw_w0"),
                          ("a0", "rw_a0"), ("k_k", "rw_k_k"), ("k_a", "rw_k_a"), ("ln_w", "rw_ln_w"),
                          ("ln_b", "rw_ln_b"), ("gn", "ret_gn"), ("db", "conv_b"), ("cln_w", "conv_ln_w"),
                          ("cln_b", "conv_ln_b")):
            put(f"{name}{l}", column(a[key][l]))
        put(f"r_k{l}", column(a["rw_r_k"][l].reshape(-1)))
        put(f"sb_q{l}", np.concatenate([a["sb_q_norm"][l]] * 2)[:, None])
        put(f"sb_k{l}", np.concatenate([a["sb_k_norm"][l]] * 2)[:, None])
        put(f"dw{l}", a["conv_dw"][l].reshape(TAPS, 2, P).transpose(2, 1, 0).reshape(P, -1))
        put(f"w2a2{l}", np.concatenate([a["rw_w2"][l], a["rw_a2"][l]], 0))
        put(f"g2{l}", a["rw_g2"][l])
    put("router", a["router"][0].reshape(KT, P, NE).transpose(1, 0, 2).reshape(P, -1))
    put("a_norm", column(a["a_norm_2"][0]))
    put("a_conv_w", a["a_conv_w_2"][0].reshape(TAPS2, KT, P).transpose(2, 1, 0).reshape(P, -1))
    put("a_conv_b", column(a["a_conv_b_2"][0]))
    put("a_gate_b", column(a["a_gate_b_2"][0].reshape(-1)))
    put("a_lambda", column(a["a_lambda_2"][0]))
    put("kv_norm", column(a["kv_norm_2"]))
    put("k_norm", np.concatenate([a["k_norm_2"]] * 2, 1).T)
    put("cmp_pos", a["cmp_pos_2"].reshape(2, CB // 2, 2 * HD).transpose(2, 0, 1).reshape(P, -1))
    put("cmp_b1", column(a["cmp_b1_2"].reshape(-1)))
    put("cmp_b2k", np.concatenate([a["cmp_b2_2"][0]] * 2)[:, None])
    put("cmp_b2v", a["cmp_b2_2"][1][None, :], slice(0, 1))
    w2 = a["cmp_w2_2"].reshape(2, 2, P, HD)
    put("cmp_w2k", np.concatenate([w2[0]] * 2, 2).transpose(1, 0, 2).reshape(P, -1))
    put("cmp_w2v", w2[1].transpose(1, 0, 2).reshape(P, -1))
    put("b_norm", column(a["b_norm_2"][0]))
    put("gate_w", a["b_w_in_2"][0][:, D:].reshape(KT, P, 48).transpose(1, 0, 2).reshape(P, -1))
    put("gate_b", a["b_gate_b_2"][0][None, :], slice(0, 1))
    put("q_norm", np.concatenate([a["q_norm_2"][0]] * 2)[:, None])
    put("f_norm0", column(a["f_norm_2"][0]))
    put("f_norm1", column(a["f_norm_2"][1]))
    return c


def weight_stream(a):
    slabs = []

    def add(w):
        w = w.reshape(P, -1)
        slab = np.zeros((P, SLAB), np.float32)
        slab[:, :w.shape[1]] = w
        slabs.append(slab)

    def rows(w):
        return w.reshape(-1, P, w.shape[-1]).transpose(1, 0, 2)

    def wide(w):
        for n in range(0, w.shape[1], 512):
            cut = w[:, n:n + 512]
            if cut.shape[1] < 512:
                cut = np.concatenate([cut, np.zeros((cut.shape[0], 512 - cut.shape[1]), np.float32)], 1)
            add(rows(cut))

    def expert(w1, w3, w2):
        for f in range(0, FE, 2 * P):
            pad = np.zeros((D, max(0, f + 2 * P - FE)), np.float32)
            cut = rows(np.concatenate([w1[:, f:f + 2 * P], pad, w3[:, f:f + 2 * P], pad], 1))
            add(cut.reshape(P, KT, 2, 2, P).transpose(0, 3, 1, 2, 4))
        for f in range(0, FE, 4 * P):
            add(rows(w2[f:f + 4 * P]))

    for l in range(2):
        w = a["w_in"][l]
        rw, sb, ret = 1024, 1792, 2816
        order = [w[:, 0:rw], w[:, rw:rw + 512], w[:, sb:sb + 512],
                 w[:, rw + 512:sb], w[:, sb + 512:sb + 768], w[:, sb + 768:ret], w[:, ret:]]
        wide(np.concatenate(order, 1))
        for i in range(4):
            wide(a["w_gate"][l, i])
        for i in range(0, 4, 2):
            add(rows(a["w_branch"][l, i:i + 2].reshape(512, D)))
        wide(a["w_out"][l])
        if l == 0:
            for h in range(2):
                s = slice(h * FE, h * FE + FE)
                expert(a["ffn_w1"][0][:, s], a["ffn_w3"][0][:, s], a["ffn_w2"][0][s])
        else:
            for e in range(NE):
                expert(a["moe_w1"][0, e], a["moe_w3"][0, e], a["moe_w2"][0, e])

    def ffn(l):
        for h in range(2):
            s = slice(h * FE, h * FE + FE)
            w = a["f_w_in_2"][l]
            expert(w[:, :2 * FE][:, s], w[:, 2 * FE:][:, s], a["f_w_out_2"][l][s])

    wide(a["a_w_in_2"][0])
    add(a["a_gate_w_2"][0].transpose(2, 0, 1, 3))
    wide(a["a_w_out_2"][0])
    ffn(0)
    kv = a["kv_w_2"]
    wide(np.concatenate([kv[:, 0:768], kv[:, 1024:1280], kv[:, 768:1024], kv[:, 1280:1536]], 1))
    for v in range(2):
        add(rows(a["cmp_w1_2"][v]))
    wide(a["b_w_in_2"][0][:, :D])
    wide(a["b_w_out_2"][0])
    ffn(1)
    return np.stack(slabs)


class Steps:

    def __init__(self, sem, *names):
        self.sem, self.names, self.count = sem, names, 0

    def at(self, name, rnd=0):
        return rnd * len(self.names) + self.names.index(name) + 1

    def mark(self, ins, name, rnd=0):
        self.count += 1
        assert self.count == self.at(name, rnd), (name, rnd, self.count)
        ins.then_inc(self.sem, 1)
        return self.count


class Chain:

    def __init__(self, eng, sem):
        self.eng, self.sem, self.count = eng, sem, 0

    def to(self, ins, sem, value):
        ins.then_inc(sem, 1)
        self.eng.wait_ge(sem, value)

    def run(self, ins, steps=None, name=None, rnd=0):
        if steps is None:
            self.count += 1
            ins.then_inc(self.sem, 1)
            self.eng.wait_ge(self.sem, self.count)
        else:
            self.eng.wait_ge(steps.sem, steps.mark(ins, name, rnd))


def build(nc, stream, consts_in, params_in, x_in, out):
    n_slabs = stream.shape[0]
    assert n_slabs % RING == 0
    with ExitStack() as ctx:
        def sb(name, shape, dt=F32):
            return ctx.enter_context(nc.sbuf_tensor(name, shape, dt))

        def sem(name):
            return ctx.enter_context(nc.semaphore(name))

        x = sb("x", [P, TT, D])
        hT = sb("hT", [P, KT, T])
        scr = sb("scr", [P, 2048])
        ring = sb("ring", [P, RING, SLAB])
        consts = sb("consts", [P, N_CONSTS])
        params = sb("params", [P, N_PARAMS])
        small = sb("small", [P, 256])
        router_gates = sb("router_gates", [P, TT, NE])
        crowded = sb("crowded", [P, 1], I32)
        top_index = sb("top_index", [P, TT, 8], U32)
        glu = sb("glu", [P, 2, T])
        with ExitStack() as shared:
            def split_operand(name, shape, dt=F32R):
                return shared.enter_context(nc.sbuf_tensor(name, shape, dt))

            w_hi = split_operand("w_hi", [P, SPLIT_BUFS, HALF_SLAB])
            w_lo = split_operand("w_lo", [P, SPLIT_BUFS, HALF_SLAB])
            h_hi, h_lo = split_operand("h_hi", [P, KT, T]), split_operand("h_lo", [P, KT, T])
            g_hi, g_lo = split_operand("g_hi", [P, FT, T]), split_operand("g_lo", [P, FT, T])
            hidden = split_operand("hidden", [P, FT, T], F32)
        work = sb("work", [P, 27136])
        banks = ctx.enter_context(nc.psum_tensor("banks", [P, 8, 512], F32))

        def const(name, *index):
            at, n = CONSTS[name]
            return consts[:, at:at + n]

        def par(name, i=0, n=1, rows=slice(0, P)):
            at, _ = PARAMS[name]
            return params[rows, at + i:at + i + n]

        def w(at, *dims, rows=slice(0, P)):
            n = 1
            for d in dims:
                n *= d
            ap = work[rows, at:at + n]
            return ap if len(dims) == 1 else ap.rearrange(
                "p (a b) -> p a b" if len(dims) == 2 else "p (a b c) -> p a b c", **dict(zip("abc", dims)))

        def bank(b, n=1, rows=slice(0, P)):
            return banks[rows, b:b + n, :].rearrange("p a b -> p (a b)")

        def grid(ap, a):
            return ap.rearrange("p (a b) -> p a b", a=a)

        PAIR = 2 * T + 2 * P

        def pairs(b):
            return grid(bank(b, 4), 2)[:, :, 0:PAIR]

        def diagonals(at):
            s = w(at, 2, PAIR)
            return (s[:, :, 0:2 * T].rearrange("p r (t s) -> p r t s", t=2)[:, :, :, 0:P],
                    s[:, :, 2 * T:PAIR].rearrange("p r (t s) -> p r t s", t=2))

        def matrix(h, c):
            return (h % 2) * 4 + 2 * c + h // 2

        def half(r):
            return slice(HD * r, HD * r + HD)

        PT, VT, BR, SIG, MATS, INV, MX = 0, 5632, 6656, 8704, 16896, 20992, 25088
        LEVEL_AT = (INV + 3072, MX + 1024)
        pT = w(PT, 22, T)
        vt = w(VT, TT, 512)
        br = w(BR, KT, T)
        sig = w(SIG, 4 * KT, T)

        sel = w(3072, TT, CAP)
        sel_gate = w(3264, TT, CAP)
        sel_turned = w(3456, TT * P, rows=slice(0, CAP))
        gathered = w(3712, KT, CAP)
        result = w(4480, D, rows=slice(0, CAP))
        chosen, slot, gate_of = (w(5504 + 32 * i, TT, 16) for i in range(3))

        loaded = sem("loaded")
        landed = [sem(f"landed{i}") for i in range(RING)]
        slab_used = sem("slab_used")
        stored = sem("stored")
        v_chain, a_chain = sem("v_chain"), sem("a_chain")
        NORM_V = Steps(sem("norm_vector"), "rows", "hT")
        NORM_A = Steps(sem("norm_scalar"), "root")
        NORM_P = Steps(sem("norm_transposed"), "done")
        win_full, win_out = sem("win_full"), sem("win_out")
        gate_full, gate_out = sem("gate_full"), sem("gate_out")
        br_full, br_out = sem("branch_full"), sem("branch_merged")
        RW_P = Steps(sem("rw_products"), "lora", "squares", "bonus", "mats0", "mats1",
                     *[f"{s}{n}" for n in range(LEVELS) for s in ("T", "X")],
                     "w0", "u0", "state", "w1", "u1", "y", "mean", "var")
        RW_V = Steps(sem("rw_vector"), "mixed", "k_squared", "decays", "operands", "bonus_used", "mats0", "mats1",
                     *[f"X{n}" for n in range(LEVELS)], "state", "y", "centred", "done")
        RW_A = Steps(sem("rw_scalar"), "lora", "sigmoids", "norm", "exps", "rows", *[f"T{n}" for n in range(LEVELS)],
                     "w0", "u0", "w1", "u1", "dev")
        RW_G = Steps(sem("rw_masks"), "zeroed", *[f"M{n}" for n in range(LEVELS)])
        SB_P = Steps(sem("sb_products"), "squares", "scores", "suffix", "out")
        SB_V = Steps(sem("sb_vector"), "squares", "qk", "softplus", "logs", "done")
        SB_A = Steps(sem("sb_scalar"), "norm", "scores", "ln", "weights")
        RET_P = Steps(sem("ret_products"), "rotated", "scores", "out", "mean", "var")
        RET_V = Steps(sem("ret_vector"), "qk", "scores", "y", "centred", "done")
        RET_A = Steps(sem("ret_scalar"), "silu", "dev")
        CV_P = Steps(sem("conv_products"), "mean", "var")
        CV_V = Steps(sem("conv_vector"), "conv", "centred", "affine")
        CV_A = Steps(sem("conv_scalar"), "sigmoid", "dev", "done")
        proj_full, proj_added = sem("proj_full"), sem("proj_added")
        glu_full, glu_silu, glu_done = sem("glu_full"), sem("glu_silu"), sem("glu_done")
        ffn_added = sem("ffn_added")
        input_half, input_hi, input_lo = sem("input_half"), sem("input_hi"), sem("input_lo")
        unit_hi, unit_lo = sem("unit_hi"), sem("unit_lo")
        hidden_hi, hidden_lo = sem("hidden_hi"), sem("hidden_lo")
        out_used = sem("out_used")
        RT_P = Steps(sem("router_products"), "logits", "slots")
        RT_V = Steps(sem("router_vector"), "gap", "chosen", "flag")
        sp_selected, sp_inputs, sp_gathered = sem("sp_selected"), sem("sp_inputs"), sem("sp_gathered")
        sp_result, sp_scattered, sp_added = sem("sp_result"), sem("sp_scattered"), sem("sp_added")
        sp_copied, sp_turned = sem("sp_copied"), sem("sp_turned")
        RT_A = Steps(sem("router_scalar"), "exp")
        ain_full, ain_out = sem("ain_full"), sem("ain_out")
        ag_full, ag_out = sem("lru_gate_full"), sem("lru_gate_out")
        LR_V = Steps(sem("lru_vector"), "conv", "log_a", "square", "done")
        LR_A = Steps(sem("lru_scalar"), "lambda", "exps", "root")
        kv_full, kv_out = sem("kv_full"), sem("kv_out")
        KV_V = Steps(sem("kv_vector"), "windows", "cmp_squares", "cmp_normed", "cmp_rope", "v_cmp", "k_squares",
                     "k_normed", "k_rope")
        KV_P = Steps(sem("kv_products"), "hidden0", "hidden1", "k_cmp", "cmp_mean", "cmp_rot", "v_cmp", "k_mean", "k_rot")
        KV_A = Steps(sem("kv_scalar"), "hidden0", "hidden1", "k_cmp", "cmp_norm", "k_norm", "k_copies")
        Q_P = Steps(sem("q_products"), "full0", "full1", "full2", "full3", "gates", "mean", "rot")
        Q_A = Steps(sem("q_scalar"), "out0", "out1", "out2", "out3", "gates", "norm")
        Q_V = Steps(sem("q_vector"), "squares", "normed", "rope")
        AT_P = Steps(sem("at_products"), "scores", "turned", "out")
        AT_V = Steps(sem("at_vector"), "masked", "probs")
        AT_A = Steps(sem("at_scalar"), "exps", "turned", "out")

        FIRST_EXPERT = {"dense": 0, "moe": 2, "f0": 2 + NE, "f1": 4 + NE}
        MIX, REC, ATT = 7 + 8 + 2 + 2, 4 + 1 + 2, 3 + 2 + 2 + 2
        LAST_MOE_SLAB = 2 * MIX + 3 * EXPERT_SLABS
        FIRST_SLAB = {"dense": MIX, "f0": 2 * MIX + 10 * EXPERT_SLABS + REC,
                      "f1": 2 * MIX + 12 * EXPERT_SLABS + REC + ATT}
        SPLIT = {"dense": 0, "f0": 1, "f1": 2}
        SPLIT_NORMS = {1: "dense", 5: "f0", 8: "f1"}
        N_PARTS = {"dense": 2, "moe": NE, "f0": 2, "f1": 2}

        def unit_count(part, u):
            return part * len(UNITS) + UNITS.index(u) + 1

        def wait_unit_free(eng, name, h, u):
            before, part = u - SPLIT_BUFS, 2 * SPLIT[name] + h
            if before >= OUT_UNIT:
                eng.wait_ge(out_used, part * OUT_UNITS + before - OUT_UNIT + 1)
            elif before >= 0:
                eng.wait_ge(glu_full, (FIRST_EXPERT[name] + h) * FT + min(before, FT - 1) + 1)
            elif part:
                eng.wait_ge(out_used, part * OUT_UNITS + before + 1)

        def unit_of_ring(u, first):
            return ring[:, (first + u // 2) % RING, (u % 2) * HALF_SLAB:(u % 2) * HALF_SLAB + HALF_SLAB]

        block = ctx.enter_context(nc.Block())

        @block.sync
        def _(sp):
            sp.dma_start(x[:, :, :], x_in.rearrange("o (a p) d -> p (o a) d", p=P)).then_inc(loaded, 16)
            sp.dma_start(consts[:, :], consts_in).then_inc(loaded, 16)
            sp.dma_start(params[:, :], params_in).then_inc(loaded, 16)
            for n in range(RING):
                sp.dma_start(ring[:, n, :], stream[n]).then_inc(landed[n], 16)
            with sp.Fori(1, n_slabs // RING) as i:
                for n in range(RING):
                    sp.wait_ge(slab_used, i * RING + (n + 1 - RING))
                    sp.dma_start(ring[:, n, :], stream[i * RING + n]).then_inc(landed[n], 16)
            sp.wait_ge(ffn_added, 4 * (FIRST_EXPERT["f1"] + 2) + 1)
            sp.dma_start(out.rearrange("o (a p) d -> p (o a) d", p=P), x[:, :, :]).then_inc(stored, 16)
            sp.wait_ge(stored, 16)

        @block.gpsimd
        def _(pool):
            def ffn_split(name):
                for h in range(2):
                    for t in range(FT):
                        pool.wait_ge(glu_done, (h + FIRST_EXPERT[name]) * FT + t + 2)
                        n = (h + 2 * SPLIT[name]) * FT + t + 1
                        pool.tensor_copy(g_hi[:, t, :], hidden[:, t, :]).then_inc(hidden_hi, 1)
                        pool.wait_ge(hidden_hi, n)
                        pool.tensor_tensor(g_lo[:, t, :], hidden[:, t, :], g_hi[:, t, :].bitcast(F32),
                                           ALU.subtract).then_inc(hidden_lo, 1)

            for l in range(2):
                if l:
                    pool.wait_ge(NORM_V.sem, NORM_V.at("rows", 2 * l))
                RW_G.mark(pool.memset(w(MATS, 4096), 0.0), "zeroed", l)
                pool.wait_ge(RW_V.sem, RW_V.at("mats1", l))
                for n in range(LEVELS):
                    if n >= 2:
                        pool.wait_ge(RW_P.sem, RW_P.at(f"T{n - 2}", l))
                    at, _ = CONSTS["levels"]
                    mask = consts[:, at + n * P:at + n * P + P].unsqueeze(1).to_broadcast([P, 8, P])
                    RW_G.mark(pool.tensor_tensor(w(LEVEL_AT[n % 2], 8, P), w(MATS, 8, P), mask, ALU.mult),
                              f"M{n}", l)
                if l == 0:
                    ffn_split("dense")
            ffn_split("f0")
            ffn_split("f1")

        @block.scalar
        def _(act):
            chain = Chain(act, a_chain)
            run = chain.run

            def f(out_, in_, func, **kw):
                return act.activation(out_, in_, func, **kw)

            def norm(n):
                if n == 0:
                    act.wait_ge(loaded, 48)
                elif n in (1, 3):
                    act.wait_ge(proj_added, 2 * (n // 2 + 1))
                elif n == 2:
                    act.wait_ge(ffn_added, 4 * FIRST_EXPERT["moe"] + 1)
                elif n == 4:
                    act.wait_ge(ffn_added, 4 * FIRST_EXPERT["f0"] + 1)
                elif n == 5:
                    act.wait_ge(proj_added, 6)
                elif n == 6:
                    act.wait_ge(ffn_added, 4 * FIRST_EXPERT["f1"] + 1)
                elif n == 7:
                    act.wait_ge(NORM_P.sem, NORM_P.at("done", 6))
                elif n == 8:
                    act.wait_ge(proj_added, 8)
                for a in range(TT):
                    run(f(scr[:, a * D:a * D + D], x[:, a, :], ACT.Square, accum_out=small[:, a:a + 1]))
                run(f(small[:, 2:4], small[:, 0:2], ACT.Sqrt, scale=1.0 / D, bias=const("rms_eps")), NORM_A, "root", n)

            def win(l):
                for q in range(13):
                    act.wait_ge(win_full, 13 * l + q + 1)
                    src = banks[:, 4 + q % 4, :]
                    if q < 8:
                        dst = w(PT + 512 * q, 512)
                    elif q < 10:
                        dst = vt[:, q - 8, :]
                    else:
                        dst = w(PT + 512 * (q - 2), 512)
                    chain.to(f(dst, src, ACT.Copy), win_out, 13 * l + q + 1)

            def gates(l, slabs):
                for s in slabs:
                    for q in range(2):
                        n = 2 * s + q
                        act.wait_ge(gate_full, 16 * l + n + 1)
                        f(w(SIG + 512 * n, 512), banks[:, 6 + q, :], ACT.Sigmoid).then_inc(gate_out, 1)

            def rwkv_front(l):
                act.wait_ge(RW_V.sem, RW_V.at("mixed", l))
                run(f(w(INV + 3584, T, rows=half(0)), w(MX + 6 * T, T, rows=half(0)), ACT.Tanh))
                run(f(w(INV + 3840, T), w(MX + 7 * T, T), ACT.Sigmoid), RW_A, "lora", l)
                act.wait_ge(RW_P.sem, RW_P.at("lora", l))
                for j in range(2):
                    run(f(w(INV + 1536 + j * T, T), bank(0)[:, j * T:j * T + T], ACT.Sigmoid, bias=par(f"w0{l}", j)))
                    run(f(w(MX + (6 + j) * T, T), bank(1)[:, j * T:j * T + T], ACT.Sigmoid, bias=par(f"a0{l}", j)))
                run(f(scr[:, 0:512], bank(2), ACT.Copy), RW_A, "sigmoids", l)
                act.wait_ge(RW_P.sem, RW_P.at("squares", l))
                run(f(w(INV + 1024, 512), bank(3), ACT.Sqrt), RW_A, "norm", l)
                act.wait_ge(RW_V.sem, RW_V.at("decays", l))
                run(f(w(PT, 512), w(INV + 2560, 512), ACT.Exp, bias=const("shift")))
                run(f(w(INV + 3072, 512), w(INV + 2048, 512), ACT.Exp, scale=-1.0, bias=const("minus_shift")))
                run(f(w(PT + 1536, 512), w(INV + 2048, 512), ACT.Exp, bias=const("shift")))
                run(f(small[:, 8:10], w(INV + 2048, 2, T)[:, :, P - 1], ACT.Exp), RW_A, "exps", l)
                act.wait_ge(RW_P.sem, RW_P.at("bonus", l))
                run(f(scr[:, 1024:2048], bank(4, 2), ACT.Copy), RW_A, "rows", l)

            def rwkv_level(l, n):
                act.wait_ge(RW_P.sem, RW_P.at(f"T{n}", l))
                run(f(w(INV + 2048, 1024), bank(0, 2), ACT.Copy), RW_A, f"T{n}", l)

            def rwkv_back(l):
                for name, at in (("w0", 0), ("u0", 256), ("w1", 0), ("u1", 512)):
                    act.wait_ge(RW_P.sem, RW_P.at(name, l))
                    if at:
                        run(f(w(MX + at, 256), bank(2)[:, 0:256], ACT.Copy), RW_A, name, l)
                    else:
                        run(f(w(MX, 2, P), grid(bank(0, 2), 2)[:, :, 0:P], ACT.Copy), RW_A, name, l)
                act.wait_ge(RW_P.sem, RW_P.at("var", l))
                run(f(w(INV + 1536, 512), bank(5), ACT.Sqrt, bias=const("rw_eps")), RW_A, "dev", l)

            def stick(l):
                act.wait_ge(SB_P.sem, SB_P.at("squares", l))
                run(f(w(MATS, 1024), bank(0, 2), ACT.Sqrt, bias=const("rms_eps")), SB_A, "norm", l)
                act.wait_ge(SB_P.sem, SB_P.at("scores", l))
                run(f(w(MATS + 2048, 2, PAIR), pairs(0), ACT.Copy), SB_A, "scores", l)
                run(f(w(INV, 1536), w(MATS + 2048, 1536), ACT.Abs))
                run(f(w(INV, 1536), w(INV, 1536), ACT.Exp, scale=-1.0))
                run(f(w(INV, 1536), w(INV, 1536), ACT.Ln, bias=const("one")), SB_A, "ln", l)
                act.wait_ge(SB_V.sem, SB_V.at("logs", l))
                run(f(w(INV, 1536), w(INV, 1536), ACT.Exp), SB_A, "weights", l)

            def retention(l):
                run(f(w(MX, 512), w(PT + 16 * T, 512), ACT.Silu), RET_A, "silu", l)
                act.wait_ge(RET_P.sem, RET_P.at("var", l))
                run(f(w(INV + 1536, 512), bank(1), ACT.Sqrt, bias=const("ln_eps")), RET_A, "dev", l)

            def conv_front(l):
                run(f(w(MX + 1536, 512), w(PT + 20 * T, 512), ACT.Sigmoid), CV_A, "sigmoid", l)

            def conv_back(l):
                act.wait_ge(CV_P.sem, CV_P.at("var", l))
                run(f(w(MX + 1024, T), bank(1)[:, 0:T], ACT.Sqrt, bias=const("ln_eps")), CV_A, "dev", l)
                act.wait_ge(CV_V.sem, CV_V.at("affine", l))
                run(f(w(BR + 6 * T, 512), w(INV, 512), ACT.Silu), CV_A, "done", l)

            def split_unit(name, h, u):
                first = FIRST_SLAB[name] + h * EXPERT_SLABS
                n = first + u // 2
                act.wait_ge(landed[n % RING], 16 * (n // RING + 1))
                wait_unit_free(act, name, h, u)
                f(w_hi[:, u % SPLIT_BUFS, :], unit_of_ring(u, first), ACT.Copy).then_inc(unit_hi, 1)

            def split_input(name, n):
                for i in range(2):
                    if i:
                        act.wait_ge(NORM_V.sem, NORM_V.at("hT", n))
                    else:
                        act.wait_ge(input_half, SPLIT[name] + 1)
                    f(h_hi[:, 4 * i:4 * i + 4, :], hT[:, 4 * i:4 * i + 4, :], ACT.Copy).then_inc(input_hi, 1)

            def ffn_split(name, n):
                for u in UNITS[:2]:
                    split_unit(name, 0, u)
                split_input(name, n)
                split_unit(name, 0, UNITS[2])
                for h in range(2):
                    for t in range(FT):
                        act.wait_ge(glu_full, (h + FIRST_EXPERT[name]) * FT + t + 1)
                        act.wait_ge(glu_done, (h + FIRST_EXPERT[name]) * FT + t)
                        f(glu[:, t % 2, :], banks[:, 4 + t % 4, 0:T], ACT.Silu).then_inc(glu_silu, 1)
                        split_unit(name, h, UNITS[t + 3])
                    for u in UNITS[FT + 3:]:
                        split_unit(name, h, u)
                    if h == 0:
                        for u in UNITS[:3]:
                            split_unit(name, 1, u)

            def ffn(name):
                first = FIRST_EXPERT[name]
                with act.Fori(0, N_PARTS[name]) as e:
                    for t in range(FT):
                        act.wait_ge(glu_full, (e + first) * FT + t + 1)
                        act.wait_ge(glu_done, (e + first) * FT + (t if t >= 2 else 1))
                        f(glu[:, t % 2, :], banks[:, 4 + t % 4, 0:T], ACT.Silu).then_inc(glu_silu, 1)

            def experts_short():
                first = FIRST_EXPERT["moe"]
                with act.Fori(0, NE) as e:
                    for t in range(FT):
                        act.wait_ge(glu_full, (e + first) * FT + t + 1)
                        act.wait_ge(glu_done, (e + first) * FT + (t if t >= 2 else 1))
                        f(glu[:, t % 2, 0:CAP], banks[:, 6 + t % 2, 0:CAP], ACT.Silu).then_inc(glu_silu, 1)
                    act.wait_ge(sp_inputs, e + 2)
                    act.wait_ge(sp_scattered, e + 1)
                    f(grid(sel_turned, 2), banks[0:CAP, 4:6, 384:512], ACT.Copy).then_inc(sp_turned, 1)
                    act.wait_ge(sp_result, e + 1)
                    f(result, bank(0, 2, rows=slice(0, CAP)), ACT.Copy).then_inc(sp_copied, 1)

            def lru():
                run(f(small[:, 16:24], par("a_lambda", 0, KT), ACT.Abs))
                run(f(small[:, 16:24], small[:, 16:24], ACT.Exp, scale=-1.0), LR_A, "lambda")
                for q in range(8):
                    act.wait_ge(ain_full, q + 1)
                    src = banks[:, 4 + q % 4, :]
                    if q < 4:
                        ins = f(w(512 * q, 512), src, ACT.Gelu_apprx_tanh)
                    else:
                        dst = w(2048, KT, T + 4)[:, 2 * (q - 4):2 * (q - 4) + 2, 3:3 + T]
                        ins = f(dst, grid(src, 2), ACT.Copy)
                    chain.to(ins, ain_out, q + 1)
                for h in range(KT):
                    act.wait_ge(ag_full, h + 1)
                    src = banks[:, 4 + h % 4, :]
                    run(f(w(8192 + h * T, T), src[:, 0:T], ACT.Sigmoid, bias=par("a_gate_b", h)))
                    chain.to(f(w(10240 + h * T, T), src[:, T:2 * T], ACT.Sigmoid, bias=par("a_gate_b", KT + h)),
                             ag_out, h + 1)
                act.wait_ge(LR_V.sem, LR_V.at("log_a"))
                run(f(w(12288, 2048), w(8192, 2048), ACT.Exp))
                run(f(w(14336, 2048), w(8192, 2048), ACT.Tanh, scale=-1.0), LR_A, "exps")
                act.wait_ge(LR_V.sem, LR_V.at("square"))
                run(f(w(14336, 2048), w(14336, 2048), ACT.Sqrt), LR_A, "root")

            KC, EXW, HIDN, KR, KD, VSW, QR, GA, KCM, VCM = 0, 2048, 3968, 4224, 6272, 8320, 9344, 11392, 11520, 11584

            def kv():
                for n in range(2):
                    act.wait_ge(kv_full, n + 1)
                    src = grid(banks[:, 4 + n, :], 2)
                    dst = w(KC + 1024 * n, G, T)
                    for r in range(2):
                        run(f(dst[0:HD, r::2, :], src[half(r), :, :], ACT.Copy))
                        ins = f(dst[HD:P, r::2, 0:T - 1], src[half(r), :, 1:T], ACT.Copy)
                        if r:
                            chain.to(ins, kv_out, n + 1)
                        else:
                            run(ins)
                for n in range(2):
                    act.wait_ge(kv_full, n + 3)
                    chain.to(f(w(KR + 512 * n, 512), banks[:, 6 + n, :], ACT.Copy), kv_out, n + 3)
                for n in range(2):
                    act.wait_ge(kv_full, n + 5)
                    chain.to(f(w(VSW + 512 * n, 512), banks[:, 4 + n, :], ACT.Copy), kv_out, n + 5)
                for v in range(2):
                    act.wait_ge(KV_P.sem, KV_P.at(f"hidden{v}"))
                    for m in range(2):
                        ins = f(w(HIDN + 128 * v + 64 * m, G * NC), bank(v)[:, 64 * m:64 * m + G * NC],
                                ACT.Gelu_apprx_tanh, bias=par("cmp_b1", 2 * v + m))
                        if m:
                            run(ins, KV_A, f"hidden{v}")
                        else:
                            run(ins)
                act.wait_ge(KV_P.sem, KV_P.at("k_cmp"))
                run(f(w(KCM, G * NC), bank(2)[:, 0:G * NC], ACT.Identity, bias=par("cmp_b2k")), KV_A, "k_cmp")
                act.wait_ge(KV_P.sem, KV_P.at("cmp_mean"))
                run(f(w(EXW, G * NC), bank(3)[:, 0:G * NC], ACT.Sqrt, bias=const("rms_eps")), KV_A, "cmp_norm")
                act.wait_ge(KV_P.sem, KV_P.at("k_mean"))
                run(f(w(EXW + 64, 1024), bank(0, 2), ACT.Sqrt, bias=const("rms_eps")), KV_A, "k_norm")
                act.wait_ge(KV_V.sem, KV_V.at("k_rope"))
                for b in range(2):
                    for d in range(2):
                        for r in range(2):
                            ins = f(w(KD + 1024 * b, G, T)[half(d), r::2, :], w(KR + 512 * b, 2, T)[half(r), :, :], ACT.Copy)
                            if (b, d, r) == (1, 1, 1):
                                run(ins, KV_A, "k_copies")
                            else:
                                run(ins)

            def queries():
                for q in range(4):
                    act.wait_ge(Q_P.sem, Q_P.at(f"full{q}"))
                    run(f(w(QR + 512 * q, 512), banks[:, 4 + q, :], ACT.Copy), Q_A, f"out{q}")
                act.wait_ge(Q_P.sem, Q_P.at("gates"))
                run(f(w(GA, 96), bank(0)[:, 0:96], ACT.Sigmoid), Q_A, "gates")
                act.wait_ge(Q_P.sem, Q_P.at("mean"))
                run(f(w(16896, 2048), bank(0, 4), ACT.Sqrt, bias=const("rms_eps")), Q_A, "norm")

            def attend(u):
                a = u % TT
                n = P * (a + 1)
                act.wait_ge(AT_V.sem, AT_V.at("masked", u))
                for b in range(2):
                    for h in range(4):
                        s = w(16896 + 1024 * b + h * n, n)
                        run(f(s, s, ACT.Exp, bias=small[:, 32 + 4 * b + h:33 + 4 * b + h],
                              accum_out=small[:, 48 + 4 * b + h:49 + 4 * b + h]))
                for h in range(4):
                    s = w(18944 + h * NC, NC)
                    ins = f(s, s, ACT.Exp, bias=small[:, 40 + h:41 + h], accum_out=small[:, 56 + h:57 + h])
                    if h == 3:
                        run(ins, AT_A, "exps", u)
                    else:
                        run(ins)
                act.wait_ge(AT_P.sem, AT_P.at("turned", u))
                run(f(w(19456, 2048)[:, 0:4 * n], bank(0, 2)[:, 0:4 * n], ACT.Copy))
                run(f(w(20480, 2048)[:, 0:4 * n], bank(2, 2)[:, 0:4 * n], ACT.Copy))
                run(f(w(21504, 512, rows=slice(0, NC)), bank(5, rows=slice(0, NC)), ACT.Copy), AT_A, "turned", u)
                act.wait_ge(AT_P.sem, AT_P.at("out", u))
                g = u // TT
                run(f(w(22016, KT, T)[:, 2 * g:2 * g + 2, a * P:a * P + P], grid(bank(6)[:, 0:2 * P], 2), ACT.Copy),
                    AT_A, "out", u)

            for l in range(2):
                norm(2 * l)
                win(l)
                rwkv_front(l)
                for n in range(LEVELS):
                    gates(l, [n])
                    rwkv_level(l, n)
                gates(l, [7])
                rwkv_back(l)
                stick(l)
                retention(l)
                conv_front(l)
                conv_back(l)
                norm(2 * l + 1)
                if l == 0:
                    ffn_split("dense", 1)
                else:
                    act.wait_ge(RT_V.sem, RT_V.at("gap"))
                    run(f(small[:, 4:6], small[:, 6:8], ACT.Exp), RT_A, "exp")
                    act.wait_ge(RT_V.sem, RT_V.at("flag"))
                    with act.If(act.value_load(crowded[0:1, 0:1], min_val=0, max_val=1) == 0):
                        experts_short()
                    with act.Else():
                        ffn("moe")
            norm(4)
            lru()
            norm(5)
            ffn_split("f0", 5)
            norm(6)
            kv()
            norm(7)
            queries()
            for u in range(2 * G):
                attend(u)
            norm(8)
            ffn_split("f1", 8)

        @block.tensor
        def _(pe):
            slab = [0]

            def take(n=None):
                n = slab[0]
                pe.wait_ge(landed[n % RING], 16 * (n // RING + 1))
                slab[0] += 1
                return ring[:, n % RING, :]

            def mm(out_, lhsT, rhs, start=True, stop=True, **kw):
                return pe.matmul(out_, lhsT, rhs, start=start, stop=stop, **kw)

            pending = []

            def used(full, value):
                pending.append((full, value))

            def release():
                while pending:
                    pe.wait_ge(*pending.pop())
                    pe.sem_inc(slab_used, 1)

            def feature_tile(out_, cols, width=512):
                for k in range(KT):
                    ins = mm(out_, cols(k), hT[:, k, :], k == 0, k == KT - 1)
                return ins

            def norm(n):
                pe.wait_ge(NORM_V.sem, NORM_V.at("rows", n))
                for k in range(KT):
                    for a in range(TT):
                        at = (k % 2) * T + a * P
                        ins = pe.transpose(bank(k // 2)[:, at:at + P], scr[:, a * D + k * P:a * D + k * P + P],
                                           const("ident"))
                NORM_P.mark(ins, "done", n)
                pe.wait_ge(NORM_V.sem, NORM_V.at("hT", n))

            def two_tiles(s, q, out_):
                for j in range(2):
                    c = (2 * q + j) * P
                    ins = feature_tile(out_[:, j * T:j * T + T], lambda k: s[:, k * 512 + c:k * 512 + c + P])
                return ins

            def token_tile(s, a, out_, lhs):
                for k in range(KT):
                    ins = mm(out_, lhs[:, k, a * P:a * P + P], s[:, k * 512:k * 512 + 512], k == 0, k == KT - 1)
                return ins

            def fill(s, q, tile, full, out_sem, base, n, last):
                if n >= 4:
                    pe.wait_ge(out_sem, base + n - 3)
                two_tiles(s, q, banks[:, 4 + n % 4, :]).then_inc(full, 1)
                release()
                if last:
                    used(full, base + n + 1)

            def win(l):
                base = 13 * l
                n = 0
                for c in range(7):
                    s = take()
                    for q in range(1 if c == 6 else 2):
                        if c == 4:
                            pe.wait_ge(win_out, base + n - 3)
                            token_tile(s, q, banks[:, 4 + n % 4, :], hT).then_inc(win_full, 1)
                            release()
                            if q == 1:
                                used(win_full, base + n + 1)
                        else:
                            fill(s, q, None, win_full, win_out, base, n, q == 1 or c == 6)
                        n += 1

            def gates(l, slabs):
                for c in slabs:
                    s = take()
                    for q in range(2):
                        n = 2 * c + q
                        if n >= 2:
                            pe.wait_ge(gate_out, 16 * l + n - 1)
                        else:
                            pe.wait_ge(win_out, 13 * l + 13)
                        two_tiles(s, q, banks[:, 6 + q, :]).then_inc(gate_full, 1)
                        release()
                    used(gate_full, 16 * l + 2 * c + 2)

            def mat(q, m):
                return w(MATS + 1024 * q + P * m, P)

            def chunk(at, h, c):
                return w(at + (h // 2) * T + c * P, P, rows=half(h % 2))

            AT_, BT_, KT_, RT_ = PT, PT + 512, PT + 1024, PT + 1536

            def rwkv_front(l):
                pe.wait_ge(RW_A.sem, RW_A.at("lora", l))
                for j in range(2):
                    mm(bank(0)[:, j * T:j * T + T], par(f"w2a2{l}", j * P, P, half(0)), w(INV + 3584, T, rows=half(0)))
                for j in range(2):
                    mm(bank(1)[:, j * T:j * T + T], par(f"w2a2{l}", j * P, P, half(1)), w(MX + 6 * T, T, rows=half(1)))
                for j in range(2):
                    ins = mm(bank(2)[:, j * T:j * T + T], par(f"g2{l}", j * P, P), w(INV + 3840, T))
                RW_P.mark(ins, "lora", l)
                pe.wait_ge(RW_V.sem, RW_V.at("k_squared", l))
                RW_P.mark(mm(bank(3), const("head_sum"), w(INV + 512, 512)), "squares", l)
                pe.wait_ge(RW_V.sem, RW_V.at("operands", l))
                mm(bank(3), const("head_sum"), w(MX, 512))
                for c in range(2):
                    for j in range(2):
                        pe.transpose(bank(4)[:, c * T + j * P:c * T + j * P + P],
                                     w(MX + (4 + j) * T + c * P, P), const("ident"))
                for i, at in enumerate((BT_, KT_)):
                    for j in range(2):
                        ins = pe.transpose(bank(5)[:, i * T + j * P:i * T + j * P + P],
                                           w(at + j * T, P), const("ident"))
                RW_P.mark(ins, "bonus", l)
                pe.wait_ge(RW_V.sem, RW_V.at("bonus_used", l))
                for i, pairs in enumerate((((BT_, AT_), (KT_, AT_)), ((BT_, RT_), (KT_, RT_)))):
                    if i:
                        pe.wait_ge(RW_V.sem, RW_V.at("mats0", l))
                    for q, (lhs, rhs) in enumerate(pairs):
                        for c in range(2):
                            for h in range(NH):
                                at = matrix(h, c) * P
                                ins = mm(bank(2 * q, 2)[:, at:at + P], chunk(lhs, h, c), chunk(rhs, h, c))
                    RW_P.mark(ins, f"mats{i}", l)
                pe.wait_ge(RW_V.sem, RW_V.at("mats1", l))

            def rwkv_level(l, n):
                X, XT, TM, LM = INV, INV + 1024, INV + 2048, LEVEL_AT[n % 2]
                pe.wait_ge(RW_G.sem, RW_G.at(f"M{n}", l))
                if n:
                    pe.wait_ge(RW_V.sem, RW_V.at(f"X{n - 1}", l))
                for m in range(8):
                    ins = mm(bank(0, 2)[:, m * P:m * P + P], w(LM + m * P, P), w(X + m * P, P))
                RW_P.mark(ins, f"T{n}", l)
                pe.wait_ge(RW_A.sem, RW_A.at(f"T{n}", l))
                for m in range(8):
                    ins = mm(bank(2, 2)[:, m * P:m * P + P], w(TM + m * P, P), w(XT + m * P, P))
                if n < LEVELS - 1:
                    for m in range(8):
                        ins = mm(bank(4, 2)[:, m * P:m * P + P], w(XT + m * P, P), w(TM + m * P, P))
                RW_P.mark(ins, f"X{n}", l)

            def rwkv_back(l):
                pe.wait_ge(RW_V.sem, RW_V.at(f"X{LEVELS - 1}", l))
                vrow, brow, krow = 1024, 1536, 1792
                for c in range(2):
                    for h in range(NH):
                        o = bank(h % 2)[:, (h // 2) * HD:(h // 2) * HD + HD]
                        ins = mm(o, mat(1, matrix(h, c)), scr[:, vrow + c * T + h * HD:vrow + c * T + h * HD + HD],
                                 True, c == 0)
                        if c:
                            ins = mm(o, chunk(AT_, h, 1), w(MX + 768 + (h // 2) * HD, HD, rows=half(h % 2)),
                                     False, True)
                    RW_P.mark(ins, f"w{c}", l)
                    pe.wait_ge(RW_A.sem, RW_A.at(f"w{c}", l))
                    for h in range(NH):
                        ins = mm(bank(2)[:, h * HD:h * HD + HD], w(INV + 1024 + matrix(h, c) * P, P),
                                 w(MX + (h % 2) * 2 * HD + (h // 2) * HD, HD))
                    RW_P.mark(ins, f"u{c}", l)
                    pe.wait_ge(RW_A.sem, RW_A.at(f"u{c}", l))
                    if c == 0:
                        for h in range(NH):
                            o = bank(4, rows=half(h % 2))[:, (h // 2) * HD:(h // 2) * HD + HD]
                            mm(o, scr[:, krow + h * HD:krow + h * HD + HD], scr[:, vrow + h * HD:vrow + h * HD + HD],
                               True, False)
                            ins = mm(o, scr[:, brow + h * HD:brow + h * HD + HD], w(MX + 256 + h * HD, HD),
                                     False, True)
                        RW_P.mark(ins, "state", l)
                        pe.wait_ge(RW_V.sem, RW_V.at("state", l))
                for h in range(NH):
                    for c in range(2):
                        o = bank(3, rows=half(h % 2))[:, (h // 2) * T + c * P:(h // 2) * T + c * P + P]
                        mm(o, w(MX + 256 + 256 * c + h * HD, HD), mat(2, matrix(h, c)), True, False)
                        ins = mm(o, scr[:, vrow + c * T + h * HD:vrow + c * T + h * HD + HD], mat(3, matrix(h, c)),
                                 False, c == 0)
                        if c:
                            ins = mm(o, w(MX + 768 + (h // 2) * HD, HD, rows=half(h % 2)), chunk(RT_, h, 1),
                                     False, True)
                RW_P.mark(ins, "y", l)
                pe.wait_ge(RW_V.sem, RW_V.at("y", l))
                RW_P.mark(mm(bank(4), const("head_mean"), w(INV, 512)), "mean", l)
                pe.wait_ge(RW_V.sem, RW_V.at("centred", l))
                RW_P.mark(mm(bank(5), const("head_mean"), w(INV + 1024, 512)), "var", l)

            def scores(q, k, b):
                for t in range(2):
                    for r in range(2):
                        mm(bank(b + 2 * r)[:, t * T:t * T + T], w(k + t * T, P, rows=half(r)), w(q + t * T, T, rows=half(r)))
                for t in range(2):
                    for r in range(2):
                        ins = mm(bank(b + 2 * r + 1)[:, t * P:t * P + P], w(k + t * T + P, P, rows=half(r)),
                                 w(q + t * T + P, P, rows=half(r)))
                return ins

            def weighted(b, v0, at):
                for h in range(NH):
                    r, t = h % 2, h // 2
                    o = bank(b, rows=half(r))[:, t * T:t * T + T]
                    mm(o, vt[:, 0, v0 + h * HD:v0 + h * HD + HD], w(at + r * PAIR + t * T, T), True, False)
                    ins = mm(o[:, P:T], vt[:, 1, v0 + h * HD:v0 + h * HD + HD], w(at + r * PAIR + 2 * T + t * P, P),
                             False, True)
                return ins

            def stick(l):
                pe.wait_ge(SB_V.sem, SB_V.at("squares", l))
                for j in range(2):
                    ins = mm(bank(j), const("head_mean"), w(MATS + 512 * j, 512))
                SB_P.mark(ins, "squares", l)
                pe.wait_ge(SB_V.sem, SB_V.at("qk", l))
                SB_P.mark(scores(PT + 8 * T, PT + 10 * T, 0), "scores", l)
                pe.wait_ge(SB_V.sem, SB_V.at("softplus", l))
                for r in range(2):
                    first, second = MATS + r * PAIR, MATS + r * PAIR + 2 * T
                    mm(bank(2 * r), const("suffix"), w(first, 2 * T), True, False)
                    for t in range(2):
                        mm(bank(2 * r)[:, t * T + P:t * T + T], const("ones"), w(second + t * P, P), False, t == 1)
                    ins = mm(bank(2 * r + 1)[:, 0:2 * P], const("suffix"), w(second, 2 * P))
                SB_P.mark(ins, "suffix", l)
                pe.wait_ge(SB_A.sem, SB_A.at("weights", l))
                SB_P.mark(weighted(4, 0, INV), "out", l)

            def retention(l):
                pe.wait_ge(SB_V.sem, SB_V.at("done", l))
                for j in range(2):
                    ins = mm(bank(j), const("swap"), w(PT + 12 * T + 512 * j, 512))
                RET_P.mark(ins, "rotated", l)
                pe.wait_ge(RET_V.sem, RET_V.at("qk", l))
                RET_P.mark(scores(PT + 12 * T, PT + 14 * T, 0), "scores", l)
                pe.wait_ge(RET_V.sem, RET_V.at("scores", l))
                RET_P.mark(weighted(5, 256, MATS), "out", l)
                pe.wait_ge(RET_V.sem, RET_V.at("y", l))
                RET_P.mark(mm(bank(0), const("head_mean"), w(INV, 512)), "mean", l)
                pe.wait_ge(RET_V.sem, RET_V.at("centred", l))
                RET_P.mark(mm(bank(1), const("head_mean"), w(INV + 1024, 512)), "var", l)

            def conv(l):
                pe.wait_ge(CV_V.sem, CV_V.at("conv", l))
                for j in range(2):
                    ins = mm(bank(0)[:, 0:T], const("ones"), w(MX + 512 + j * T, T), j == 0, j == 1)
                CV_P.mark(ins, "mean", l)
                pe.wait_ge(CV_V.sem, CV_V.at("centred", l))
                for j in range(2):
                    ins = mm(bank(1)[:, 0:T], const("ones"), w(INV + 1024 + j * T, T), j == 0, j == 1)
                CV_P.mark(ins, "var", l)

            def branches(l):
                pe.wait_ge(RET_V.sem, RET_V.at("done", l))
                for c in range(2):
                    if c:
                        pe.wait_ge(CV_A.sem, CV_A.at("done", l))
                    s = take()
                    for i in range(2):
                        for q in range(4):
                            n = 8 * c + 4 * i + q
                            if n >= 4:
                                pe.wait_ge(br_out, 16 * l + n - 3)
                            else:
                                pe.wait_ge(gate_out, 16 * l + 16)
                            for j in range(2):
                                for k in range(2):
                                    at = (2 * i + k) * D + (2 * q + j) * P
                                    ins = mm(banks[:, 4 + n % 4, j * T:j * T + T], s[:, at:at + P],
                                             br[:, 2 * (2 * c + i) + k, :], k == 0, k == 1)
                            ins.then_inc(br_full, 1)
                            release()
                    used(br_full, 16 * l + 8 * c + 8)

            def project(r, lhs):
                for c in range(2):
                    s = take()
                    for a in range(TT):
                        ins = token_tile(s, a, banks[:, 2 * c + a, :], lhs)
                        if a == 0:
                            release()
                    ins.then_inc(proj_full, 1)
                    used(proj_full, 2 * r + c + 1)
                release()

            def slab_of_part(e, j):
                n = slab[0] + j
                pe.wait_ge(landed[n % RING], e * (16 * EXPERT_SLABS // RING) + 16 * (n // RING + 1))
                return ring[:, n % RING, :]

            def split_mm(out_, lhsT, rhs, start, stop):
                mm(out_, lhsT[0], rhs[0], start, False)
                mm(out_, lhsT[0], rhs[1], False, False)
                return mm(out_, lhsT[1], rhs[0], False, stop)

            def ffn_split(name):
                first, first_part = FIRST_EXPERT[name], 2 * SPLIT[name]
                pe.wait_ge(input_lo, 2 * SPLIT[name] + 2)
                with pe.Fori(0, 2) as e:
                    for t in range(FT):
                        if t >= 4:
                            pe.wait_ge(glu_done, (e + first) * FT + t - 2)
                        pe.wait_ge(unit_lo, unit_count(e + first_part, t))
                        for m in range(2):
                            for k in range(KT):
                                at = k * 2 * P + m * P
                                ins = split_mm(banks[:, 4 + t % 4, m * T:m * T + T],
                                               [v[:, t % SPLIT_BUFS, at:at + P] for v in (w_hi, w_lo)],
                                               [v[:, k, :] for v in (h_hi, h_lo)], k == 0, k == KT - 1)
                        ins.then_inc(glu_full, 1)
                    pe.wait_ge(ffn_added, (e + first) * 4 + 1)
                    for k in range(FT):
                        u = OUT_UNIT + k // 2
                        if k % 2 == 0:
                            pe.wait_ge(unit_lo, unit_count(e + first_part, u))
                        pe.wait_ge(hidden_lo, (e + first_part) * FT + k + 1)
                        for b in range(4):
                            at = (k % 2) * D + (b % 2) * 512
                            ins = split_mm(banks[:, b, :],
                                           [v[:, k, (b // 2) * P:(b // 2) * P + P] for v in (g_hi, g_lo)],
                                           [v[:, u % SPLIT_BUFS, at:at + 512] for v in (w_hi, w_lo)],
                                           k == 0, k == FT - 1)
                        if k % 2 or k == FT - 1:
                            ins.then_inc(out_used, 1)
                slab[0] += 2 * EXPERT_SLABS
                pe.wait_ge(slab_used, slab[0])

            def ffn(name):
                first = FIRST_EXPERT[name]
                release()
                with pe.Fori(0, N_PARTS[name]) as e:
                    for j in range(IN_SLABS):
                        s = slab_of_part(e, j)
                        for t in range(2 * j, min(2 * j + 2, FT)):
                            if t >= 4:
                                pe.wait_ge(glu_done, (e + first) * FT + t - 2)
                            for m in range(2):
                                c = (t % 2) * HALF_SLAB + m * P
                                ins = feature_tile(banks[:, 4 + t % 4, m * T:m * T + T],
                                                   lambda k: s[:, k * 2 * P + c:k * 2 * P + c + P])
                            ins.then_inc(glu_full, 1)
                            release()
                        used(glu_full, (e + first) * FT + min(2 * j + 2, FT))
                    pe.wait_ge(ffn_added, (e + first) * 4 + 1)
                    for k in range(FT):
                        if k % 4 == 0:
                            s = slab_of_part(e, IN_SLABS + k // 4)
                        pe.wait_ge(glu_done, (e + first) * FT + k + 2)
                        for b in range(4):
                            at = (k % 4) * D + (b % 2) * 512
                            ins = mm(banks[:, b, :], w(k * T + (b // 2) * P, P), s[:, at:at + 512],
                                     k == 0, k == FT - 1)
                        release()
                        if k % 4 == 3 or k == FT - 1:
                            ins.then_inc(slab_used, 1)
                slab[0] += EXPERT_SLABS * N_PARTS[name]

            def gather():
                for k in range(KT):
                    o = bank(4 + k // 4)[:, (k % 4) * CAP:(k % 4) * CAP + CAP]
                    for a in range(TT):
                        ins = mm(o, scr[:, a * D + k * P:a * D + k * P + P], sel[:, a, :], a == 0, a == TT - 1)
                return ins

            def scatter():
                for b in range(4):
                    ins = mm(bank(b), sel_turned[:, (b // 2) * P:(b // 2) * P + P],
                             result[:, (b % 2) * 512:(b % 2) * 512 + 512])
                ins.then_inc(sp_scattered, 1)

            def experts_short():
                first = FIRST_EXPERT["moe"]
                pe.wait_ge(sp_selected, 1)
                gather().then_inc(sp_gathered, 1)
                with pe.Fori(0, NE) as e:
                    pe.wait_ge(sp_inputs, e + 1)
                    for j in range(IN_SLABS):
                        s = slab_of_part(e, j)
                        for t in range(2 * j, min(2 * j + 2, FT)):
                            if t >= 2:
                                pe.wait_ge(glu_done, (e + first) * FT + t)
                            for m in range(2):
                                for k in range(KT):
                                    at = (t % 2) * HALF_SLAB + k * 2 * P + m * P
                                    ins = mm(banks[:, 6 + t % 2, m * P:m * P + CAP], s[:, at:at + P],
                                             gathered[:, k, :], k == 0, k == KT - 1)
                            ins.then_inc(glu_full, 1)
                            release()
                            if t == 5:
                                pe.wait_ge(sp_copied, e + 1)
                                pe.wait_ge(sp_turned, e + 1)
                                scatter()
                            if t == 8:
                                pe.wait_ge(sp_selected, e + 2)
                                gather()
                                for a in range(TT):
                                    ins = pe.transpose(banks[0:CAP, 4 + a, 384:512], sel_gate[:, a, :], const("ident"))
                                ins.then_inc(sp_gathered, 1)
                        used(glu_full, (e + first) * FT + min(2 * j + 2, FT))
                    pe.wait_ge(sp_added, 4 * e + 5)
                    for k in range(FT):
                        if k % 4 == 0:
                            s = slab_of_part(e, IN_SLABS + k // 4)
                        pe.wait_ge(glu_done, (e + first) * FT + k + 2)
                        for b in range(2):
                            at = (k % 4) * D + b * 512
                            ins = mm(bank(b, rows=slice(0, CAP)), w(k * CAP, CAP), s[:, at:at + 512],
                                     k == 0, k == FT - 1)
                        release()
                        if k % 4 == 3:
                            ins.then_inc(slab_used, 1)
                    ins.then_inc(sp_result, 1)
                    pe.wait_ge(sp_result, e + 1)
                    pe.sem_inc(slab_used, 1)
                pe.wait_ge(sp_copied, NE + 1)
                pe.wait_ge(sp_turned, NE + 1)
                scatter()

            def lru():
                for c in range(4):
                    s = take()
                    for q in range(2):
                        fill(s, q, None, ain_full, ain_out, 0, 2 * c + q, q == 1)
                release()
                s = take()
                pe.wait_ge(LR_V.sem, LR_V.at("conv"))
                for h in range(KT):
                    if h < 4:
                        pe.wait_ge(ain_out, 5 + h)
                    else:
                        pe.wait_ge(ag_out, h - 3)
                    for g in range(2):
                        ins = mm(banks[:, 4 + h % 4, g * T:g * T + T], s[:, g * D + h * P:g * D + h * P + P],
                                 w(6144 + h * T, T))
                    ins.then_inc(ag_full, 1)
                    release()
                used(ag_full, KT)
                release()
                pe.wait_ge(LR_V.sem, LR_V.at("done"))
                project(2, w(6144, KT, T))

            KC, EXW, HIDN, KR, KD, VSW, QR, GA, KCM, VCM = 0, 2048, 3968, 4224, 6272, 8320, 9344, 11392, 11520, 11584

            def kv():
                for c in range(2):
                    s = take()
                    for q in range(2):
                        two_tiles(s, q, banks[:, 4 + 2 * c + q, :]).then_inc(kv_full, 1)
                        release()
                    used(kv_full, 2 * c + 2)
                s = take()
                for a in range(TT):
                    pe.wait_ge(kv_out, a + 1)
                    token_tile(s, a, banks[:, 4 + a, :], hT).then_inc(kv_full, 1)
                    release()
                used(kv_full, 6)
                release()
                pe.wait_ge(KV_V.sem, KV_V.at("windows"))
                for v in range(2):
                    s = take()
                    for m in range(2):
                        for j in range(CB // 2):
                            ins = mm(bank(v)[:, 64 * m:64 * m + G * NC], s[:, j * HID + m * P:j * HID + m * P + P],
                                     w(EXW + 960 * v + j * G * NC, G * NC), j == 0, j == CB // 2 - 1)
                    KV_P.mark(ins, f"hidden{v}")
                    release()
                    used(KV_P.sem, KV_P.at(f"hidden{v}"))
                release()
                pe.wait_ge(KV_A.sem, KV_A.at("hidden1"))
                for m in range(2):
                    ins = mm(bank(2)[:, 0:G * NC], par("cmp_w2k", m * P, P), w(HIDN + 64 * m, G * NC), m == 0, m == 1)
                KV_P.mark(ins, "k_cmp")
                pe.wait_ge(KV_V.sem, KV_V.at("cmp_squares"))
                KV_P.mark(mm(bank(3)[:, 0:G * NC], const("head_mean"), w(EXW, G * NC)), "cmp_mean")
                pe.wait_ge(KV_V.sem, KV_V.at("cmp_normed"))
                KV_P.mark(mm(bank(2)[:, 0:G * NC], const("swap"), w(KCM, G * NC)), "cmp_rot")
                r = slice(0, NC)
                for g in range(G):
                    o = bank(3, rows=r)[:, g * HD:g * HD + HD]
                    for m in range(2):
                        mm(o, w(HIDN + 128 + 64 * m + g * NC, NC), par("cmp_w2v", m * HD, HD), m == 0, False)
                    at, _ = CONSTS["ones"]
                    ins = mm(o, consts[0:1, at:at + NC], par("cmp_b2v", 0, HD, slice(0, 1)), False, True)
                KV_P.mark(ins, "v_cmp")
                pe.wait_ge(KV_V.sem, KV_V.at("k_squares"))
                for j in range(2):
                    ins = mm(bank(j), const("head_mean"), w(EXW + 64 + 512 * j, 512))
                KV_P.mark(ins, "k_mean")
                pe.wait_ge(KV_V.sem, KV_V.at("k_normed"))
                for j in range(2):
                    ins = mm(bank(j), const("swap"), w(KR + 512 * j, 512))
                KV_P.mark(ins, "k_rot")

            def queries():
                for c in range(2):
                    s = take()
                    for q in range(2):
                        Q_P.mark(two_tiles(s, q, banks[:, 4 + 2 * c + q, :]), f"full{2 * c + q}")
                        release()
                    used(Q_P.sem, Q_P.at(f"full{2 * c + 1}"))
                release()
                for a in range(TT):
                    o = bank(0)[:, a * 48:a * 48 + 48]
                    for k in range(KT):
                        mm(o, hT[:, k, a * P:a * P + P], par("gate_w", k * 48, 48), k == 0, False)
                    at, _ = CONSTS["ones"]
                    ins = mm(o, consts[0:1, at:at + P], par("gate_b", 0, 48, slice(0, 1)), False, True)
                Q_P.mark(ins, "gates")
                pe.wait_ge(Q_A.sem, Q_A.at("gates"))
                pe.wait_ge(Q_V.sem, Q_V.at("squares"))
                for j in range(4):
                    ins = mm(bank(j), const("head_mean"), w(16896 + 512 * j, 512))
                Q_P.mark(ins, "mean")
                pe.wait_ge(Q_V.sem, Q_V.at("normed"))
                for j in range(4):
                    ins = mm(bank(j), const("swap"), w(QR + 512 * j, 512))
                Q_P.mark(ins, "rot")
                pe.wait_ge(Q_V.sem, Q_V.at("rope"))
                pe.wait_ge(KV_A.sem, KV_A.at("k_copies"))
                pe.wait_ge(KV_V.sem, KV_V.at("v_cmp"))

            def attend(u):
                g, a = u // TT, u % TT
                n = P * (a + 1)
                if u:
                    pe.wait_ge(AT_A.sem, AT_A.at("out", u - 1))
                for b in range(2):
                    for t in range(2):
                        for r in range(2):
                            mm(bank(2 * b + r)[:, t * n:t * n + n], w(QR + (2 * g + t) * T + a * P, P, rows=half(r)),
                               w(KD + 1024 * b + g * T, n, rows=half(r)))
                for t in range(2):
                    for r in range(2):
                        ins = mm(bank(4 + r)[:, t * NC:t * NC + NC], w(QR + (2 * g + t) * T + a * P, P, rows=half(r)),
                                 w(KCM + g * NC, NC, rows=half(r)))
                AT_P.mark(ins, "scores", u)
                pe.wait_ge(AT_V.sem, AT_V.at("probs", u))
                for b in range(2):
                    for i in range(4):
                        for c in range(a + 1):
                            pe.transpose(bank(2 * b, 2)[:, i * n + c * P:i * n + c * P + P],
                                         w(16896 + 1024 * b + i * n + c * P, P), const("ident"))
                for i in range(4):
                    ins = pe.transpose(bank(5, rows=slice(0, NC))[:, i * P:i * P + P], w(18944 + i * NC, NC),
                                       const("ident"))
                AT_P.mark(ins, "turned", u)
                pe.wait_ge(AT_A.sem, AT_A.at("turned", u))
                for i in range(4):
                    o = bank(6, rows=half(i // 2))[:, (i % 2) * P:(i % 2) * P + P]
                    mm(o, w(VCM + g * HD, HD, rows=slice(0, NC)), w(21504 + i * P, P, rows=slice(0, NC)), True, False)
                    for b in range(2):
                        for c in range(a + 1):
                            ins = mm(o, w(VSW + 512 * c + 256 * b + g * HD, HD),
                                     w(19456 + 1024 * b + i * n + c * P, P), False, b == 1 and c == a)
                AT_P.mark(ins, "out", u)

            for l in range(2):
                norm(2 * l)
                win(l)
                rwkv_front(l)
                for n in range(LEVELS):
                    gates(l, [n])
                    rwkv_level(l, n)
                gates(l, [7])
                rwkv_back(l)
                stick(l)
                retention(l)
                conv(l)
                branches(l)
                pe.wait_ge(br_out, 16 * l + 16)
                project(l, scr[:, :].rearrange("p (k t) -> p k t", k=KT))
                norm(2 * l + 1)
                if l == 0:
                    ffn_split("dense")
                else:
                    for a in range(TT):
                        for k in range(KT):
                            ins = mm(bank(0)[:, a * NE:a * NE + NE], hT[:, k, a * P:a * P + P],
                                     par("router", k * NE, NE), k == 0, k == KT - 1)
                    RT_P.mark(ins, "logits")
                    pe.wait_ge(RT_V.sem, RT_V.at("chosen"))
                    for a in range(TT):
                        mm(bank(1)[:, a * NE:a * NE + NE], const("strict"), chosen[:, a, 0:NE], True, a == 0)
                        if a:
                            mm(bank(1)[:, a * NE:a * NE + NE], const("ones"), chosen[:, 0, 0:NE], False, True)
                    for a in range(TT):
                        ins = mm(bank(1)[:, 2 * NE:3 * NE], const("ones"), chosen[:, a, 0:NE], a == 0, a == 1)
                    RT_P.mark(ins, "slots")
                    release()
                    pe.wait_ge(RT_V.sem, RT_V.at("flag"))
                    with pe.If(pe.value_load(crowded[0:1, 0:1], min_val=0, max_val=1) == 0):
                        experts_short()
                    with pe.Else():
                        ffn("moe")
                        slab[0] -= EXPERT_SLABS * NE
                    slab[0] += EXPERT_SLABS * NE
            norm(4)
            lru()
            norm(5)
            ffn_split("f0")
            norm(6)
            kv()
            norm(7)
            queries()
            for u in range(2 * G):
                attend(u)
            pe.wait_ge(AT_A.sem, AT_A.at("out", 2 * G - 1))
            project(3, w(22016, KT, T))
            norm(8)
            ffn_split("f1")
            assert slab[0] == n_slabs

        @block.vector
        def _(dve):
            chain = Chain(dve, v_chain)
            run = chain.run
            tt, ts, stt = dve.tensor_tensor, dve.tensor_scalar, dve.scalar_tensor_tensor
            MUL, ADD, SUB, MAX = ALU.mult, ALU.add, ALU.subtract, ALU.max

            def bc(ap, n):
                return ap.unsqueeze(1).to_broadcast([ap.shape[0], n, ap.shape[1]])

            def bc22(ap):
                return ap.unsqueeze(1).unsqueeze(1).to_broadcast([P, 2, 2, P])

            chain.to(dve.memset(small[:, 13:14], 0.0), glu_done, 1)
            chain.to(dve.memset(small[:, 14:15], 0.0), ffn_added, 1)

            def split_unit(name, h, u):
                first = FIRST_SLAB[name] + h * EXPERT_SLABS
                n = unit_count(2 * SPLIT[name] + h, u)
                dve.wait_ge(unit_hi, n)
                wait_unit_free(dve, name, h, u)
                tt(w_lo[:, u % SPLIT_BUFS, :], unit_of_ring(u, first), w_hi[:, u % SPLIT_BUFS, :].bitcast(F32),
                   SUB).then_inc(unit_lo, 1)
                if u % 2 or u == FT - 1:
                    dve.wait_ge(unit_lo, n)
                    dve.sem_inc(slab_used, 1)

            def split_input(name):
                for i in range(2):
                    dve.wait_ge(input_hi, 2 * SPLIT[name] + i + 1)
                    ks = slice(4 * i, 4 * i + 4)
                    tt(h_lo[:, ks, :], hT[:, ks, :], h_hi[:, ks, :].bitcast(F32), SUB).then_inc(input_lo, 1)

            def ffn_split(name):
                split_input(name)
                split_unit(name, 0, UNITS[1])
                split_unit(name, 0, UNITS[2])
                for h in range(2):
                    first = FIRST_EXPERT[name] + h
                    for t in range(FT):
                        dve.wait_ge(glu_silu, first * FT + t + 1)
                        tt(hidden[:, t, :], glu[:, t % 2, :], banks[:, 4 + t % 4, T:2 * T], MUL).then_inc(glu_done, 1)
                        split_unit(name, h, UNITS[t + 3])
                    for u in UNITS[FT + 3:]:
                        split_unit(name, h, u)
                    if h == 0:
                        for u in UNITS[:2]:
                            split_unit(name, 1, u)
                    dve.wait_ge(out_used, (2 * SPLIT[name] + h + 1) * OUT_UNITS)
                    dve.wait_ge(ffn_added, first * 4 + 1)
                    for b in range(4):
                        xs = x[:, b // 2, (b % 2) * 512:(b % 2) * 512 + 512]
                        tt(xs, xs, banks[:, b, :], ADD).then_inc(ffn_added, 1)
                    if h == 0:
                        split_unit(name, 1, UNITS[2])
                dve.wait_ge(ffn_added, 4 * (FIRST_EXPERT[name] + 2) + 1)

            def norm(n, gain):
                dve.wait_ge(NORM_A.sem, NORM_A.at("root", n))
                run(dve.reciprocal(small[:, 0:2], small[:, 2:4]))
                for a in range(TT):
                    ins = ts(scr[:, a * D:a * D + D], x[:, a, :], small[:, a:a + 1], None, MUL)
                    if a:
                        run(ins, NORM_V, "rows", n)
                    else:
                        run(ins)
                split = SPLIT_NORMS.get(n)
                if split:
                    dve.wait_ge(slab_used, FIRST_SLAB[split])
                    split_unit(split, 0, UNITS[0])
                dve.wait_ge(NORM_P.sem, NORM_P.at("done", n))
                for k in range(KT):
                    ins = ts(hT[:, k, :], bank(k // 2)[:, (k % 2) * T:(k % 2) * T + T], par(gain, k), None, MUL)
                    if split and k == KT // 2 - 1:
                        chain.to(ins, input_half, SPLIT[split] + 1)
                    elif k == KT - 1:
                        run(ins, NORM_V, "hT", n)
                    else:
                        run(ins)

            def rwkv_front(l):
                dve.wait_ge(win_out, 13 * l + 4)
                p, d = w(PT, 8, T), w(INV, 8, T)
                run(tt(d[:, :, 1:T], p[:, :, 0:T - 1], p[:, :, 1:T], SUB))
                run(ts(d[:, :, 0:1], p[:, :, 0:1], -1.0, None, MUL))
                m = w(MX, 8, T)
                for j in range(8):
                    ins = stt(m[:, j, :], d[:, j, :], par(f"mu{l}", j), p[:, j, :], MUL, ADD)
                    if j == 7:
                        run(ins, RW_V, "mixed", l)
                    else:
                        run(ins)
                r, k, v, a = (w(MX + 512 * i, 512) for i in range(4))
                kk, sq, rinv = w(INV, 512), w(INV + 512, 512), w(INV + 1024, 512)
                sw, c, cex = w(INV + 1536, 512), w(INV + 2048, 512), w(INV + 2560, 512)
                e1, e2, e3 = w(PT, 512), w(INV + 3072, 512), w(PT + 1536, 512)
                at_, bt_, kt_, rt_ = (w(PT + 512 * i, 512) for i in range(4))
                for j in range(2):
                    run(ts(kk[:, j * T:j * T + T], k[:, j * T:j * T + T], par(f"k_k{l}", j), None, MUL))
                run(tt(sq, kk, kk, MUL), RW_V, "k_squared", l)
                dve.wait_ge(RW_A.sem, RW_A.at("sigmoids", l))
                run(ts(sw, sw, -DECAY_SCALE, None, MUL))
                for j in range(4):
                    s = slice(j * P, j * P + P)
                    run(dve.tensor_tensor_scan(c[:, s], const("ones"), sw[:, s], 0.0, MUL, ADD))
                run(tt(cex, c, sw, SUB), RW_V, "decays", l)
                dve.wait_ge(RW_A.sem, RW_A.at("norm", l))
                run(ts(rinv, rinv, 1e-12, None, MAX))
                run(dve.reciprocal(rinv, rinv))
                run(tt(kk, kk, rinv, MUL))
                for j in range(2):
                    s = slice(j * T, j * T + T)
                    run(ts(sq[:, s], a[:, s], 1.0, par(f"k_a{l}", j), SUB, MUL))
                run(stt(k, sq, 1.0, k, ADD, MUL))
                run(tt(sw, kk, a, MUL))
                dve.wait_ge(RW_A.sem, RW_A.at("exps", l))
                run(stt(at_, kk, -1.0, e1, MUL, MUL))
                run(tt(bt_, sw, e2, MUL))
                run(tt(kt_, k, e2, MUL))
                run(tt(rt_, r, e3, MUL))
                for j in range(2):
                    s = slice(j * T, j * T + T)
                    ins = stt(r[:, s], r[:, s], par(f"r_k{l}", j), k[:, s], MUL, MUL)
                    if j:
                        run(ins, RW_V, "operands", l)
                    else:
                        run(ins)
                dve.wait_ge(RW_P.sem, RW_P.at("bonus", l))
                run(tt(scr[:, 512:1024], bank(3), v, MUL), RW_V, "bonus_used", l)
                dve.wait_ge(RW_G.sem, RW_G.at("zeroed", l))
                for i in range(2):
                    dve.wait_ge(RW_P.sem, RW_P.at(f"mats{i}", l))
                    mask = bc(const("causal" if i else "strict").bitcast(I32), 8)
                    for q in range(2):
                        ins = dve.copy_predicated(w(MATS + 1024 * (2 * i + q), 8, P), mask, grid(bank(2 * q, 2), 8))
                        if q:
                            run(ins, RW_V, f"mats{i}", l)
                        else:
                            run(ins)
                    if i == 0:
                        for at in (INV, INV + 1024):
                            run(dve.tensor_copy(w(at, 8, P), bc(const("ident"), 8)))

            def rwkv_level(l, n):
                dve.wait_ge(RW_P.sem, RW_P.at(f"X{n}", l))
                xt = w(INV + 1024, 1024)
                if n < LEVELS - 1:
                    run(tt(w(INV, 1024), w(INV, 1024), bank(4, 2), ADD))
                run(tt(xt, xt, bank(2, 2), ADD), RW_V, f"X{n}", l)

            def head_norm(b_mean, P_, V_, A_, y, xc, sq, dev, l):
                dve.wait_ge(P_.sem, P_.at("mean", l))
                run(tt(xc, y, bank(b_mean), SUB))
                run(tt(sq, xc, xc, MUL), V_, "centred", l)
                dve.wait_ge(A_.sem, A_.at("dev", l))
                run(dve.reciprocal(dev, dev))
                run(tt(y, xc, dev, MUL))

            def rwkv_back(l):
                dve.wait_ge(RW_P.sem, RW_P.at("state", l))
                for j in range(2):
                    ins = ts(w(MX + 768 + j * HD, HD), bank(4)[:, j * HD:j * HD + HD], small[:, 8 + j:9 + j], None, MUL)
                    if j:
                        run(ins, RW_V, "state", l)
                    else:
                        run(ins)
                dve.wait_ge(RW_P.sem, RW_P.at("y", l))
                y, xc, sq, dev = (w(INV + 512 * i, 512) for i in range(4))
                run(dve.tensor_copy(y, bank(3)), RW_V, "y", l)
                head_norm(4, RW_P, RW_V, RW_A, y, xc, sq, dev, l)
                for j in range(2):
                    s = slice(j * T, j * T + T)
                    run(ts(y[:, s], y[:, s], par(f"ln_w{l}", j), par(f"ln_b{l}", j), MUL, ADD))
                run(tt(y, y, scr[:, 512:1024], ADD))
                run(tt(w(BR, 512), y, scr[:, 0:512], MUL), RW_V, "done", l)

            def stick(l):
                qk, sq = w(PT + 8 * T, 1024), w(MATS, 1024)
                run(tt(sq, qk, qk, MUL), SB_V, "squares", l)
                dve.wait_ge(SB_A.sem, SB_A.at("norm", l))
                run(dve.reciprocal(sq, sq))
                run(tt(qk, qk, sq, MUL))
                run(ts(qk[:, 0:512], qk[:, 0:512], par(f"sb_q{l}"), HD ** -0.5, MUL, MUL))
                run(ts(qk[:, 512:1024], qk[:, 512:1024], par(f"sb_k{l}"), None, MUL), SB_V, "qk", l)
                z, ln, sp_ = w(MATS + 2048, 1536), w(INV, 1536), w(MATS, 1536)
                dve.wait_ge(SB_A.sem, SB_A.at("ln", l))
                run(stt(sp_, z, 0.0, ln, MAX, ADD))
                first, second = diagonals(MATS)
                run(tt(first, first, bc22(const("strict")), MUL))
                run(tt(second, second, bc22(const("strict")), MUL), SB_V, "softplus", l)
                dve.wait_ge(SB_P.sem, SB_P.at("suffix", l))
                run(tt(w(INV, 2, PAIR), w(MATS + 2048, 2, PAIR), pairs(0), SUB))
                first, second = diagonals(INV)
                run(tt(first, first, bc22(const("not_before")), ADD))
                run(tt(second, second, bc22(const("not_before")), ADD), SB_V, "logs", l)
                dve.wait_ge(SB_P.sem, SB_P.at("out", l))
                run(dve.tensor_copy(w(BR + 512, 512), bank(4)), SB_V, "done", l)

            def rotate(dst, rot, cos, sin, tmp, groups, steps, name, rnd=0):
                run(tt(tmp, rot, bc(sin, groups), MUL))
                run(tt(dst, dst, bc(cos, groups), MUL))
                run(tt(dst, dst, tmp, ADD), steps, name, rnd)

            def retention(l):
                dve.wait_ge(RET_P.sem, RET_P.at("rotated", l))
                rotate(w(PT + 12 * T, 4, T), grid(bank(0, 2), 4), const("cos"), const("sin"), w(MATS, 4, T), 4,
                       RET_V, "qk", l)
                dve.wait_ge(RET_P.sem, RET_P.at("scores", l))
                dec = grid(const("decay"), 2)
                s = pairs(0)
                run(tt(w(MATS, 2, PAIR)[:, :, 0:2 * T], s[:, :, 0:2 * T], dec, MUL))
                dec = dec.rearrange("p r (t s) -> p r t s", t=2)[:, :, :, 0:P]
                run(tt(diagonals(MATS)[1], s[:, :, 2 * T:PAIR].rearrange("p r (t s) -> p r t s", t=2), dec, MUL),
                    RET_V, "scores", l)
                dve.wait_ge(RET_P.sem, RET_P.at("out", l))
                y, xc, sq, dev = (w(INV + 512 * i, 512) for i in range(4))
                run(dve.tensor_copy(y, bank(5)), RET_V, "y", l)
                head_norm(0, RET_P, RET_V, RET_A, y, xc, sq, dev, l)
                dve.wait_ge(RET_A.sem, RET_A.at("silu", l))
                for j in range(2):
                    ins = stt(w(BR + 1024 + j * T, T), y[:, j * T:j * T + T], par(f"gn{l}", j),
                              w(MX + j * T, T), MUL, MUL)
                    if j:
                        run(ins, RET_V, "done", l)
                    else:
                        run(ins)

            def conv(l):
                dve.wait_ge(CV_A.sem, CV_A.at("sigmoid", l))
                pad = TAPS - 1
                u = w(MATS, 2, pad + T)
                run(dve.memset(u[:, :, 0:pad], 0.0))
                run(tt(u[:, :, pad:pad + T], w(PT + 18 * T, 2, T), w(MX + 1536, 2, T), MUL))
                acc = [w(MX + 512 + j * T, T) for j in range(2)]
                for i in range(TAPS):
                    for j in range(2):
                        if i == 0:
                            ins = ts(acc[j], u[:, j, i:i + T], par(f"dw{l}", j * TAPS + i), par(f"db{l}", j), MUL, ADD)
                        else:
                            ins = stt(acc[j], u[:, j, i:i + T], par(f"dw{l}", j * TAPS + i), acc[j], MUL, ADD)
                        if i == TAPS - 1 and j == 1:
                            run(ins, CV_V, "conv", l)
                        else:
                            run(ins)
                y, xc, sq, dev = w(MX + 512, 2, T), w(INV + 512, 2, T), w(INV + 1024, 2, T), w(MX + 1024, T)
                dve.wait_ge(CV_P.sem, CV_P.at("mean", l))
                run(stt(xc, bc(bank(0)[:, 0:T], 2), -1.0 / 256, y, MUL, ADD))
                run(stt(sq, xc, 1.0 / 256, xc, MUL, MUL), CV_V, "centred", l)
                dve.wait_ge(CV_A.sem, CV_A.at("dev", l))
                run(dve.reciprocal(dev, dev))
                run(tt(xc, xc, bc(dev, 2), MUL))
                for j in range(2):
                    ins = ts(w(INV + j * T, T), xc[:, j, :], par(f"cln_w{l}", j), par(f"cln_b{l}", j), MUL, ADD)
                    if j:
                        run(ins, CV_V, "affine", l)
                    else:
                        run(ins)

            def merge(l):
                dve.wait_ge(gate_out, 16 * l + 16)
                for n in range(16):
                    dve.wait_ge(br_full, 16 * l + n + 1)
                    q = n % 4
                    b = banks[:, 4 + n % 4, :]
                    dst = scr[:, 512 * q:512 * q + 512]
                    if n < 4:
                        ins = tt(dst, w(SIG + 512 * n, 512), b, MUL)
                    else:
                        s = w(SIG + 512 * n, 512)
                        run(tt(s, s, b, MUL))
                        ins = tt(dst, dst, s, ADD)
                    chain.to(ins, br_out, 16 * l + n + 1)

            def project(r):
                for c in range(2):
                    dve.wait_ge(proj_full, 2 * r + c + 1)
                    for a in range(TT):
                        xs = x[:, a, 512 * c:512 * c + 512]
                        ins = tt(xs, xs, banks[:, 2 * c + a, :], ADD)
                        if a:
                            chain.to(ins, proj_added, 2 * r + c + 1)
                        else:
                            run(ins)

            def route():
                dve.wait_ge(RT_P.sem, RT_P.at("logits"))
                lg = small[:, 64:64 + TT * NE].rearrange("p (a e) -> p a e", a=TT)
                top = small[:, 96:96 + TT * 8].rearrange("p (a e) -> p a e", a=TT)
                idx = small[:, 128:128 + TT * 8].rearrange("p (a e) -> p a e", a=TT)
                run(dve.tensor_copy(lg, bank(0)[:, 0:TT * NE].rearrange("p (a e) -> p a e", a=TT)))
                for a in range(TT):
                    run(dve.max(top[:, a, :], lg[:, a, :]))
                    run(dve.max_index(top_index[:, a, :], top[:, a, :], lg[:, a, :]))
                run(dve.tensor_copy(idx, top_index[:, :, :]))
                run(tt(small[:, 6:8], top[:, :, 1], top[:, :, 0], SUB), RT_V, "gap")
                dve.wait_ge(RT_A.sem, RT_A.at("exp"))
                run(ts(small[:, 8:10], small[:, 4:6], 1.0, None, ADD))
                run(dve.reciprocal(small[:, 8:10], small[:, 8:10]))
                run(tt(small[:, 10:12], small[:, 8:10], small[:, 4:6], MUL))
                run(dve.memset(w(5504, 96), 0.0))
                for a in range(TT):
                    tmp = small[:, 160:160 + NE]
                    run(ts(router_gates[:, a, :], const("experts"), idx[:, a, 0:1], small[:, 8 + a:9 + a],
                           ALU.is_equal, MUL))
                    run(ts(tmp, const("experts"), idx[:, a, 1:2], small[:, 10 + a:11 + a], ALU.is_equal, MUL))
                    run(tt(router_gates[:, a, :], router_gates[:, a, :], tmp, ADD))
                    run(ts(tmp, const("experts"), idx[:, a, 0:1], None, ALU.is_equal))
                    ins = stt(chosen[:, a, 0:NE], const("experts"), idx[:, a, 1:2], tmp, ALU.is_equal, ADD)
                    if a:
                        run(ins, RT_V, "chosen")
                    else:
                        run(ins)
                run(dve.tensor_copy(gate_of[:, :, 0:NE], router_gates[:, :, :]))
                dve.wait_ge(RT_P.sem, RT_P.at("slots"))
                run(dve.tensor_copy(slot[:, :, 0:NE], grid(bank(1)[:, 0:2 * NE], 2)))
                run(dve.tensor_reduce(small[:, 12:13], bank(1)[:, 2 * NE:3 * NE], AX, MAX))
                run(ts(crowded[:, :], small[:, 12:13], float(CAP), None, ALU.is_gt), RT_V, "flag")

            def select(dst, weight, e):
                for a in range(TT):
                    ins = ts(dst[:, a, :], const("slots"), slot[:, a, bass.ds(e, 1)], weight[:, a, bass.ds(e, 1)],
                             ALU.is_equal, MUL)
                return ins

            def take_inputs():
                src = banks[:, 4:6, 0:4 * CAP].rearrange("p b (k s) -> p b k s", k=4)
                gain = par("norm_ffn1", 0, KT).rearrange("p (b k) -> p b k", b=2).unsqueeze(3)
                tt(gathered.rearrange("p (b k) s -> p b k s", b=2), src, gain.to_broadcast([P, 2, 4, CAP]),
                   MUL).then_inc(sp_inputs, 1)

            def add_scattered(e):
                dve.wait_ge(sp_scattered, e + 1)
                dve.wait_ge(sp_added, 4 * e + 1)
                for b in range(4):
                    xs = x[:, b // 2, (b % 2) * 512:(b % 2) * 512 + 512]
                    tt(xs, xs, bank(b), ADD).then_inc(sp_added, 1)

            def experts_short():
                first = FIRST_EXPERT["moe"]
                dve.memset(result, 0.0).then_inc(sp_copied, 1)
                dve.memset(sel_turned, 0.0).then_inc(sp_turned, 1)
                dve.memset(small[:, 13:14], 0.0).then_inc(sp_added, 1)
                select(sel, chosen, 0).then_inc(sp_selected, 1)
                dve.wait_ge(sp_gathered, 1)
                take_inputs()
                with dve.Fori(0, NE) as e:
                    dve.wait_ge(sp_gathered, e + 1)
                    select(sel_gate, gate_of, e)
                    select(sel, chosen, e + 1).then_inc(sp_selected, 1)
                    for t in range(FT):
                        dve.wait_ge(glu_silu, (e + first) * FT + t + 1)
                        tt(w(t * CAP, CAP), glu[:, t % 2, 0:CAP], banks[:, 6 + t % 2, P:P + CAP], MUL)\
                            .then_inc(glu_done, 1)
                        if t == 6:
                            add_scattered(e)
                    dve.wait_ge(sp_gathered, e + 2)
                    take_inputs()
                add_scattered(NE)
                dve.wait_ge(sp_added, 4 * NE + 5)
                dve.sem_inc(ffn_added, 4 * NE)

            def ffn(name, gates_):
                first = FIRST_EXPERT[name]
                with dve.Fori(0, N_PARTS[name]) as e:
                    for t in range(FT):
                        dve.wait_ge(glu_silu, (e + first) * FT + t + 1)
                        tt(w(t * T, T), glu[:, t % 2, :], banks[:, 4 + t % 4, T:2 * T], MUL).then_inc(glu_done, 1)
                    dve.wait_ge(slab_used, e * EXPERT_SLABS + LAST_MOE_SLAB)
                    dve.wait_ge(ffn_added, (e + first) * 4 + 1)
                    for b in range(4):
                        xs = x[:, b // 2, (b % 2) * 512:(b % 2) * 512 + 512]
                        stt(xs, banks[:, b, :], gates_[:, b // 2, bass.ds(e, 1)], xs, MUL, ADD).then_inc(ffn_added, 1)
                dve.wait_ge(ffn_added, 4 * (first + N_PARTS[name]) + 1)

            def lru():
                lam = par("a_lambda", 0, KT)
                e, s, s2, acc, cl = (small[:, 16 + 8 * i:24 + 8 * i] for i in range(5))
                dve.wait_ge(LR_A.sem, LR_A.at("lambda"))
                run(ts(s, e, 2.0, None, ADD))
                run(dve.reciprocal(s, s))
                run(tt(s, s, e, MUL))
                run(tt(s2, s, s, MUL))
                run(ts(acc, s2, 1.0 / 17, 1.0 / 15, MUL, ADD))
                for n in (13, 11, 9, 7, 5, 3, 1):
                    run(tt(acc, acc, s2, MUL))
                    run(ts(acc, acc, 1.0 / n, None, ADD))
                run(tt(acc, acc, s, MUL))
                run(ts(cl, lam, -1.0, 0.0, MUL, MAX))
                run(stt(cl, acc, 2.0, cl, MUL, ADD))
                run(ts(cl, cl, -LRU_C, None, MUL))
                z = w(2048, KT, T + 4)
                xr = w(6144, KT, T)
                run(dve.memset(z[:, :, 0:3], 0.0))
                for q in range(4):
                    dve.wait_ge(ain_out, 5 + q)
                    for i in range(TAPS2):
                        for k in range(2 * q, 2 * q + 2):
                            wk = par("a_conv_w", k * TAPS2 + i)
                            if i == 0:
                                ins = ts(xr[:, k, :], z[:, k, i:i + T], wk, par("a_conv_b", k), MUL, ADD)
                            else:
                                ins = stt(xr[:, k, :], z[:, k, i:i + T], wk, xr[:, k, :], MUL, ADD)
                            if (q, i, k) == (3, TAPS2 - 1, KT - 1):
                                run(ins, LR_V, "conv")
                            else:
                                run(ins)
                la, gi, a, th = w(8192, KT, T), w(10240, 2048), w(12288, 2048), w(14336, 2048)
                for h in range(KT):
                    dve.wait_ge(ag_out, h + 1)
                    ins = ts(la[:, h, :], la[:, h, :], cl[:, h:h + 1], None, MUL)
                    if h == KT - 1:
                        run(ins, LR_V, "log_a")
                    else:
                        run(ins)
                run(tt(gi, gi, w(6144, 2048), MUL))
                dve.wait_ge(LR_A.sem, LR_A.at("exps"))
                run(tt(w(8192, 2048), a, a, MUL))
                run(stt(th, w(8192, 2048), 1.0, th, ADD, MUL), LR_V, "square")
                dve.wait_ge(LR_A.sem, LR_A.at("root"))
                run(tt(gi, gi, th, MUL))
                for h in range(KT):
                    s_ = slice(h * T, h * T + T)
                    run(dve.tensor_tensor_scan(w(8192, 2048)[:, s_], a[:, s_], gi[:, s_], 0.0, MUL, ADD))
                run(tt(w(6144, 2048), w(8192, 2048), w(0, 2048), MUL), LR_V, "done")

            KC, EXW, HIDN, KR, KD, VSW, QR, GA, KCM, VCM = 0, 2048, 3968, 4224, 6272, 8320, 9344, 11392, 11520, 11584

            def kv():
                dve.wait_ge(kv_out, 2)
                for v in range(2):
                    src = w(KC + 1024 * v, G, T).rearrange("p g (n s) -> p s g n", s=CS)
                    for j in range(2):
                        pos = par("cmp_pos", 16 * v + 8 * j, 8).unsqueeze(2).unsqueeze(3).to_broadcast([P, 8, G, NC])
                        ins = tt(w(EXW + 960 * v + 480 * j, 8, G, NC), src[:, 0::2, :, j:j + NC], pos, ADD)
                        if v and j:
                            run(ins, KV_V, "windows")
                        else:
                            run(ins)

            def keys():
                dve.wait_ge(kv_out, 4)
                dve.wait_ge(KV_P.sem, KV_P.at("hidden1"))
                k, sq = w(KR, 1024), w(EXW + 64, 1024)
                run(tt(sq, k, k, MUL), KV_V, "k_squares")
                dve.wait_ge(KV_A.sem, KV_A.at("k_norm"))
                run(dve.reciprocal(sq, sq))
                run(tt(k, k, sq, MUL))
                run(ts(k[:, 0:512], k[:, 0:512], par("k_norm", 1), None, MUL))
                run(ts(k[:, 512:1024], k[:, 512:1024], par("k_norm", 2), None, MUL), KV_V, "k_normed")
                dve.wait_ge(KV_P.sem, KV_P.at("k_rot"))
                rotate(w(KR, 4, T), grid(bank(0, 2), 4), const("cos"), const("sin"), w(EXW + 64, 4, T), 4,
                       KV_V, "k_rope")

            def kv_cmp():
                dve.wait_ge(KV_A.sem, KV_A.at("k_cmp"))
                k, sq = w(KCM, G * NC), w(EXW, G * NC)
                run(tt(sq, k, k, MUL), KV_V, "cmp_squares")
                dve.wait_ge(KV_A.sem, KV_A.at("cmp_norm"))
                run(dve.reciprocal(sq, sq))
                run(tt(k, k, sq, MUL))
                run(ts(k, k, par("k_norm", 0), None, MUL), KV_V, "cmp_normed")
                dve.wait_ge(KV_P.sem, KV_P.at("cmp_rot"))
                rotate(w(KCM, G, NC), grid(bank(2)[:, 0:G * NC], G), const("cos_cmp"), const("sin_cmp"),
                       w(EXW, G, NC), G, KV_V, "cmp_rope")
                dve.wait_ge(KV_P.sem, KV_P.at("v_cmp"))
                r = slice(0, NC)
                run(dve.tensor_copy(w(VCM, G * HD, rows=r), bank(3, rows=r)[:, 0:G * HD]), KV_V, "v_cmp")

            def queries():
                dve.wait_ge(Q_A.sem, Q_A.at("out3"))
                q, sq = w(QR, 2048), w(16896, 2048)
                run(tt(sq, q, q, MUL), Q_V, "squares")
                dve.wait_ge(Q_A.sem, Q_A.at("norm"))
                run(dve.reciprocal(sq, sq))
                run(tt(q, q, sq, MUL))
                run(ts(q, q, par("q_norm"), None, MUL), Q_V, "normed")
                dve.wait_ge(Q_P.sem, Q_P.at("rot"))
                rotate(w(QR, KT, T), grid(bank(0, 4), KT), const("cos"), const("sin"), w(16896, KT, T), KT,
                       Q_V, "rope")

            def attend(u):
                g, a = u // TT, u % TT
                n = P * (a + 1)
                at, _ = CONSTS["causal_add"]
                mask = consts[:, at + (1 - a) * P:at + 2 * P]
                dve.wait_ge(AT_P.sem, AT_P.at("scores", u))
                for b in range(2):
                    s = w(16896 + 1024 * b, 4, n)
                    for r in range(2):
                        run(stt(s[:, 2 * r:2 * r + 2, :], grid(bank(2 * b + r)[:, 0:2 * n], 2), HD ** -0.5, bc(mask, 2),
                                MUL, ADD))
                    run(dve.tensor_reduce(small[:, 32 + 4 * b:36 + 4 * b], s, AX, MAX, negate=True))
                s = w(18944, 4, NC)
                at, _ = CONSTS["cmp_add"]
                for r in range(2):
                    run(stt(s[:, 2 * r:2 * r + 2, :], grid(bank(4 + r)[:, 0:2 * NC], 2), HD ** -0.5,
                            bc(consts[:, at + a * NC:at + a * NC + NC], 2), MUL, ADD))
                run(dve.tensor_reduce(small[:, 40:44], s, AX, MAX, negate=True), AT_V, "masked", u)
                dve.wait_ge(AT_A.sem, AT_A.at("exps", u))
                run(dve.reciprocal(small[:, 48:60], small[:, 48:60]))
                ga = w(GA + 48 * a, 3, 16)[:, :, 4 * g:4 * g + 4].rearrange("p c (t r) -> p c r t", t=2)
                for b, c in ((0, 1), (1, 2), (2, 0)):
                    wt = grid(small[:, 48 + 4 * b:52 + 4 * b], 2)
                    run(tt(wt, wt, ga[:, c, :, :], MUL))
                at, _ = CONSTS["cmp_keep"]
                run(tt(s, s, bc(consts[:, at + a * NC:at + a * NC + NC], 4), MUL))
                run(tt(s, s, small[:, 56:60].unsqueeze(2).to_broadcast([P, 4, NC]), MUL))
                for b in range(2):
                    s = w(16896 + 1024 * b, 4, n)
                    ins = tt(s, s, small[:, 48 + 4 * b:52 + 4 * b].unsqueeze(2).to_broadcast([P, 4, n]), MUL)
                    if b:
                        run(ins, AT_V, "probs", u)
                    else:
                        run(ins)

            for l in range(2):
                norm(2 * l, f"norm_mix{l}")
                rwkv_front(l)
                for n in range(LEVELS):
                    rwkv_level(l, n)
                rwkv_back(l)
                stick(l)
                retention(l)
                conv(l)
                merge(l)
                project(l)
                norm(2 * l + 1, f"norm_ffn{l}")
                if l == 0:
                    ffn_split("dense")
                else:
                    route()
                    with dve.If(dve.value_load(crowded[0:1, 0:1], min_val=0, max_val=1) == 0):
                        experts_short()
                    with dve.Else():
                        ffn("moe", router_gates)
            norm(4, "a_norm")
            lru()
            project(2)
            norm(5, "f_norm0")
            ffn_split("f0")
            norm(6, "kv_norm")
            kv()
            kv_cmp()
            keys()
            norm(7, "b_norm")
            queries()
            for u in range(2 * G):
                attend(u)
            project(3)
            norm(8, "f_norm1")
            ffn_split("f1")


def kernel(**inputs):
    import concourse.bacc as bacc
    from concourse.bass_utils import run_bass_kernel_spmd

    a = {name: np.asarray(v) for name, v in inputs.items()}
    arrays = {"weights_in": weight_stream(a), "consts_in": constant_arrays(), "params_in": parameter_array(a),
              "x_in": np.ascontiguousarray(a["x"])}
    nc = bacc.Bacc("TRN2", target_bir_lowering=False, num_devices=1)
    aps = [nc.dram_tensor(name, v.shape, F32, kind="ExternalInput").ap() for name, v in arrays.items()]
    out = nc.dram_tensor("out", (1, T, D), F32, kind="ExternalOutput").ap()
    build(nc, *aps, out)
    return run_bass_kernel_spmd(nc, [arrays], core_ids=[0]).results[0]["out"]
```

```python
from contextlib import ExitStack

import numpy as np

import concourse.bass as bass
from concourse import mybir

F32 = mybir.dt.float32
F32R = mybir.dt.float32r
I32 = mybir.dt.int32
U32 = mybir.dt.uint32
ALU = mybir.AluOpType
ACT = mybir.ActivationFunctionType
AX = mybir.AxisListType.X

P = 128
T = 256
TT = T // P
D = 1024
KT = D // P
HD = 64
NH = 4
NHQ = 16
G = 4
LORA = 64
DECAY_SCALE = 0.606531
SHIFT = DECAY_SCALE * P / 2
EPS = 1e-6
RW_EPS = 64e-5
LN_EPS = 1e-5
TAPS = 31
TAPS2 = 4
NE = 8
FE = 1408
FT = FE // P
CAP = 96
LRU_C = 8.0
CB, CS = 32, 16
NC = (T - CB) // CS + 1
HID = 256
NEG = -1e30
LEVELS = 7
SIDE = ("sb_squares", "sb_scores0", "sb_scores1", "sb_suffix0", "sb_suffix1", "ret_rotated", "sb_out",
        "ret_scores0", "ret_scores1", "ret_out", "ret_mean", "ret_var", "conv_mean", "conv_var")
assert len(SIDE) == 2 * LEVELS
BRANCH_BANK = (6, 7, 0, 1)
BRANCH_ORDER = (1, 2, 3, 0)

SLAB = 4096
RING = 3
IN_SLABS, OUT_SLABS = 6, 3
EXPERT_SLABS = IN_SLABS + OUT_SLABS
HALF_SLAB = SLAB // 2
OUT_UNIT = 2 * IN_SLABS
OUT_UNITS = 2 * OUT_SLABS
UNITS = [*range(FT), *range(OUT_UNIT, OUT_UNIT + OUT_UNITS)]
SPLIT_BUFS = 3
PART_COLS = [SLAB] * EXPERT_SLABS
PART_COLS[IN_SLABS - 1] = (FT - 2 * (IN_SLABS - 1)) * HALF_SLAB
PART_COLS[-1] = (FT - 4 * (OUT_SLABS - 1)) * D
assert 2 * EXPERT_SLABS % SPLIT_BUFS == 0


def columns(widths):
    place, at = {}, 0
    for name, n in widths:
        place[name] = (at, n)
        at += n
    return place, at


CONSTS, N_CONSTS = columns([
    ("ident", P), ("head_sum", P), ("head_mean", P), ("ones", P), ("strict", P), ("causal", P),
    ("suffix", P), ("levels", LEVELS * P), ("swap", P), ("cos", T), ("sin", T), ("cos_cmp", NC),
    ("sin_cmp", NC), ("decay", NH * T), ("not_before", P), ("causal_add", T + P), ("cmp_add", TT * NC),
    ("cmp_keep", TT * NC), ("experts", NE), ("slots", CAP), ("rms_eps", 1), ("rw_eps", 1), ("ln_eps", 1),
    ("shift", 1), ("minus_shift", 1), ("one", 1)])

LAYER_COLS = [
    ("norm_mix", KT), ("norm_ffn", KT), ("mu", KT), ("w0", 2), ("a0", 2), ("k_k", 2), ("k_a", 2),
    ("r_k", 2), ("ln_w", 2), ("ln_b", 2), ("sb_q", 1), ("sb_k", 1), ("gn", 2), ("dw", 2 * TAPS),
    ("db", 2), ("cln_w", 2), ("cln_b", 2), ("w2a2", 2 * P), ("g2", 2 * P)]
PARAMS, N_PARAMS = columns(
    [(f"{name}{l}", n) for l in range(2) for name, n in LAYER_COLS] + [
        ("router", KT * NE), ("a_norm", KT), ("a_conv_w", KT * TAPS2), ("a_conv_b", KT),
        ("a_gate_b", 2 * KT), ("a_lambda", KT), ("kv_norm", KT), ("k_norm", 3), ("cmp_pos", 2 * CB // 2),
        ("cmp_b1", 4), ("cmp_b2k", 1), ("cmp_b2v", HD), ("cmp_w2k", 2 * P), ("cmp_w2v", 2 * HD),
        ("b_norm", KT), ("gate_w", KT * 48), ("gate_b", 48), ("q_norm", 1), ("f_norm0", KT), ("f_norm1", KT)])


def constant_arrays():
    c = np.zeros((P, N_CONSTS), np.float32)

    def put(name, a):
        at, n = CONSTS[name]
        c[:, at:at + n] = np.asarray(a, np.float32).reshape(P, n)

    i = np.arange(P)
    row, col = i[:, None], i[None, :]
    same_head = (row // HD == col // HD).astype(np.float32)
    put("ident", np.eye(P))
    put("head_sum", same_head)
    put("head_mean", same_head / HD)
    put("ones", np.ones((P, P)))
    put("strict", row < col)
    put("causal", row <= col)
    put("suffix", row >= col)
    levels = []
    for n in range(LEVELS):
        b = 1 << n
        levels.append((row < col) & (row // (2 * b) == col // (2 * b)) & (row // b != col // b))
    put("levels", np.stack(levels, 1))
    swap = np.zeros((P, P), np.float32)
    for m in range(P):
        d = m % HD
        if d < HD // 2:
            swap[m + HD // 2, m] = -1.0
        else:
            swap[m - HD // 2, m] = 1.0
    put("swap", swap)
    freq = np.float32(10000.0) ** (-np.arange(0, HD, 2, dtype=np.float32) / np.float32(HD))
    freq = freq[i % (HD // 2)].astype(np.float32)[:, None]
    pos = np.arange(T, dtype=np.float32)[None, :]
    cmp_last = np.arange(NC) * CS + CB - 1
    put("cos", np.cos(pos * freq))
    put("sin", np.sin(pos * freq))
    put("cos_cmp", np.cos(cmp_last.astype(np.float32)[None, :] * freq))
    put("sin_cmp", np.sin(cmp_last.astype(np.float32)[None, :] * freq))
    gamma = np.log(1.0 - 2.0 ** (-5.0 - np.arange(NH)))
    rel = np.arange(T)[None, None, :] - i[:, None, None]
    decay = np.where(rel >= 0, np.exp(np.maximum(rel, 0) * gamma[None, :, None]) * HD ** -0.5, 0.0)
    put("decay", decay[:, [0, 2, 1, 3]])
    put("not_before", np.where(row < col, 0.0, NEG))
    put("causal_add", np.concatenate([np.zeros((P, P)), np.where(col <= row, 0.0, NEG), np.zeros((P, P))], 1))
    t = i[:, None, None] + P * np.arange(TT)[None, :, None]
    seen = cmp_last[None, None, :] <= t
    put("cmp_add", np.where(seen, 0.0, NEG))
    put("cmp_keep", seen)
    put("experts", np.broadcast_to(np.arange(NE), (P, NE)))
    put("slots", np.broadcast_to(np.arange(CAP), (P, CAP)))
    for name, value in (("rms_eps", EPS), ("rw_eps", RW_EPS), ("ln_eps", LN_EPS), ("shift", SHIFT),
                        ("minus_shift", -SHIFT), ("one", 1.0)):
        put(name, np.full((P, 1), value))
    return c


def parameter_array(a):
    c = np.zeros((P, N_PARAMS), np.float32)

    def put(name, v, rows=slice(0, P)):
        at, n = PARAMS[name]
        c[rows, at:at + n] = v

    def column(v):
        return v.reshape(-1, P).T

    for l in range(2):
        for name, key in (("norm_mix", "norm_mix"), ("norm_ffn", "norm_ffn"), ("mu", "rw_mu"), ("w0", "rw_w0"),
                          ("a0", "rw_a0"), ("k_k", "rw_k_k"), ("k_a", "rw_k_a"), ("ln_w", "rw_ln_w"),
                          ("ln_b", "rw_ln_b"), ("gn", "ret_gn"), ("db", "conv_b"), ("cln_w", "conv_ln_w"),
                          ("cln_b", "conv_ln_b")):
            put(f"{name}{l}", column(a[key][l]))
        put(f"r_k{l}", column(a["rw_r_k"][l].reshape(-1)))
        put(f"sb_q{l}", np.concatenate([a["sb_q_norm"][l]] * 2)[:, None])
        put(f"sb_k{l}", np.concatenate([a["sb_k_norm"][l]] * 2)[:, None])
        put(f"dw{l}", a["conv_dw"][l].reshape(TAPS, 2, P).transpose(2, 1, 0).reshape(P, -1))
        put(f"w2a2{l}", np.concatenate([a["rw_w2"][l], a["rw_a2"][l]], 0))
        put(f"g2{l}", a["rw_g2"][l])
    put("router", a["router"][0].reshape(KT, P, NE).transpose(1, 0, 2).reshape(P, -1))
    put("a_norm", column(a["a_norm_2"][0]))
    put("a_conv_w", a["a_conv_w_2"][0].reshape(TAPS2, KT, P).transpose(2, 1, 0).reshape(P, -1))
    put("a_conv_b", column(a["a_conv_b_2"][0]))
    put("a_gate_b", column(a["a_gate_b_2"][0].reshape(-1)))
    put("a_lambda", column(a["a_lambda_2"][0]))
    put("kv_norm", column(a["kv_norm_2"]))
    put("k_norm", np.concatenate([a["k_norm_2"]] * 2, 1).T)
    put("cmp_pos", a["cmp_pos_2"].reshape(2, CB // 2, 2 * HD).transpose(2, 0, 1).reshape(P, -1))
    put("cmp_b1", column(a["cmp_b1_2"].reshape(-1)))
    put("cmp_b2k", np.concatenate([a["cmp_b2_2"][0]] * 2)[:, None])
    put("cmp_b2v", a["cmp_b2_2"][1][None, :], slice(0, 1))
    w2 = a["cmp_w2_2"].reshape(2, 2, P, HD)
    put("cmp_w2k", np.concatenate([w2[0]] * 2, 2).transpose(1, 0, 2).reshape(P, -1))
    put("cmp_w2v", w2[1].transpose(1, 0, 2).reshape(P, -1))
    put("b_norm", column(a["b_norm_2"][0]))
    put("gate_w", a["b_w_in_2"][0][:, D:].reshape(KT, P, 48).transpose(1, 0, 2).reshape(P, -1))
    put("gate_b", a["b_gate_b_2"][0][None, :], slice(0, 1))
    put("q_norm", np.concatenate([a["q_norm_2"][0]] * 2)[:, None])
    put("f_norm0", column(a["f_norm_2"][0]))
    put("f_norm1", column(a["f_norm_2"][1]))
    return c


def weight_stream(a):
    slabs = []

    def add(w):
        w = w.reshape(P, -1)
        slab = np.zeros((P, SLAB), np.float32)
        slab[:, :w.shape[1]] = w
        slabs.append(slab)

    def rows(w):
        return w.reshape(-1, P, w.shape[-1]).transpose(1, 0, 2)

    def wide(w):
        for n in range(0, w.shape[1], 512):
            cut = w[:, n:n + 512]
            if cut.shape[1] < 512:
                cut = np.concatenate([cut, np.zeros((cut.shape[0], 512 - cut.shape[1]), np.float32)], 1)
            add(rows(cut))

    def expert(w1, w3, w2):
        for f in range(0, FE, 2 * P):
            pad = np.zeros((D, max(0, f + 2 * P - FE)), np.float32)
            cut = rows(np.concatenate([w1[:, f:f + 2 * P], pad, w3[:, f:f + 2 * P], pad], 1))
            add(cut.reshape(P, KT, 2, 2, P).transpose(0, 3, 1, 2, 4))
        for f in range(0, FE, 4 * P):
            add(rows(w2[f:f + 4 * P]))

    for l in range(2):
        w = a["w_in"][l]
        rw, sb, ret = 1024, 1792, 2816
        order = [w[:, 0:rw], w[:, rw:rw + 512], w[:, sb:sb + 512],
                 w[:, rw + 512:sb], w[:, sb + 512:sb + 768], w[:, sb + 768:ret], w[:, ret:]]
        wide(np.concatenate(order, 1))
        for i in range(4):
            wide(a["w_gate"][l, i])
        for i in range(0, 4, 2):
            add(rows(np.concatenate([a["w_branch"][l, b] for b in BRANCH_ORDER[i:i + 2]])))
        wide(a["w_out"][l])
        if l == 0:
            for h in range(2):
                s = slice(h * FE, h * FE + FE)
                expert(a["ffn_w1"][0][:, s], a["ffn_w3"][0][:, s], a["ffn_w2"][0][s])
        else:
            for e in range(NE):
                expert(a["moe_w1"][0, e], a["moe_w3"][0, e], a["moe_w2"][0, e])

    def ffn(l):
        for h in range(2):
            s = slice(h * FE, h * FE + FE)
            w = a["f_w_in_2"][l]
            expert(w[:, :2 * FE][:, s], w[:, 2 * FE:][:, s], a["f_w_out_2"][l][s])

    wide(a["a_w_in_2"][0])
    add(a["a_gate_w_2"][0].transpose(2, 0, 1, 3))
    wide(a["a_w_out_2"][0])
    ffn(0)
    kv = a["kv_w_2"]
    wide(np.concatenate([kv[:, 0:768], kv[:, 1024:1280], kv[:, 768:1024], kv[:, 1280:1536]], 1))
    wide(a["b_w_in_2"][0][:, :D // 2])
    for v in range(2):
        add(rows(a["cmp_w1_2"][v]))
    wide(a["b_w_in_2"][0][:, D // 2:D])
    wide(a["b_w_out_2"][0])
    ffn(1)
    return np.stack(slabs)


class Steps:

    def __init__(self, sem, *names):
        self.sem, self.names, self.count = sem, names, 0

    def at(self, name, rnd=0):
        return rnd * len(self.names) + self.names.index(name) + 1

    def mark(self, ins, name, rnd=0):
        self.count += 1
        assert self.count == self.at(name, rnd), (name, rnd, self.count)
        ins.then_inc(self.sem, 1)
        return self.count


class Chain:

    def __init__(self, eng, sem):
        self.eng, self.sem, self.count = eng, sem, 0

    def to(self, ins, sem, value):
        ins.then_inc(sem, 1)
        self.eng.wait_ge(sem, value)

    def run(self, ins, steps=None, name=None, rnd=0):
        if steps is None:
            self.count += 1
            ins.then_inc(self.sem, 1)
            self.eng.wait_ge(self.sem, self.count)
        else:
            self.eng.wait_ge(steps.sem, steps.mark(ins, name, rnd))


def build(nc, stream, consts_in, params_in, x_in, out):
    n_slabs = stream.shape[0]
    assert EXPERT_SLABS % RING == 0
    with ExitStack() as ctx:
        def sb(name, shape, dt=F32):
            return ctx.enter_context(nc.sbuf_tensor(name, shape, dt))

        def sem(name):
            return ctx.enter_context(nc.semaphore(name))

        x = sb("x", [P, TT, D])
        hT = sb("hT", [P, KT, T])
        scr = sb("scr", [P, 2048])
        ring = sb("ring", [P, RING, SLAB])
        consts = sb("consts", [P, N_CONSTS])
        params = sb("params", [P, N_PARAMS])
        small = sb("small", [P, 256])
        router_gates = sb("router_gates", [P, TT, NE])
        crowded = sb("crowded", [P, 1], I32)
        top_index = sb("top_index", [P, TT, 8], U32)
        glu = sb("glu", [P, 2, T])
        with ExitStack() as shared:
            def split_operand(name, shape, dt=F32R):
                return shared.enter_context(nc.sbuf_tensor(name, shape, dt))

            w_hi = split_operand("w_hi", [P, SPLIT_BUFS, HALF_SLAB])
            w_lo = split_operand("w_lo", [P, SPLIT_BUFS, HALF_SLAB])
            h_hi, h_lo = split_operand("h_hi", [P, KT, T]), split_operand("h_lo", [P, KT, T])
            g_hi, g_lo = split_operand("g_hi", [P, FT, T]), split_operand("g_lo", [P, FT, T])
            hidden = split_operand("hidden", [P, FT, T], F32)
        work = sb("work", [P, 27136])
        banks = ctx.enter_context(nc.psum_tensor("banks", [P, 8, 512], F32))

        def const(name, *index):
            at, n = CONSTS[name]
            return consts[:, at:at + n]

        def par(name, i=0, n=1, rows=slice(0, P)):
            at, _ = PARAMS[name]
            return params[rows, at + i:at + i + n]

        def w(at, *dims, rows=slice(0, P)):
            n = 1
            for d in dims:
                n *= d
            ap = work[rows, at:at + n]
            return ap if len(dims) == 1 else ap.rearrange(
                "p (a b) -> p a b" if len(dims) == 2 else "p (a b c) -> p a b c", **dict(zip("abc", dims)))

        def bank(b, n=1, rows=slice(0, P)):
            return banks[rows, b:b + n, :].rearrange("p a b -> p (a b)")

        def grid(ap, a):
            return ap.rearrange("p (a b) -> p a b", a=a)

        PAIR = 2 * T + 2 * P

        def diagonals(s):
            return grid(s[:, 0:2 * T], 2)[:, :, 0:P], grid(s[:, 2 * T:PAIR], 2)

        def matrix(h, c):
            return (h % 2) * 4 + 2 * c + h // 2

        def half(r):
            return slice(HD * r, HD * r + HD)

        PT, VT, BR, SIG, MATS, INV, MX = 0, 5632, 6656, 8704, 16896, 20992, 25088
        LEVEL_AT = MX + 1024
        Z_AT = (INV + 3072, MX)
        TAIL = SIG + 6144
        LN_AT = (TAIL, TAIL + PAIR)
        MERGED = SIG + 512 * 4 * BRANCH_ORDER[0]
        pT = w(PT, 22, T)
        vt = w(VT, TT, 512)
        br = w(BR, KT, T)
        sig = w(SIG, 4 * KT, T)

        sel = w(3072, TT, CAP)
        sel_gate = w(3264, TT, CAP)
        sel_turned = w(3456, TT * P, rows=slice(0, CAP))
        gathered = w(3712, KT, CAP)
        result = w(4480, D, rows=slice(0, CAP))
        chosen, slot, gate_of = (w(5504 + 32 * i, TT, 16) for i in range(3))

        KC, EXW, HIDN, KR, KD, VSW, QR, GA, KCM, VCM = 0, 2048, 3968, 4224, 6272, 8320, 9344, 11392, 11520, 11584
        HB, KSQ, QSQ = 12288, 14336, 16896
        Q_BANK = (6, 7, 4, 5)

        loaded = sem("loaded")
        landed = [sem(f"landed{i}") for i in range(RING)]
        slab_used = sem("slab_used")
        stored = sem("stored")
        v_chain, a_chain = sem("v_chain"), sem("a_chain")
        NORM_V = Steps(sem("norm_vector"), "diagonal", "hT")
        NORM_A = Steps(sem("norm_scalar"), "root", "hT")
        NORM_P = Steps(sem("norm_products"), "bank0", "bank1", "bank2", "bank3")
        win_full, win_out = sem("win_full"), sem("win_out")
        gate_full, gate_out = sem("gate_full"), sem("gate_out")
        br_full, br_out = sem("branch_full"), sem("branch_merged")
        RW_P = Steps(sem("rw_products"), "lora", "squares", "bonus", "mats0", "mats1",
                     *[f"{s}{n}" for n in range(LEVELS) for s in ("T", "X")],
                     "w0", "u0", "state", "w1", "u1", "y", "mean", "var")
        RW_V = Steps(sem("rw_vector"), "mixed", "k_squared", "decays", "operands", "bonus_used", "mats0", "mats1",
                     *[f"X{n}" for n in range(LEVELS)], "state", "y", "centred", "done")
        RW_A = Steps(sem("rw_scalar"), "lora", "sigmoids", "norm", "exps", "rows", *[f"T{n}" for n in range(LEVELS)],
                     "w0", "u0", "w1", "u1", "dev")
        RW_G = Steps(sem("rw_masks"), "zeroed", *[f"M{n}" for n in range(LEVELS)])
        SB_P = Steps(sem("sb_products"), "squares", "scores0", "scores1", "suffix0", "suffix1", "out")
        SB_V = Steps(sem("sb_vector"), "squares", "qk", "softplus0", "softplus1", "logs0", "logs1", "done")
        SB_A = Steps(sem("sb_scalar"), "norm", "scores0", "ln0", "scores1", "ln1", "weights0", "weights1")
        RET_P = Steps(sem("ret_products"), "rotated", "scores0", "scores1", "out", "mean", "var")
        RET_V = Steps(sem("ret_vector"), "qk", "scores0", "scores1", "y", "centred", "done")
        RET_A = Steps(sem("ret_scalar"), "silu", "dev")
        CV_P = Steps(sem("conv_products"), "mean", "var")
        CV_V = Steps(sem("conv_vector"), "conv", "centred", "affine")
        CV_A = Steps(sem("conv_scalar"), "sigmoid", "dev", "done")
        proj_full, proj_added = sem("proj_full"), sem("proj_added")
        glu_full, glu_silu, glu_done = sem("glu_full"), sem("glu_silu"), sem("glu_done")
        ffn_added = sem("ffn_added")
        input_half, input_hi, input_lo = sem("input_half"), sem("input_hi"), sem("input_lo")
        unit_hi, unit_lo = sem("unit_hi"), sem("unit_lo")
        hidden_hi, hidden_lo = sem("hidden_hi"), sem("hidden_lo")
        out_used = sem("out_used")
        RT_P = Steps(sem("router_products"), "logits", "slots")
        RT_V = Steps(sem("router_vector"), "gap", "chosen", "flag")
        sp_selected, sp_inputs, sp_gathered = sem("sp_selected"), sem("sp_inputs"), sem("sp_gathered")
        sp_result, sp_scattered, sp_added = sem("sp_result"), sem("sp_scattered"), sem("sp_added")
        sp_copied, sp_turned = sem("sp_copied"), sem("sp_turned")
        RT_A = Steps(sem("router_scalar"), "exp")
        ain_full, ain_out = sem("ain_full"), sem("ain_out")
        ag_full, ag_out = sem("lru_gate_full"), sem("lru_gate_out")
        lru_conv = sem("lru_conv")
        LR_V = Steps(sem("lru_vector"), "rate", "square0", "done0", "square1", "done1")
        LR_A = Steps(sem("lru_scalar"), "lambda", "exps0", "root0", "exps1", "root1")
        kv_full, kv_out = sem("kv_full"), sem("kv_out")
        KV_V = Steps(sem("kv_vector"), "windows", "k_squares", "k_normed", "k_rope", "cmp_squares", "cmp_normed",
                     "cmp_rope", "v_cmp")
        KV_P = Steps(sem("kv_products"), "k_mean", "k_rot", "hidden0", "hidden1", "k_cmp", "cmp_mean", "cmp_rot",
                     "v_cmp")
        KV_A = Steps(sem("kv_scalar"), "k_norm", "hidden0", "hidden1", "k_cmp", "k_copies", "cmp_norm")
        Q_P = Steps(sem("q_products"), "full0", "full1", "mean0", "full2", "rot0", "full3", "gates", "mean1", "rot1")
        Q_A = Steps(sem("q_scalar"), "out0", "out1", "norm0", "out2", "out3", "gates", "norm1")
        Q_V = Steps(sem("q_vector"), "input", "squares0", "normed0", "rope0", "squares1", "normed1", "rope1")
        at_scores, at_turned, at_out = sem("at_scores"), sem("at_turned"), sem("at_out")
        at_masked, at_probs = sem("at_masked"), sem("at_probs")
        at_exps, at_copied, at_stored = sem("at_exps"), sem("at_copied"), sem("at_stored")
        CA_P = Steps(sem("cmp_at_products"), "scores")
        CA_V = Steps(sem("cmp_at_vector"), "shifted", "probs")
        CA_A = Steps(sem("cmp_at_scalar"), "exps")

        FIRST_EXPERT = {"dense": 0, "moe": 2, "f0": 2 + NE, "f1": 4 + NE}
        MIX, REC, ATT = 7 + 8 + 2 + 2, 4 + 1 + 2, 3 + 2 + 2 + 2
        LAST_MOE_SLAB = 2 * MIX + 3 * EXPERT_SLABS
        FIRST_SLAB = {"dense": MIX, "f0": 2 * MIX + 10 * EXPERT_SLABS + REC,
                      "f1": 2 * MIX + 12 * EXPERT_SLABS + REC + ATT}
        SPLIT = {"dense": 0, "f0": 1, "f1": 2}
        SPLIT_NORMS = {1: "dense", 5: "f0", 7: "f1"}
        N_PARTS = {"dense": 2, "moe": NE, "f0": 2, "f1": 2}

        TASKS = [(g, a, b) for g in range(G) for a in range(TT) for b in range(2)]

        def at_s(k):
            return w(QSQ + 1024 * (k % 3), 4, P * (TASKS[k][1] + 1))

        def at_t(k):
            return w(1024 * (k % 4), 1024)

        def at_cmp_t(u):
            return w(24064 + 512 * (u % 2), 512, rows=slice(0, NC))

        CMP_S = 25088

        def unit_count(part, u):
            return part * len(UNITS) + UNITS.index(u) + 1

        def wait_unit_free(eng, name, h, u):
            before, part = u - SPLIT_BUFS, 2 * SPLIT[name] + h
            if before >= OUT_UNIT:
                eng.wait_ge(out_used, part * OUT_UNITS + before - OUT_UNIT + 1)
            elif before >= 0:
                eng.wait_ge(glu_full, (FIRST_EXPERT[name] + h) * FT + min(before, FT - 1) + 1)
            elif part:
                eng.wait_ge(out_used, part * OUT_UNITS + before + 1)

        def unit_cols(u):
            return D if u == UNITS[-1] and FT % 2 else HALF_SLAB

        def unit_of_ring(u, first):
            return ring[:, (first + u // 2) % RING, (u % 2) * HALF_SLAB:(u % 2) * HALF_SLAB + unit_cols(u)]

        block = ctx.enter_context(nc.Block())

        @block.sync
        def _(sp):
            sp.dma_start(x[:, :, :], x_in.rearrange("o (a p) d -> p (o a) d", p=P)).then_inc(loaded, 16)
            sp.dma_start(consts[:, :], consts_in).then_inc(loaded, 16)
            sp.dma_start(params[:, :], params_in).then_inc(loaded, 16)
            def load_slab(slot, n, cols=SLAB):
                sp.dma_start(ring[:, slot % RING, 0:cols], stream[n, :, 0:cols]).then_inc(landed[slot % RING], 16)

            def singles(first, last):
                for n in range(first, last):
                    if n >= RING:
                        sp.wait_ge(slab_used, n + 1 - RING)
                    load_slab(n, n)

            def parts(first, count):
                with sp.Fori(0, count) as e:
                    for j in range(EXPERT_SLABS):
                        sp.wait_ge(slab_used, e * EXPERT_SLABS + (first + j + 1 - RING))
                        load_slab(first + j, e * EXPERT_SLABS + (first + j), PART_COLS[j])
                return first + count * EXPERT_SLABS

            singles(0, MIX)
            n = parts(MIX, 2)
            singles(n, n + MIX)
            n = parts(n + MIX, NE)
            singles(n, n + REC)
            n = parts(n + REC, 2)
            singles(n, n + ATT)
            n = parts(n + ATT, 2)
            assert n == n_slabs
            sp.wait_ge(ffn_added, 4 * (FIRST_EXPERT["f1"] + 2) + 1)
            sp.dma_start(out.rearrange("o (a p) d -> p (o a) d", p=P), x[:, :, :]).then_inc(stored, 16)
            sp.wait_ge(stored, 16)

        @block.gpsimd
        def _(pool):
            def ffn_split(name):
                for h in range(2):
                    for t in range(FT):
                        pool.wait_ge(glu_done, (h + FIRST_EXPERT[name]) * FT + t + 2)
                        n = (h + 2 * SPLIT[name]) * FT + t + 1
                        pool.tensor_copy(g_hi[:, t, :], hidden[:, t, :]).then_inc(hidden_hi, 1)
                        pool.wait_ge(hidden_hi, n)
                        pool.tensor_tensor(g_lo[:, t, :], hidden[:, t, :], g_hi[:, t, :].bitcast(F32),
                                           ALU.subtract).then_inc(hidden_lo, 1)

            for l in range(2):
                if l:
                    pool.wait_ge(NORM_V.sem, NORM_V.at("diagonal", 2 * l))
                RW_G.mark(pool.memset(w(MATS, 4096), 0.0), "zeroed", l)
                pool.wait_ge(RW_V.sem, RW_V.at("mats1", l))
                for n in range(LEVELS):
                    if n:
                        pool.wait_ge(RW_P.sem, RW_P.at(f"T{n - 1}", l))
                    at, _ = CONSTS["levels"]
                    mask = consts[:, at + n * P:at + n * P + P].unsqueeze(1).to_broadcast([P, 8, P])
                    RW_G.mark(pool.tensor_tensor(w(LEVEL_AT, 8, P), w(MATS, 8, P), mask, ALU.mult),
                              f"M{n}", l)
                if l == 0:
                    ffn_split("dense")
            ffn_split("f0")
            ffn_split("f1")

        @block.scalar
        def _(act):
            chain = Chain(act, a_chain)
            run = chain.run

            def f(out_, in_, func, **kw):
                return act.activation(out_, in_, func, **kw)

            def norm(n):
                if n == 0:
                    act.wait_ge(loaded, 48)
                elif n in (1, 3):
                    act.wait_ge(proj_added, 2 * (n // 2 + 1))
                elif n == 5:
                    act.wait_ge(proj_added, 6)
                elif n == 7:
                    act.wait_ge(proj_added, 8)
                for a in range(TT):
                    if n in (2, 4, 6):
                        after = FIRST_EXPERT[{2: "moe", 4: "f0", 6: "f1"}[n]]
                        act.wait_ge(ffn_added, 4 * after + 1 - 2 * (TT - 1 - a))
                    run(f(scr[:, a * D:a * D + D], x[:, a, :], ACT.Square, accum_out=small[:, a:a + 1]))
                run(f(small[:, 2:4], small[:, 0:2], ACT.Sqrt, scale=1.0 / D, bias=const("rms_eps")), NORM_A, "root", n)

            def norm_out(n, gain):
                for b in (1, 3):
                    act.wait_ge(NORM_P.sem, NORM_P.at(f"bank{b}", n))
                    for k in (2 * b, 2 * b + 1):
                        ins = f(hT[:, k, :], bank(b)[:, (k % 2) * T:(k % 2) * T + T], ACT.Copy, scale=par(gain, k))
                    if b == 3:
                        run(ins, NORM_A, "hT", n)
                    else:
                        run(ins)
                    if n in SPLIT_NORMS:
                        split_input(n, b // 2)

            def win(l, halves):
                for q in halves:
                    act.wait_ge(win_full, 13 * l + q + 1)
                    src = banks[:, 6 + q % 2, :]
                    if q < 8:
                        dst = w(PT + 512 * q, 512)
                    elif q < 10:
                        dst = vt[:, q - 8, :]
                    else:
                        dst = w(PT + 512 * (q - 2), 512)
                    chain.to(f(dst, src, ACT.Copy), win_out, 13 * l + q + 1)

            def gate(l, n):
                act.wait_ge(gate_full, 16 * l + n + 1)
                f(w(SIG + 512 * n, 512), banks[:, 6 + n % 2, :], ACT.Sigmoid).then_inc(gate_out, 1)

            def rw_lora(l):
                act.wait_ge(RW_V.sem, RW_V.at("mixed", l))
                run(f(w(INV + 3584, T, rows=half(0)), w(MX + 6 * T, T, rows=half(0)), ACT.Tanh))
                run(f(w(INV + 3840, T), w(MX + 7 * T, T), ACT.Sigmoid), RW_A, "lora", l)

            def rw_sigmoids(l):
                act.wait_ge(RW_P.sem, RW_P.at("lora", l))
                for j in range(2):
                    run(f(w(INV + 1536 + j * T, T), bank(0)[:, j * T:j * T + T], ACT.Sigmoid, bias=par(f"w0{l}", j)))
                    run(f(w(MX + (6 + j) * T, T), bank(1)[:, j * T:j * T + T], ACT.Sigmoid, bias=par(f"a0{l}", j)))
                run(f(scr[:, 0:512], bank(2), ACT.Copy), RW_A, "sigmoids", l)
                act.wait_ge(RW_P.sem, RW_P.at("squares", l))
                run(f(w(INV + 1024, 512), bank(3), ACT.Sqrt), RW_A, "norm", l)

            def rw_exps(l):
                act.wait_ge(RW_V.sem, RW_V.at("decays", l))
                run(f(w(PT, 512), w(INV + 2560, 512), ACT.Exp, bias=const("shift")))
                run(f(w(INV + 3072, 512), w(INV + 2048, 512), ACT.Exp, scale=-1.0, bias=const("minus_shift")))
                run(f(w(PT + 1536, 512), w(INV + 2048, 512), ACT.Exp, bias=const("shift")))
                run(f(small[:, 8:10], w(INV + 2048, 2, T)[:, :, P - 1], ACT.Exp), RW_A, "exps", l)

            def rw_rows(l):
                act.wait_ge(RW_P.sem, RW_P.at("bonus", l))
                run(f(scr[:, 1024:2048], bank(4, 2), ACT.Copy), RW_A, "rows", l)

            def rw_turned(l, n):
                act.wait_ge(RW_P.sem, RW_P.at(f"T{n}", l))
                run(f(w(INV + 2048, 1024), bank(0, 2), ACT.Copy), RW_A, f"T{n}", l)

            def rw_back(l, name):
                act.wait_ge(RW_P.sem, RW_P.at(name, l))
                if name[0] == "w":
                    run(f(w(MX, 2, P), grid(bank(0, 2), 2)[:, :, 0:P], ACT.Copy), RW_A, name, l)
                else:
                    run(f(w(MX + 256 + 256 * int(name[1]), 256), bank(2)[:, 0:256], ACT.Copy), RW_A, name, l)

            def rw_dev(l):
                act.wait_ge(RW_P.sem, RW_P.at("var", l))
                run(f(w(INV + 1536, 512), bank(5), ACT.Sqrt, bias=const("rw_eps")), RW_A, "dev", l)

            def side(l, name):
                if name == "sb_squares":
                    act.wait_ge(SB_P.sem, SB_P.at("squares", l))
                    run(f(w(TAIL, 1024), bank(4, 2), ACT.Sqrt, bias=const("rms_eps")), SB_A, "norm", l)
                elif name[:-1] == "sb_scores":
                    r = int(name[-1])
                    z, ln = w(Z_AT[r], PAIR), w(LN_AT[r], PAIR)
                    act.wait_ge(SB_P.sem, SB_P.at(f"scores{r}", l))
                    run(f(z, bank(4, 2)[:, 0:PAIR], ACT.Copy), SB_A, f"scores{r}", l)
                    run(f(ln, z, ACT.Abs))
                    run(f(ln, ln, ACT.Exp, scale=-1.0))
                    run(f(ln, ln, ACT.Ln, bias=const("one")), SB_A, f"ln{r}", l)
                elif name[:-1] == "sb_suffix":
                    r = int(name[-1])
                    act.wait_ge(SB_V.sem, SB_V.at(f"logs{r}", l))
                    run(f(w(Z_AT[r], PAIR), w(Z_AT[r], PAIR), ACT.Exp), SB_A, f"weights{r}", l)
                elif name == "ret_scores0":
                    run(f(w(PT + 16 * T, 512), w(PT + 16 * T, 512), ACT.Silu), RET_A, "silu", l)
                elif name == "ret_var":
                    act.wait_ge(RET_P.sem, RET_P.at("var", l))
                    run(f(w(INV + 3072, 512), bank(4), ACT.Sqrt, bias=const("ln_eps")), RET_A, "dev", l)
                elif name == "conv_var":
                    act.wait_ge(CV_P.sem, CV_P.at("var", l))
                    run(f(w(INV + 3072, T), bank(4)[:, 0:T], ACT.Sqrt, bias=const("ln_eps")), CV_A, "dev", l)
                    act.wait_ge(CV_V.sem, CV_V.at("affine", l))
                    run(f(w(BR + 6 * T, 512), w(PT + 20 * T, 512), ACT.Silu), CV_A, "done", l)

            def mixers(l):
                win(l, range(4))
                rw_lora(l)
                win(l, (4, 5))
                rw_sigmoids(l)
                win(l, (6,))
                rw_exps(l)
                win(l, (7, 8))
                rw_rows(l)
                win(l, range(9, 13))
                run(f(w(PT + 20 * T, 512), w(PT + 20 * T, 512), ACT.Sigmoid), CV_A, "sigmoid", l)
                for n in range(LEVELS):
                    rw_turned(l, n)
                    side(l, SIDE[2 * n])
                    gate(l, 2 * n)
                    side(l, SIDE[2 * n + 1])
                    gate(l, 2 * n + 1)
                rw_back(l, "w0")
                rw_back(l, "u0")
                gate(l, 14)
                rw_back(l, "w1")
                gate(l, 15)
                rw_back(l, "u1")
                rw_dev(l)

            def split_unit(name, h, u):
                first = FIRST_SLAB[name] + h * EXPERT_SLABS
                n = first + u // 2
                act.wait_ge(landed[n % RING], 16 * (n // RING + 1))
                wait_unit_free(act, name, h, u)
                f(w_hi[:, u % SPLIT_BUFS, 0:unit_cols(u)], unit_of_ring(u, first), ACT.Copy).then_inc(unit_hi, 1)

            def split_input(n, i):
                if i:
                    act.wait_ge(NORM_V.sem, NORM_V.at("hT", n))
                else:
                    act.wait_ge(input_half, SPLIT[SPLIT_NORMS[n]] + 1)
                f(h_hi[:, 4 * i:4 * i + 4, :], hT[:, 4 * i:4 * i + 4, :], ACT.Copy).then_inc(input_hi, 1)

            def ffn_split(name, n, gain):
                for u in UNITS[:2]:
                    split_unit(name, 0, u)
                norm_out(n, gain)
                split_unit(name, 0, UNITS[2])
                for h in range(2):
                    for t in range(FT):
                        act.wait_ge(glu_full, (h + FIRST_EXPERT[name]) * FT + t + 1)
                        act.wait_ge(glu_done, (h + FIRST_EXPERT[name]) * FT + t)
                        f(glu[:, t % 2, :], banks[:, 4 + t % 4, 0:T], ACT.Silu).then_inc(glu_silu, 1)
                        split_unit(name, h, UNITS[t + 3])
                    for u in UNITS[FT + 3:]:
                        split_unit(name, h, u)
                    if h == 0:
                        for u in UNITS[:3]:
                            split_unit(name, 1, u)

            def ffn(name):
                first = FIRST_EXPERT[name]
                with act.Fori(0, N_PARTS[name]) as e:
                    for t in range(FT):
                        act.wait_ge(glu_full, (e + first) * FT + t + 1)
                        act.wait_ge(glu_done, (e + first) * FT + (t if t >= 2 else 1))
                        f(glu[:, t % 2, :], banks[:, 4 + t % 4, 0:T], ACT.Silu).then_inc(glu_silu, 1)

            def experts_short():
                first = FIRST_EXPERT["moe"]
                with act.Fori(0, NE) as e:
                    for t in range(FT):
                        act.wait_ge(glu_full, (e + first) * FT + t + 1)
                        act.wait_ge(glu_done, (e + first) * FT + (t if t >= 2 else 1))
                        f(glu[:, t % 2, 0:CAP], banks[:, 6 + t % 2, 0:CAP], ACT.Silu).then_inc(glu_silu, 1)
                    act.wait_ge(sp_inputs, e + 2)
                    act.wait_ge(sp_scattered, e + 1)
                    f(grid(sel_turned, 2), banks[0:CAP, 4:6, 384:512], ACT.Copy).then_inc(sp_turned, 1)
                    act.wait_ge(sp_result, e + 1)
                    f(result, bank(0, 2, rows=slice(0, CAP)), ACT.Copy).then_inc(sp_copied, 1)

            def lru():
                run(f(small[:, 16:24], par("a_lambda", 0, KT), ACT.Abs))
                run(f(small[:, 16:24], small[:, 16:24], ACT.Exp, scale=-1.0), LR_A, "lambda")
                for q in range(8):
                    act.wait_ge(ain_full, q + 1)
                    src = banks[:, 4 + q % 4, :]
                    if q < 4:
                        ins = f(w(512 * q, 512), src, ACT.Gelu_apprx_tanh)
                    else:
                        dst = w(2048, KT, T + 4)[:, 2 * (q - 4):2 * (q - 4) + 2, 3:3 + T]
                        ins = f(dst, grid(src, 2), ACT.Copy)
                    chain.to(ins, ain_out, q + 1)
                act.wait_ge(LR_V.sem, LR_V.at("rate"))
                for i in range(2):
                    heads = range(4 * i, 4 * i + 4)
                    for h in heads:
                        act.wait_ge(ag_full, h + 1)
                        src = banks[:, 4 + h % 4, :]
                        f(w(8192 + h * T, T), src[:, 0:T], ACT.Sigmoid, bias=par("a_gate_b", h))
                        chain.to(f(w(10240 + h * T, T), src[:, T:2 * T], ACT.Sigmoid, bias=par("a_gate_b", KT + h)),
                                 ag_out, h + 1)
                    for h in heads:
                        r = w(8192 + h * T, T)
                        f(w(12288 + h * T, T), r, ACT.Exp, scale=small[:, 48 + h:49 + h])
                        ins = f(w(14336 + h * T, T), r, ACT.Tanh, scale=small[:, 56 + h:57 + h])
                    run(ins, LR_A, f"exps{i}")
                    lru_root(i)

            def lru_root(i):
                act.wait_ge(LR_V.sem, LR_V.at(f"square{i}"))
                v = w(14336 + 1024 * i, 1024)
                run(f(v, v, ACT.Sqrt), LR_A, f"root{i}")

            def keys_and_queries():
                for n in range(2):
                    act.wait_ge(kv_full, n + 1)
                    src = grid(banks[:, 4 + n, :], 2)
                    dst = w(KC + 1024 * n, G, T)
                    for r in range(2):
                        f(dst[0:HD, r::2, :], src[half(r), :, :], ACT.Copy)
                        ins = f(dst[HD:P, r::2, 0:T - 1], src[half(r), :, 1:T], ACT.Copy)
                    chain.to(ins, kv_out, n + 1)
                for n in range(2):
                    act.wait_ge(kv_full, n + 3)
                    chain.to(f(w(KR + 512 * n, 512), banks[:, 6 + n, :], ACT.Copy), kv_out, n + 3)
                for n in range(2):
                    act.wait_ge(kv_full, n + 5)
                    chain.to(f(w(VSW + 512 * n, 512), banks[:, 4 + n, :], ACT.Copy), kv_out, n + 5)
                act.wait_ge(KV_P.sem, KV_P.at("k_mean"))
                run(f(w(KSQ, 1024), bank(2, 2), ACT.Sqrt, bias=const("rms_eps")), KV_A, "k_norm")
                query(0)
                query(1)
                hidden_layer(0)
                query_norm(0)
                hidden_layer(1)
                query(2)
                act.wait_ge(KV_P.sem, KV_P.at("k_cmp"))
                run(f(w(KCM, G * NC), bank(2)[:, 0:G * NC], ACT.Identity, bias=par("cmp_b2k")), KV_A, "k_cmp")
                act.wait_ge(KV_V.sem, KV_V.at("k_rope"))
                for b in range(2):
                    for d in range(2):
                        for r in range(2):
                            ins = f(w(KD + 1024 * b, G, T)[half(d), r::2, :], w(KR + 512 * b, 2, T)[half(r), :, :], ACT.Copy)
                run(ins, KV_A, "k_copies")
                query(3)
                act.wait_ge(KV_P.sem, KV_P.at("cmp_mean"))
                run(f(w(EXW, G * NC), bank(3)[:, 0:G * NC], ACT.Sqrt, bias=const("rms_eps")), KV_A, "cmp_norm")
                act.wait_ge(Q_P.sem, Q_P.at("gates"))
                run(f(w(GA, 96), bank(0)[:, 0:96], ACT.Sigmoid), Q_A, "gates")
                query_norm(1)

            def hidden_layer(v):
                act.wait_ge(KV_P.sem, KV_P.at(f"hidden{v}"))
                for m in range(2):
                    ins = f(w(HIDN + 128 * v + 64 * m, G * NC), bank(v)[:, 64 * m:64 * m + G * NC],
                            ACT.Gelu_apprx_tanh, bias=par("cmp_b1", 2 * v + m))
                run(ins, KV_A, f"hidden{v}")

            def query(q):
                act.wait_ge(Q_P.sem, Q_P.at(f"full{q}"))
                run(f(w(QR + 512 * q, 512), banks[:, Q_BANK[q], :], ACT.Copy), Q_A, f"out{q}")

            def query_norm(i):
                act.wait_ge(Q_P.sem, Q_P.at(f"mean{i}"))
                run(f(w(QSQ + 1024 * i, 1024), bank(Q_BANK[2 * i], 2), ACT.Sqrt, bias=const("rms_eps")), Q_A, f"norm{i}")

            def at_exp(k):
                act.wait_ge(at_masked, k + 1)
                for h in range(4):
                    s = at_s(k)[:, h, :]
                    c = 4 * (k % 3) + h
                    ins = f(s, s, ACT.Exp, bias=small[:, 32 + c:33 + c], accum_out=small[:, 48 + c:49 + c])
                ins.then_inc(at_exps, 1)

            def at_copy(k):
                g, a, b = TASKS[k]
                act.wait_ge(at_turned, k + 1)
                if k >= 4:
                    act.wait_ge(at_out, k // 2 - 1)
                n = 4 * P * (a + 1)
                if b == 0:
                    f(at_cmp_t(k // 2), bank(7, rows=slice(0, NC)), ACT.Copy)
                f(at_t(k)[:, 0:n], bank(4, 2)[:, 0:n], ACT.Copy).then_inc(at_copied, 1)

            def at_store(u):
                g, a = u // TT, u % TT
                act.wait_ge(at_out, u + 1)
                f(w(22016, KT, T)[:, 2 * g:2 * g + 2, a * P:a * P + P], grid(bank(6)[:, 0:2 * P], 2),
                  ACT.Copy).then_inc(at_stored, 1)

            def attention():
                at_exp(0)
                act.wait_ge(CA_V.sem, CA_V.at("shifted"))
                run(f(w(CMP_S, 480), w(CMP_S, 480), ACT.Exp), CA_A, "exps")
                for k in range(len(TASKS)):
                    if k + 1 < len(TASKS):
                        at_exp(k + 1)
                    at_copy(k)
                    if k % 2 == 0 and k:
                        at_store(k // 2 - 1)
                at_store(2 * G - 1)

            for l in range(2):
                norm(2 * l)
                norm_out(2 * l, f"norm_mix{l}")
                mixers(l)
                norm(2 * l + 1)
                if l == 0:
                    ffn_split("dense", 1, "norm_ffn0")
                else:
                    norm_out(3, "norm_ffn1")
                    act.wait_ge(RT_V.sem, RT_V.at("gap"))
                    run(f(small[:, 4:6], small[:, 6:8], ACT.Exp), RT_A, "exp")
                    act.wait_ge(RT_V.sem, RT_V.at("flag"))
                    with act.If(act.value_load(crowded[0:1, 0:1], min_val=0, max_val=1) == 0):
                        experts_short()
                    with act.Else():
                        ffn("moe")
            norm(4)
            norm_out(4, "a_norm")
            lru()
            norm(5)
            ffn_split("f0", 5, "f_norm0")
            norm(6)
            norm_out(6, "kv_norm")
            keys_and_queries()
            attention()
            norm(7)
            ffn_split("f1", 7, "f_norm1")

        @block.tensor
        def _(pe):
            slab = [0]
            current = [None]

            def take(n=None):
                n = slab[0]
                pe.wait_ge(landed[n % RING], 16 * (n // RING + 1))
                slab[0] += 1
                return ring[:, n % RING, :]

            def mm(out_, lhsT, rhs, start=True, stop=True, **kw):
                return pe.matmul(out_, lhsT, rhs, start=start, stop=stop, **kw)

            pending = []

            def used(full, value):
                pending.append((full, value))

            def release():
                while pending:
                    pe.wait_ge(*pending.pop())
                    pe.sem_inc(slab_used, 1)

            def feature_tile(out_, cols, src=hT):
                for k in range(KT):
                    ins = mm(out_, cols(k), src[:, k, :], k == 0, k == KT - 1)
                return ins

            def norm(n):
                pe.wait_ge(NORM_V.sem, NORM_V.at("diagonal", n))
                for k in range(KT):
                    for a in range(TT):
                        at = (k % 2) * T + a * P
                        ins = mm(bank(k // 2)[:, at:at + P], x[:, a, k * P:k * P + P], glu[:, a, 0:P])
                    if k % 2:
                        NORM_P.mark(ins, f"bank{k // 2}", n)
                pe.wait_ge(NORM_V.sem, NORM_V.at("hT", n))
                pe.wait_ge(NORM_A.sem, NORM_A.at("hT", n))

            def two_tiles(s, q, out_, src=hT):
                for j in range(2):
                    c = (2 * q + j) * P
                    ins = feature_tile(out_[:, j * T:j * T + T], lambda k: s[:, k * 512 + c:k * 512 + c + P], src)
                return ins

            def token_tile(s, a, out_, lhs):
                for k in range(KT):
                    ins = mm(out_, lhs[:, k, a * P:a * P + P], s[:, k * 512:k * 512 + 512], k == 0, k == KT - 1)
                return ins

            def fill(s, q, full, out_sem, base, n, last):
                if n >= 4:
                    pe.wait_ge(out_sem, base + n - 3)
                two_tiles(s, q, banks[:, 4 + n % 4, :]).then_inc(full, 1)
                release()
                if last:
                    used(full, base + n + 1)

            def win(l, halves):
                base = 13 * l
                for n in halves:
                    if n % 2 == 0:
                        current[0] = take()
                    s = current[0]
                    if n >= 2:
                        pe.wait_ge(win_out, base + n - 1)
                    if n in (8, 9):
                        ins = token_tile(s, n - 8, banks[:, 6 + n % 2, :], hT)
                    else:
                        ins = two_tiles(s, n % 2, banks[:, 6 + n % 2, :])
                    ins.then_inc(win_full, 1)
                    release()
                    if n % 2 or n == 12:
                        used(win_full, base + n + 1)

            def gate(l, n, tiles=(0, 1)):
                if tiles[0] == 0:
                    if n % 2 == 0:
                        current[0] = take()
                    if n >= 2:
                        pe.wait_ge(gate_out, 16 * l + n - 1)
                    else:
                        pe.wait_ge(win_out, 13 * l + 13)
                for j in tiles:
                    c = (2 * (n % 2) + j) * P
                    ins = feature_tile(banks[:, 6 + n % 2, j * T:j * T + T],
                                       lambda k: current[0][:, k * 512 + c:k * 512 + c + P])
                if tiles[-1] == 1:
                    ins.then_inc(gate_full, 1)
                release()
                if n % 2 and tiles[-1] == 1:
                    used(gate_full, 16 * l + n + 1)

            def mat(q, m):
                return w(MATS + 1024 * q + P * m, P)

            def chunk(at, h, c):
                return w(at + (h // 2) * T + c * P, P, rows=half(h % 2))

            AT_, BT_, KT_, RT_ = PT, PT + 512, PT + 1024, PT + 1536

            def rw_lora(l):
                pe.wait_ge(RW_A.sem, RW_A.at("lora", l))
                for j in range(2):
                    mm(bank(0)[:, j * T:j * T + T], par(f"w2a2{l}", j * P, P, half(0)), w(INV + 3584, T, rows=half(0)))
                for j in range(2):
                    mm(bank(1)[:, j * T:j * T + T], par(f"w2a2{l}", j * P, P, half(1)), w(MX + 6 * T, T, rows=half(1)))
                for j in range(2):
                    ins = mm(bank(2)[:, j * T:j * T + T], par(f"g2{l}", j * P, P), w(INV + 3840, T))
                RW_P.mark(ins, "lora", l)
                pe.wait_ge(RW_V.sem, RW_V.at("k_squared", l))
                RW_P.mark(mm(bank(3), const("head_sum"), w(INV + 512, 512)), "squares", l)

            def rw_bonus(l):
                pe.wait_ge(RW_V.sem, RW_V.at("operands", l))
                mm(bank(3), const("head_sum"), w(MX, 512))
                for c in range(2):
                    for j in range(2):
                        pe.transpose(bank(4)[:, c * T + j * P:c * T + j * P + P],
                                     w(MX + (4 + j) * T + c * P, P), const("ident"))
                for i, at in enumerate((BT_, KT_)):
                    for j in range(2):
                        ins = pe.transpose(bank(5)[:, i * T + j * P:i * T + j * P + P],
                                           w(at + j * T, P), const("ident"))
                RW_P.mark(ins, "bonus", l)

            def rw_mats(l, i):
                pe.wait_ge(RW_V.sem, RW_V.at("mats0" if i else "bonus_used", l))
                for q, lhs in enumerate((BT_, KT_)):
                    for c in range(2):
                        for h in range(NH):
                            at = matrix(h, c) * P
                            ins = mm(bank(2 * q, 2)[:, at:at + P], chunk(lhs, h, c), chunk((AT_, RT_)[i], h, c))
                RW_P.mark(ins, f"mats{i}", l)

            X, XT, TM = INV, INV + 1024, INV + 2048

            def rw_turned(l, n):
                pe.wait_ge(RW_G.sem, RW_G.at(f"M{n}", l))
                pe.wait_ge(RW_V.sem, RW_V.at(f"X{n - 1}" if n else "mats1", l))
                for m in range(8):
                    ins = mm(bank(0, 2)[:, m * P:m * P + P], w(LEVEL_AT + m * P, P), w(X + m * P, P))
                RW_P.mark(ins, f"T{n}", l)

            def rw_level(l, n):
                pe.wait_ge(RW_A.sem, RW_A.at(f"T{n}", l))
                for m in range(8):
                    ins = mm(bank(2, 2)[:, m * P:m * P + P], w(TM + m * P, P), w(XT + m * P, P))
                if n < LEVELS - 1:
                    for m in range(8):
                        ins = mm(bank(0, 2)[:, m * P:m * P + P], w(XT + m * P, P), w(TM + m * P, P))
                RW_P.mark(ins, f"X{n}", l)

            VROW, BROW, KROW = 1024, 1536, 1792

            def rw_w(l, c):
                if c == 0:
                    pe.wait_ge(RW_V.sem, RW_V.at(f"X{LEVELS - 1}", l))
                else:
                    pe.wait_ge(RW_V.sem, RW_V.at("state", l))
                for h in range(NH):
                    o = bank(h % 2)[:, (h // 2) * HD:(h // 2) * HD + HD]
                    ins = mm(o, mat(1, matrix(h, c)), scr[:, VROW + c * T + h * HD:VROW + c * T + h * HD + HD],
                             True, c == 0)
                    if c:
                        ins = mm(o, chunk(AT_, h, 1), w(MX + 768 + (h // 2) * HD, HD, rows=half(h % 2)),
                                 False, True)
                RW_P.mark(ins, f"w{c}", l)

            def rw_u(l, c):
                pe.wait_ge(RW_A.sem, RW_A.at(f"w{c}", l))
                for h in range(NH):
                    ins = mm(bank(2)[:, h * HD:h * HD + HD], w(INV + 1024 + matrix(h, c) * P, P),
                             w(MX + (h % 2) * 2 * HD + (h // 2) * HD, HD))
                RW_P.mark(ins, f"u{c}", l)

            def rw_state(l):
                pe.wait_ge(RW_A.sem, RW_A.at("u0", l))
                for h in range(NH):
                    o = bank(4, rows=half(h % 2))[:, (h // 2) * HD:(h // 2) * HD + HD]
                    mm(o, scr[:, KROW + h * HD:KROW + h * HD + HD], scr[:, VROW + h * HD:VROW + h * HD + HD],
                       True, False)
                    ins = mm(o, scr[:, BROW + h * HD:BROW + h * HD + HD], w(MX + 256 + h * HD, HD), False, True)
                RW_P.mark(ins, "state", l)

            def rw_y(l):
                pe.wait_ge(RW_A.sem, RW_A.at("u1", l))
                for h in range(NH):
                    for c in range(2):
                        o = bank(3, rows=half(h % 2))[:, (h // 2) * T + c * P:(h // 2) * T + c * P + P]
                        mm(o, w(MX + 256 + 256 * c + h * HD, HD), mat(2, matrix(h, c)), True, False)
                        ins = mm(o, scr[:, VROW + c * T + h * HD:VROW + c * T + h * HD + HD], mat(3, matrix(h, c)),
                                 False, c == 0)
                        if c:
                            ins = mm(o, w(MX + 768 + (h // 2) * HD, HD, rows=half(h % 2)), chunk(RT_, h, 1),
                                     False, True)
                RW_P.mark(ins, "y", l)

            def rw_mean(l):
                pe.wait_ge(RW_V.sem, RW_V.at("y", l))
                RW_P.mark(mm(bank(4), const("head_mean"), w(INV, 512)), "mean", l)

            def rw_var(l):
                pe.wait_ge(RW_V.sem, RW_V.at("centred", l))
                RW_P.mark(mm(bank(5), const("head_mean"), w(INV + 1024, 512)), "var", l)

            def scores(q, k, r):
                for t in range(2):
                    mm(bank(4)[:, t * T:t * T + T], w(k + t * T, P, rows=half(r)), w(q + t * T, T, rows=half(r)))
                for t in range(2):
                    ins = mm(bank(5)[:, t * P:t * P + P], w(k + t * T + P, P, rows=half(r)),
                             w(q + t * T + P, P, rows=half(r)))
                return ins

            def weighted(v0):
                for h in range(NH):
                    r, t = h % 2, h // 2
                    o = bank(4, rows=half(r))[:, t * T:t * T + T]
                    mm(o, vt[:, 0, v0 + h * HD:v0 + h * HD + HD], w(Z_AT[r] + t * T, T), True, False)
                    ins = mm(o[:, P:T], vt[:, 1, v0 + h * HD:v0 + h * HD + HD], w(Z_AT[r] + 2 * T + t * P, P),
                             False, True)
                return ins

            def side(l, name):
                if name == "sb_squares":
                    pe.wait_ge(RW_A.sem, RW_A.at("rows", l))
                    pe.wait_ge(SB_V.sem, SB_V.at("squares", l))
                    for j in range(2):
                        ins = mm(bank(4 + j), const("head_mean"), w(TAIL + 512 * j, 512))
                    SB_P.mark(ins, "squares", l)
                elif name == "sb_scores0":
                    pe.wait_ge(SB_V.sem, SB_V.at("qk", l))
                    SB_P.mark(scores(PT + 8 * T, PT + 10 * T, 0), "scores0", l)
                elif name == "sb_scores1":
                    pe.wait_ge(SB_A.sem, SB_A.at("scores0", l))
                    SB_P.mark(scores(PT + 8 * T, PT + 10 * T, 1), "scores1", l)
                elif name[:-1] == "sb_suffix":
                    r = int(name[-1])
                    if r:
                        pe.wait_ge(SB_V.sem, SB_V.at("logs0", l))
                    else:
                        pe.wait_ge(SB_A.sem, SB_A.at("scores1", l))
                    pe.wait_ge(SB_V.sem, SB_V.at(f"softplus{r}", l))
                    first, second = LN_AT[r], LN_AT[r] + 2 * T
                    mm(bank(4), const("suffix"), w(first, 2 * T), True, False)
                    for t in range(2):
                        mm(bank(4)[:, t * T + P:t * T + T], const("ones"), w(second + t * P, P), False, t == 1)
                    ins = mm(bank(5)[:, 0:2 * P], const("suffix"), w(second, 2 * P))
                    SB_P.mark(ins, f"suffix{r}", l)
                elif name == "ret_rotated":
                    pe.wait_ge(SB_V.sem, SB_V.at("logs1", l))
                    for j in range(2):
                        ins = mm(bank(4 + j), const("swap"), w(PT + 12 * T + 512 * j, 512))
                    RET_P.mark(ins, "rotated", l)
                elif name == "sb_out":
                    pe.wait_ge(RET_V.sem, RET_V.at("qk", l))
                    pe.wait_ge(SB_A.sem, SB_A.at("weights1", l))
                    SB_P.mark(weighted(0), "out", l)
                elif name == "ret_scores0":
                    pe.wait_ge(SB_V.sem, SB_V.at("done", l))
                    RET_P.mark(scores(PT + 12 * T, PT + 14 * T, 0), "scores0", l)
                elif name == "ret_scores1":
                    pe.wait_ge(RET_V.sem, RET_V.at("scores0", l))
                    RET_P.mark(scores(PT + 12 * T, PT + 14 * T, 1), "scores1", l)
                elif name == "ret_out":
                    pe.wait_ge(RET_V.sem, RET_V.at("scores1", l))
                    RET_P.mark(weighted(256), "out", l)
                elif name == "ret_mean":
                    pe.wait_ge(RET_V.sem, RET_V.at("y", l))
                    RET_P.mark(mm(bank(5), const("head_mean"), w(BR + 1024, 512)), "mean", l)
                elif name == "ret_var":
                    pe.wait_ge(RET_V.sem, RET_V.at("centred", l))
                    RET_P.mark(mm(bank(4), const("head_mean"), w(MX + 512, 512)), "var", l)
                elif name == "conv_mean":
                    pe.wait_ge(CV_V.sem, CV_V.at("conv", l))
                    for j in range(2):
                        ins = mm(bank(5)[:, 0:T], const("ones"), w(PT + (20 + j) * T, T), j == 0, j == 1)
                    CV_P.mark(ins, "mean", l)
                elif name == "conv_var":
                    pe.wait_ge(RET_A.sem, RET_A.at("dev", l))
                    pe.wait_ge(CV_V.sem, CV_V.at("centred", l))
                    for j in range(2):
                        ins = mm(bank(4)[:, 0:T], const("ones"), w(MX + j * T, T), j == 0, j == 1)
                    CV_P.mark(ins, "var", l)

            def branches(l, ns):
                for n in ns:
                    if n % 8 == 0:
                        current[0] = take()
                    s, i, q = current[0], n // 4, n % 4
                    if n >= 4:
                        pe.wait_ge(br_out, 16 * l + n - 3)
                    else:
                        pe.wait_ge(gate_out, 16 * l + 16)
                        pe.wait_ge(RW_A.sem, RW_A.at("w1", l))
                    if BRANCH_ORDER[i] == 3:
                        pe.wait_ge(CV_A.sem, CV_A.at("done", l))
                    for j in range(2):
                        for k in range(2):
                            at = (2 * (i % 2) + k) * D + (2 * q + j) * P
                            ins = mm(banks[:, BRANCH_BANK[n % 4], j * T:j * T + T], s[:, at:at + P],
                                     br[:, 2 * BRANCH_ORDER[i] + k, :], k == 0, k == 1)
                    ins.then_inc(br_full, 1)
                    release()
                    if n % 8 == 7:
                        used(br_full, 16 * l + n + 1)

            def mixers(l):
                win(l, range(6))
                rw_lora(l)
                win(l, (6, 7, 8))
                rw_bonus(l)
                win(l, (9,))
                rw_mats(l, 0)
                win(l, (10,))
                rw_mats(l, 1)
                win(l, (11, 12))
                for n in range(LEVELS):
                    rw_turned(l, n)
                    side(l, SIDE[2 * n])
                    gate(l, 2 * n)
                    rw_level(l, n)
                    side(l, SIDE[2 * n + 1])
                    gate(l, 2 * n + 1)
                rw_w(l, 0)
                gate(l, 14, (0,))
                rw_u(l, 0)
                gate(l, 14, (1,))
                rw_state(l)
                gate(l, 15, (0,))
                rw_w(l, 1)
                gate(l, 15, (1,))
                rw_u(l, 1)
                branches(l, (0, 1))
                rw_y(l)
                branches(l, (2, 3))
                rw_mean(l)
                branches(l, (4, 5))
                rw_var(l)
                branches(l, range(6, 12))
                pe.wait_ge(RW_V.sem, RW_V.at("done", l))
                branches(l, range(12, 16))

            def project(r, lhs, wait_half=None):
                if wait_half:
                    slabs = [take(), take()]
                    for i in range(2):
                        wait_half(i)
                        for c in range(2):
                            for a in range(TT):
                                for k in range(4 * i, 4 * i + 4):
                                    ins = mm(banks[:, 2 * c + a, :], lhs[:, k, a * P:a * P + P],
                                             slabs[c][:, k * 512:k * 512 + 512], k == 0, k == KT - 1)
                            if i:
                                ins.then_inc(proj_full, 1)
                                used(proj_full, 2 * r + c + 1)
                    release()
                    return
                for c in range(2):
                    s = take()
                    for a in range(TT):
                        ins = token_tile(s, a, banks[:, 2 * c + a, :], lhs)
                        if a == 0:
                            release()
                    ins.then_inc(proj_full, 1)
                    used(proj_full, 2 * r + c + 1)
                release()

            def slab_of_part(e, j):
                n = slab[0] + j
                pe.wait_ge(landed[n % RING], e * (16 * EXPERT_SLABS // RING) + 16 * (n // RING + 1))
                return ring[:, n % RING, :]

            def split_mm(out_, lhsT, rhs, start, stop):
                mm(out_, lhsT[0], rhs[0], start, False)
                mm(out_, lhsT[0], rhs[1], False, False)
                return mm(out_, lhsT[1], rhs[0], False, stop)

            def ffn_split(name):
                first, first_part = FIRST_EXPERT[name], 2 * SPLIT[name]
                pe.wait_ge(input_lo, 2 * SPLIT[name] + 2)
                with pe.Fori(0, 2) as e:
                    for t in range(FT):
                        if t >= 4:
                            pe.wait_ge(glu_done, (e + first) * FT + t - 2)
                        pe.wait_ge(unit_lo, unit_count(e + first_part, t))
                        for m in range(2):
                            for k in range(KT):
                                at = k * 2 * P + m * P
                                ins = split_mm(banks[:, 4 + t % 4, m * T:m * T + T],
                                               [v[:, t % SPLIT_BUFS, at:at + P] for v in (w_hi, w_lo)],
                                               [v[:, k, :] for v in (h_hi, h_lo)], k == 0, k == KT - 1)
                        ins.then_inc(glu_full, 1)
                    pe.wait_ge(ffn_added, (e + first) * 4 + 1)
                    for k in range(FT):
                        u = OUT_UNIT + k // 2
                        if k % 2 == 0:
                            pe.wait_ge(unit_lo, unit_count(e + first_part, u))
                        pe.wait_ge(hidden_lo, (e + first_part) * FT + k + 1)
                        for b in range(4):
                            at = (k % 2) * D + (b % 2) * 512
                            ins = split_mm(banks[:, b, :],
                                           [v[:, k, (b // 2) * P:(b // 2) * P + P] for v in (g_hi, g_lo)],
                                           [v[:, u % SPLIT_BUFS, at:at + 512] for v in (w_hi, w_lo)],
                                           k == 0, k == FT - 1)
                        if k % 2 or k == FT - 1:
                            ins.then_inc(out_used, 1)
                slab[0] += 2 * EXPERT_SLABS
                pe.wait_ge(slab_used, slab[0])

            def ffn(name):
                first = FIRST_EXPERT[name]
                release()
                with pe.Fori(0, N_PARTS[name]) as e:
                    for j in range(IN_SLABS):
                        s = slab_of_part(e, j)
                        for t in range(2 * j, min(2 * j + 2, FT)):
                            if t >= 4:
                                pe.wait_ge(glu_done, (e + first) * FT + t - 2)
                            for m in range(2):
                                c = (t % 2) * HALF_SLAB + m * P
                                ins = feature_tile(banks[:, 4 + t % 4, m * T:m * T + T],
                                                   lambda k: s[:, k * 2 * P + c:k * 2 * P + c + P])
                            ins.then_inc(glu_full, 1)
                            release()
                        used(glu_full, (e + first) * FT + min(2 * j + 2, FT))
                    pe.wait_ge(ffn_added, (e + first) * 4 + 1)
                    for k in range(FT):
                        if k % 4 == 0:
                            s = slab_of_part(e, IN_SLABS + k // 4)
                        pe.wait_ge(glu_done, (e + first) * FT + k + 2)
                        for b in range(4):
                            at = (k % 4) * D + (b % 2) * 512
                            ins = mm(banks[:, b, :], w(k * T + (b // 2) * P, P), s[:, at:at + 512],
                                     k == 0, k == FT - 1)
                        release()
                        if k % 4 == 3 or k == FT - 1:
                            ins.then_inc(slab_used, 1)
                slab[0] += EXPERT_SLABS * N_PARTS[name]

            def gather():
                for k in range(KT):
                    o = bank(4 + k // 4)[:, (k % 4) * CAP:(k % 4) * CAP + CAP]
                    for a in range(TT):
                        ins = mm(o, scr[:, a * D + k * P:a * D + k * P + P], sel[:, a, :], a == 0, a == TT - 1)
                return ins

            def scatter():
                for b in range(4):
                    ins = mm(bank(b), sel_turned[:, (b // 2) * P:(b // 2) * P + P],
                             result[:, (b % 2) * 512:(b % 2) * 512 + 512])
                ins.then_inc(sp_scattered, 1)

            def experts_short():
                first = FIRST_EXPERT["moe"]
                pe.wait_ge(sp_selected, 1)
                gather().then_inc(sp_gathered, 1)
                with pe.Fori(0, NE) as e:
                    pe.wait_ge(sp_inputs, e + 1)
                    for j in range(IN_SLABS):
                        s = slab_of_part(e, j)
                        for t in range(2 * j, min(2 * j + 2, FT)):
                            if t >= 2:
                                pe.wait_ge(glu_done, (e + first) * FT + t)
                            for m in range(2):
                                for k in range(KT):
                                    at = (t % 2) * HALF_SLAB + k * 2 * P + m * P
                                    ins = mm(banks[:, 6 + t % 2, m * P:m * P + CAP], s[:, at:at + P],
                                             gathered[:, k, :], k == 0, k == KT - 1)
                            ins.then_inc(glu_full, 1)
                            release()
                            if t == 5:
                                pe.wait_ge(sp_copied, e + 1)
                                pe.wait_ge(sp_turned, e + 1)
                                scatter()
                            if t == 8:
                                pe.wait_ge(sp_selected, e + 2)
                                gather()
                                for a in range(TT):
                                    ins = pe.transpose(banks[0:CAP, 4 + a, 384:512], sel_gate[:, a, :], const("ident"))
                                ins.then_inc(sp_gathered, 1)
                        used(glu_full, (e + first) * FT + min(2 * j + 2, FT))
                    pe.wait_ge(sp_added, 4 * e + 5)
                    for k in range(FT):
                        if k % 4 == 0:
                            s = slab_of_part(e, IN_SLABS + k // 4)
                        pe.wait_ge(glu_done, (e + first) * FT + k + 2)
                        for b in range(2):
                            at = (k % 4) * D + b * 512
                            ins = mm(bank(b, rows=slice(0, CAP)), w(k * CAP, CAP), s[:, at:at + 512],
                                     k == 0, k == FT - 1)
                        release()
                        if k % 4 == 3:
                            ins.then_inc(slab_used, 1)
                    ins.then_inc(sp_result, 1)
                    pe.wait_ge(sp_result, e + 1)
                    pe.sem_inc(slab_used, 1)
                pe.wait_ge(sp_copied, NE + 1)
                pe.wait_ge(sp_turned, NE + 1)
                scatter()

            def lru():
                for c in range(4):
                    s = take()
                    for q in range(2):
                        fill(s, q, ain_full, ain_out, 0, 2 * c + q, q == 1)
                release()
                s = take()
                for h in range(KT):
                    pe.wait_ge(lru_conv, h // 2 + 1)
                    if h < 4:
                        pe.wait_ge(ain_out, 5 + h)
                    else:
                        pe.wait_ge(ag_out, h - 3)
                    for g in range(2):
                        ins = mm(banks[:, 4 + h % 4, g * T:g * T + T], s[:, g * D + h * P:g * D + h * P + P],
                                 w(6144 + h * T, T))
                    ins.then_inc(ag_full, 1)
                    release()
                used(ag_full, KT)
                release()
                project(2, w(6144, KT, T), lambda i: pe.wait_ge(LR_V.sem, LR_V.at(f"done{i}")))

            def hidden_layer(v):
                s = take()
                if v == 0:
                    pe.wait_ge(KV_V.sem, KV_V.at("windows"))
                for m in range(2):
                    for j in range(CB // 2):
                        ins = mm(bank(v)[:, 64 * m:64 * m + G * NC], s[:, j * HID + m * P:j * HID + m * P + P],
                                 w(EXW + 960 * v + j * G * NC, G * NC), j == 0, j == CB // 2 - 1)
                KV_P.mark(ins, f"hidden{v}")
                release()
                used(KV_P.sem, KV_P.at(f"hidden{v}"))

            def query(q):
                if q % 2 == 0:
                    current[0] = take()
                pe.wait_ge(kv_out, 4 if q < 2 else 6)
                if q == 0:
                    pe.wait_ge(Q_V.sem, Q_V.at("input"))
                Q_P.mark(two_tiles(current[0], q % 2, banks[:, Q_BANK[q], :], w(HB, KT, T)), f"full{q}")
                release()
                if q % 2:
                    used(Q_P.sem, Q_P.at(f"full{q}"))

            def query_mean(i):
                pe.wait_ge(Q_V.sem, Q_V.at(f"squares{i}"))
                for j in range(2):
                    ins = mm(bank(Q_BANK[2 * i + j]), const("head_mean"), w(QSQ + 1024 * i + 512 * j, 512))
                Q_P.mark(ins, f"mean{i}")

            def query_rot(i):
                pe.wait_ge(Q_V.sem, Q_V.at(f"normed{i}"))
                for j in range(2):
                    ins = mm(bank(Q_BANK[2 * i + j]), const("swap"), w(QR + 1024 * i + 512 * j, 512))
                Q_P.mark(ins, f"rot{i}")

            def keys_and_queries():
                for c in range(2):
                    s = take()
                    for q in range(2):
                        two_tiles(s, q, banks[:, 4 + 2 * c + q, :]).then_inc(kv_full, 1)
                        release()
                    used(kv_full, 2 * c + 2)
                s = take()
                for a in range(TT):
                    pe.wait_ge(kv_out, a + 1)
                    token_tile(s, a, banks[:, 4 + a, :], hT).then_inc(kv_full, 1)
                    release()
                used(kv_full, 6)
                pe.wait_ge(KV_V.sem, KV_V.at("k_squares"))
                for j in range(2):
                    ins = mm(bank(2 + j), const("head_mean"), w(KSQ + 512 * j, 512))
                KV_P.mark(ins, "k_mean")
                release()
                query(0)
                query(1)
                pe.wait_ge(KV_V.sem, KV_V.at("k_normed"))
                for j in range(2):
                    ins = mm(bank(2 + j), const("swap"), w(KR + 512 * j, 512))
                KV_P.mark(ins, "k_rot")
                hidden_layer(0)
                query_mean(0)
                hidden_layer(1)
                query(2)
                pe.wait_ge(KV_A.sem, KV_A.at("hidden1"))
                pe.wait_ge(KV_V.sem, KV_V.at("k_rope"))
                for m in range(2):
                    ins = mm(bank(2)[:, 0:G * NC], par("cmp_w2k", m * P, P), w(HIDN + 64 * m, G * NC), m == 0, m == 1)
                KV_P.mark(ins, "k_cmp")
                query_rot(0)
                query(3)
                pe.wait_ge(KV_V.sem, KV_V.at("cmp_squares"))
                KV_P.mark(mm(bank(3)[:, 0:G * NC], const("head_mean"), w(EXW, G * NC)), "cmp_mean")
                for a in range(TT):
                    o = bank(0)[:, a * 48:a * 48 + 48]
                    for k in range(KT):
                        mm(o, w(HB, KT, T)[:, k, a * P:a * P + P], par("gate_w", k * 48, 48), k == 0, False)
                    at, _ = CONSTS["ones"]
                    ins = mm(o, consts[0:1, at:at + P], par("gate_b", 0, 48, slice(0, 1)), False, True)
                Q_P.mark(ins, "gates")
                release()
                query_mean(1)
                pe.wait_ge(KV_V.sem, KV_V.at("cmp_normed"))
                KV_P.mark(mm(bank(2)[:, 0:G * NC], const("swap"), w(KCM, G * NC)), "cmp_rot")
                r = slice(0, NC)
                for g in range(G):
                    o = bank(3, rows=r)[:, g * HD:g * HD + HD]
                    for m in range(2):
                        mm(o, w(HIDN + 128 + 64 * m + g * NC, NC), par("cmp_w2v", m * HD, HD), m == 0, False)
                    at, _ = CONSTS["ones"]
                    ins = mm(o, consts[0:1, at:at + NC], par("cmp_b2v", 0, HD, slice(0, 1)), False, True)
                KV_P.mark(ins, "v_cmp")
                query_rot(1)
                pe.wait_ge(KV_A.sem, KV_A.at("k_copies"))
                pe.wait_ge(KV_V.sem, KV_V.at("v_cmp"))
                pe.wait_ge(Q_A.sem, Q_A.at("gates"))
                pe.wait_ge(Q_V.sem, Q_V.at("rope1"))

            def at_score(k):
                g, a, b = TASKS[k]
                n = P * (a + 1)
                if k >= 2:
                    pe.wait_ge(at_masked, k - 1)
                for t in range(2):
                    for r in range(2):
                        ins = mm(bank(2 * (k % 2) + r)[:, t * n:t * n + n],
                                 w(QR + (2 * g + t) * T + a * P, P, rows=half(r)),
                                 w(KD + 1024 * b + g * T, n, rows=half(r)))
                ins.then_inc(at_scores, 1)

            def at_turn(k):
                g, a, b = TASKS[k]
                n = P * (a + 1)
                if k:
                    pe.wait_ge(at_copied, k)
                else:
                    pe.wait_ge(CA_V.sem, CA_V.at("probs"))
                if b == 0:
                    for r in range(2):
                        for t in range(2):
                            i = 2 * r + t
                            pe.transpose(bank(7, rows=slice(0, NC))[:, i * P:i * P + P],
                                         w(CMP_S, 4, 8 * NC)[:, 2 * r + a, (2 * g + t) * NC:(2 * g + t) * NC + NC],
                                         const("ident"))
                pe.wait_ge(at_probs, k + 1)
                for i in range(4):
                    for c in range(a + 1):
                        ins = pe.transpose(bank(4, 2)[:, i * n + c * P:i * n + c * P + P],
                                           at_s(k)[:, i, c * P:c * P + P], const("ident"))
                ins.then_inc(at_turned, 1)

            def at_sum(u):
                g, a = u // TT, u % TT
                n = P * (a + 1)
                pe.wait_ge(at_copied, 2 * u + 2)
                if u:
                    pe.wait_ge(at_stored, u)
                for i in range(4):
                    o = bank(6, rows=half(i // 2))[:, (i % 2) * P:(i % 2) * P + P]
                    mm(o, w(VCM + g * HD, HD, rows=slice(0, NC)), at_cmp_t(u)[:, i * P:i * P + P], True, False)
                    for b in range(2):
                        for c in range(a + 1):
                            ins = mm(o, w(VSW + 512 * c + 256 * b + g * HD, HD),
                                     at_t(2 * u + b)[:, i * n + c * P:i * n + c * P + P], False, b == 1 and c == a)
                ins.then_inc(at_out, 1)

            def attention():
                for a in range(TT):
                    for j in range(KT):
                        for r in range(2):
                            ins = mm(bank(4 + r)[:, (8 * a + j) * NC:(8 * a + j) * NC + NC],
                                     w(QR + j * T + a * P, P, rows=half(r)), w(KCM + (j // 2) * NC, NC, rows=half(r)))
                CA_P.mark(ins, "scores")
                at_score(0)
                at_score(1)
                for k in range(len(TASKS)):
                    if k + 2 < len(TASKS):
                        at_score(k + 2)
                    at_turn(k)
                    if k % 2 == 0 and k:
                        at_sum(k // 2 - 1)
                at_sum(2 * G - 1)

            for l in range(2):
                norm(2 * l)
                mixers(l)
                pe.wait_ge(br_out, 16 * l + 16)
                project(l, w(MERGED, KT, T))
                norm(2 * l + 1)
                if l == 0:
                    ffn_split("dense")
                else:
                    for a in range(TT):
                        for k in range(KT):
                            ins = mm(bank(0)[:, a * NE:a * NE + NE], hT[:, k, a * P:a * P + P],
                                     par("router", k * NE, NE), k == 0, k == KT - 1)
                    RT_P.mark(ins, "logits")
                    pe.wait_ge(RT_V.sem, RT_V.at("chosen"))
                    for a in range(TT):
                        mm(bank(1)[:, a * NE:a * NE + NE], const("strict"), chosen[:, a, 0:NE], True, a == 0)
                        if a:
                            mm(bank(1)[:, a * NE:a * NE + NE], const("ones"), chosen[:, 0, 0:NE], False, True)
                    for a in range(TT):
                        ins = mm(bank(1)[:, 2 * NE:3 * NE], const("ones"), chosen[:, a, 0:NE], a == 0, a == 1)
                    RT_P.mark(ins, "slots")
                    release()
                    pe.wait_ge(RT_V.sem, RT_V.at("flag"))
                    with pe.If(pe.value_load(crowded[0:1, 0:1], min_val=0, max_val=1) == 0):
                        experts_short()
                    with pe.Else():
                        ffn("moe")
                        slab[0] -= EXPERT_SLABS * NE
                    slab[0] += EXPERT_SLABS * NE
            norm(4)
            lru()
            norm(5)
            ffn_split("f0")
            norm(6)
            keys_and_queries()
            attention()
            pe.wait_ge(at_stored, 2 * G)
            project(3, w(22016, KT, T))
            norm(7)
            ffn_split("f1")
            assert slab[0] == n_slabs

        @block.vector
        def _(dve):
            chain = Chain(dve, v_chain)
            run = chain.run
            tt, ts, stt = dve.tensor_tensor, dve.tensor_scalar, dve.scalar_tensor_tensor
            MUL, ADD, SUB, MAX = ALU.mult, ALU.add, ALU.subtract, ALU.max

            def bc(ap, n):
                return ap.unsqueeze(1).to_broadcast([ap.shape[0], n, ap.shape[1]])

            chain.to(dve.memset(small[:, 13:14], 0.0), glu_done, 1)
            chain.to(dve.memset(small[:, 14:15], 0.0), ffn_added, 1)

            def split_unit(name, h, u):
                first = FIRST_SLAB[name] + h * EXPERT_SLABS
                n = unit_count(2 * SPLIT[name] + h, u)
                dve.wait_ge(unit_hi, n)
                wait_unit_free(dve, name, h, u)
                hi, lo = (v[:, u % SPLIT_BUFS, 0:unit_cols(u)] for v in (w_hi, w_lo))
                tt(lo, unit_of_ring(u, first), hi.bitcast(F32), SUB).then_inc(unit_lo, 1)
                if u % 2 or u == FT - 1:
                    dve.wait_ge(unit_lo, n)
                    dve.sem_inc(slab_used, 1)

            def split_input(name):
                for i in range(2):
                    dve.wait_ge(input_hi, 2 * SPLIT[name] + i + 1)
                    ks = slice(4 * i, 4 * i + 4)
                    tt(h_lo[:, ks, :], hT[:, ks, :], h_hi[:, ks, :].bitcast(F32), SUB).then_inc(input_lo, 1)

            def ffn_split(name):
                split_input(name)
                split_unit(name, 0, UNITS[1])
                split_unit(name, 0, UNITS[2])
                for h in range(2):
                    first = FIRST_EXPERT[name] + h
                    for t in range(FT):
                        dve.wait_ge(glu_silu, first * FT + t + 1)
                        tt(hidden[:, t, :], glu[:, t % 2, :], banks[:, 4 + t % 4, T:2 * T], MUL).then_inc(glu_done, 1)
                        split_unit(name, h, UNITS[t + 3])
                    for u in UNITS[FT + 3:]:
                        split_unit(name, h, u)
                    if h == 0:
                        for u in UNITS[:2]:
                            split_unit(name, 1, u)
                    dve.wait_ge(out_used, (2 * SPLIT[name] + h + 1) * OUT_UNITS)
                    dve.wait_ge(ffn_added, first * 4 + 1)
                    for b in range(4):
                        xs = x[:, b // 2, (b % 2) * 512:(b % 2) * 512 + 512]
                        tt(xs, xs, banks[:, b, :], ADD).then_inc(ffn_added, 1)
                    if h == 0:
                        split_unit(name, 1, UNITS[2])
                dve.wait_ge(ffn_added, 4 * (FIRST_EXPERT[name] + 2) + 1)

            def norm(n, gain):
                dve.wait_ge(NORM_A.sem, NORM_A.at("root", n))
                run(dve.reciprocal(small[:, 0:2], small[:, 2:4]))
                for a in range(TT):
                    ins = ts(glu[:, a, 0:P], const("ident"), small[:, a:a + 1], None, MUL)
                run(ins, NORM_V, "diagonal", n)
                split = SPLIT_NORMS.get(n)
                if split:
                    dve.wait_ge(slab_used, FIRST_SLAB[split])
                    split_unit(split, 0, UNITS[0])
                for b in (0, 2):
                    dve.wait_ge(NORM_P.sem, NORM_P.at(f"bank{b}", n))
                    for k in (2 * b, 2 * b + 1):
                        ins = ts(hT[:, k, :], bank(b)[:, (k % 2) * T:(k % 2) * T + T], par(gain, k), None, MUL)
                    if b:
                        run(ins, NORM_V, "hT", n)
                    elif split:
                        chain.to(ins, input_half, SPLIT[split] + 1)
                if n == 3:
                    for a in range(TT):
                        ins = ts(scr[:, a * D:a * D + D], x[:, a, :], small[:, a:a + 1], None, MUL)
                    run(ins)

            def rw_mix(l):
                dve.wait_ge(win_out, 13 * l + 4)
                p, d = w(PT, 8, T), w(INV, 8, T)
                run(tt(d[:, :, 1:T], p[:, :, 0:T - 1], p[:, :, 1:T], SUB))
                run(ts(d[:, :, 0:1], p[:, :, 0:1], -1.0, None, MUL))
                m = w(MX, 8, T)
                for j in range(8):
                    ins = stt(m[:, j, :], d[:, j, :], par(f"mu{l}", j), p[:, j, :], MUL, ADD)
                    if j == 7:
                        run(ins, RW_V, "mixed", l)
                    else:
                        run(ins)

            def rw_operands(l):
                r, k, v, a = (w(MX + 512 * i, 512) for i in range(4))
                kk, sq, rinv = w(INV, 512), w(INV + 512, 512), w(INV + 1024, 512)
                sw, c, cex = w(INV + 1536, 512), w(INV + 2048, 512), w(INV + 2560, 512)
                e1, e2, e3 = w(PT, 512), w(INV + 3072, 512), w(PT + 1536, 512)
                at_, bt_, kt_, rt_ = (w(PT + 512 * i, 512) for i in range(4))
                for j in range(2):
                    run(ts(kk[:, j * T:j * T + T], k[:, j * T:j * T + T], par(f"k_k{l}", j), None, MUL))
                run(tt(sq, kk, kk, MUL), RW_V, "k_squared", l)
                dve.wait_ge(RW_A.sem, RW_A.at("sigmoids", l))
                run(ts(sw, sw, -DECAY_SCALE, None, MUL))
                for j in range(4):
                    s = slice(j * P, j * P + P)
                    run(dve.tensor_tensor_scan(c[:, s], const("ones"), sw[:, s], 0.0, MUL, ADD))
                run(tt(cex, c, sw, SUB), RW_V, "decays", l)
                dve.wait_ge(RW_A.sem, RW_A.at("norm", l))
                run(ts(rinv, rinv, 1e-12, None, MAX))
                run(dve.reciprocal(rinv, rinv))
                run(tt(kk, kk, rinv, MUL))
                for j in range(2):
                    s = slice(j * T, j * T + T)
                    run(ts(sq[:, s], a[:, s], 1.0, par(f"k_a{l}", j), SUB, MUL))
                run(stt(k, sq, 1.0, k, ADD, MUL))
                run(tt(sw, kk, a, MUL))
                dve.wait_ge(RW_A.sem, RW_A.at("exps", l))
                run(stt(at_, kk, -1.0, e1, MUL, MUL))
                run(tt(bt_, sw, e2, MUL))
                run(tt(kt_, k, e2, MUL))
                run(tt(rt_, r, e3, MUL))
                for j in range(2):
                    s = slice(j * T, j * T + T)
                    ins = stt(r[:, s], r[:, s], par(f"r_k{l}", j), k[:, s], MUL, MUL)
                    if j:
                        run(ins, RW_V, "operands", l)
                    else:
                        run(ins)
                dve.wait_ge(RW_P.sem, RW_P.at("bonus", l))
                run(tt(scr[:, 512:1024], bank(3), v, MUL), RW_V, "bonus_used", l)
                dve.wait_ge(RW_G.sem, RW_G.at("zeroed", l))
                for i in range(2):
                    dve.wait_ge(RW_P.sem, RW_P.at(f"mats{i}", l))
                    mask = bc(const("causal" if i else "strict").bitcast(I32), 8)
                    for q in range(2):
                        ins = dve.copy_predicated(w(MATS + 1024 * (2 * i + q), 8, P), mask, grid(bank(2 * q, 2), 8))
                        if q:
                            run(ins, RW_V, f"mats{i}", l)
                        else:
                            run(ins)
                    if i == 0:
                        for at in (INV, INV + 1024):
                            run(dve.tensor_copy(w(at, 8, P), bc(const("ident"), 8)))

            def rw_level(l, n):
                dve.wait_ge(RW_P.sem, RW_P.at(f"X{n}", l))
                xt = w(INV + 1024, 1024)
                if n < LEVELS - 1:
                    run(tt(w(INV, 1024), w(INV, 1024), bank(0, 2), ADD))
                run(tt(xt, xt, bank(2, 2), ADD), RW_V, f"X{n}", l)

            def centre(b_mean, P_, V_, y, xc, sq, dev, l):
                dve.wait_ge(P_.sem, P_.at("mean", l))
                run(tt(w(xc, 512), w(y, 512), bank(b_mean), SUB))
                run(tt(w(sq, 512), w(xc, 512), w(xc, 512), MUL), V_, "centred", l)

            def over_dev(A_, y, xc, sq, dev, l):
                dve.wait_ge(A_.sem, A_.at("dev", l))
                run(dve.reciprocal(w(dev, 512), w(dev, 512)))
                run(tt(w(y, 512), w(xc, 512), w(dev, 512), MUL))

            def rw_state(l):
                dve.wait_ge(RW_P.sem, RW_P.at("state", l))
                for j in range(2):
                    ins = ts(w(MX + 768 + j * HD, HD), bank(4)[:, j * HD:j * HD + HD], small[:, 8 + j:9 + j], None, MUL)
                    if j:
                        run(ins, RW_V, "state", l)
                    else:
                        run(ins)

            RW_Y = (INV, INV + 512, INV + 1024, INV + 1536)

            def rw_y(l):
                dve.wait_ge(RW_P.sem, RW_P.at("y", l))
                run(dve.tensor_copy(w(RW_Y[0], 512), bank(3)), RW_V, "y", l)

            def rw_done(l):
                y = w(RW_Y[0], 512)
                over_dev(RW_A, *RW_Y, l)
                for j in range(2):
                    s = slice(j * T, j * T + T)
                    run(ts(y[:, s], y[:, s], par(f"ln_w{l}", j), par(f"ln_b{l}", j), MUL, ADD))
                run(tt(y, y, scr[:, 512:1024], ADD))
                run(tt(w(BR, 512), y, scr[:, 0:512], MUL), RW_V, "done", l)

            def rotate(dst, rot, cos, sin, tmp, groups, steps, name, rnd=0):
                run(tt(tmp, rot, bc(sin, groups), MUL))
                run(tt(dst, dst, bc(cos, groups), MUL))
                run(tt(dst, dst, tmp, ADD), steps, name, rnd)

            RET_Y = (BR + 1024, MX, MX + 512, INV + 3072)

            def sb_squares(l):
                dve.wait_ge(win_out, 13 * l + 6)
                qk = w(PT + 8 * T, 1024)
                run(tt(w(TAIL, 1024), qk, qk, MUL), SB_V, "squares", l)

            def side(l, name):
                if name == "sb_squares":
                    qk, root = w(PT + 8 * T, 1024), w(TAIL, 1024)
                    dve.wait_ge(SB_A.sem, SB_A.at("norm", l))
                    run(dve.reciprocal(root, root))
                    run(tt(qk, qk, root, MUL))
                    run(ts(qk[:, 0:512], qk[:, 0:512], par(f"sb_q{l}"), HD ** -0.5, MUL, MUL))
                    run(ts(qk[:, 512:1024], qk[:, 512:1024], par(f"sb_k{l}"), None, MUL), SB_V, "qk", l)
                elif name[:-1] == "sb_scores":
                    r = int(name[-1])
                    ln = w(LN_AT[r], PAIR)
                    dve.wait_ge(SB_A.sem, SB_A.at(f"ln{r}", l))
                    run(stt(ln, w(Z_AT[r], PAIR), 0.0, ln, MAX, ADD))
                    first, second = diagonals(ln)
                    run(tt(first, first, bc(const("strict"), 2), MUL))
                    run(tt(second, second, bc(const("strict"), 2), MUL), SB_V, f"softplus{r}", l)
                elif name[:-1] == "sb_suffix":
                    r = int(name[-1])
                    z = w(Z_AT[r], PAIR)
                    dve.wait_ge(SB_P.sem, SB_P.at(f"suffix{r}", l))
                    run(tt(z, z, bank(4, 2)[:, 0:PAIR], SUB))
                    first, second = diagonals(z)
                    run(tt(first, first, bc(const("not_before"), 2), ADD))
                    run(tt(second, second, bc(const("not_before"), 2), ADD), SB_V, f"logs{r}", l)
                elif name == "ret_rotated":
                    dve.wait_ge(RET_P.sem, RET_P.at("rotated", l))
                    rotate(w(PT + 12 * T, 4, T), grid(bank(4, 2), 4), const("cos"), const("sin"), w(TAIL, 4, T), 4,
                           RET_V, "qk", l)
                elif name == "sb_out":
                    dve.wait_ge(SB_P.sem, SB_P.at("out", l))
                    run(dve.tensor_copy(w(BR + 512, 512), bank(4)), SB_V, "done", l)
                elif name[:-1] == "ret_scores":
                    r = int(name[-1])
                    z, s = w(Z_AT[r], PAIR), bank(4, 2)[:, 0:PAIR]
                    dec = grid(const("decay"), 2)[:, r, :]
                    dve.wait_ge(RET_P.sem, RET_P.at(f"scores{r}", l))
                    run(tt(z[:, 0:2 * T], s[:, 0:2 * T], dec, MUL))
                    run(tt(diagonals(z)[1], diagonals(s)[1], grid(dec, 2)[:, :, 0:P], MUL), RET_V, f"scores{r}", l)
                elif name == "ret_out":
                    dve.wait_ge(RET_P.sem, RET_P.at("out", l))
                    run(dve.tensor_copy(w(RET_Y[0], 512), bank(4)), RET_V, "y", l)
                elif name == "ret_mean":
                    centre(5, RET_P, RET_V, *RET_Y, l)
                elif name == "ret_var":
                    over_dev(RET_A, *RET_Y, l)
                    dve.wait_ge(RET_A.sem, RET_A.at("silu", l))
                    for j in range(2):
                        y = w(RET_Y[0] + j * T, T)
                        ins = stt(y, y, par(f"gn{l}", j), w(PT + (16 + j) * T, T), MUL, MUL)
                        if j:
                            run(ins, RET_V, "done", l)
                        else:
                            run(ins)
                elif name == "conv_mean":
                    y, xc, sq = w(PT + 20 * T, 2, T), w(PT + 18 * T, 2, T), w(MX, 2, T)
                    dve.wait_ge(CV_P.sem, CV_P.at("mean", l))
                    run(stt(xc, bc(bank(5)[:, 0:T], 2), -1.0 / 256, y, MUL, ADD))
                    run(stt(sq, xc, 1.0 / 256, xc, MUL, MUL), CV_V, "centred", l)
                elif name == "conv_var":
                    xc, dev = w(PT + 18 * T, 2, T), w(INV + 3072, T)
                    dve.wait_ge(CV_A.sem, CV_A.at("dev", l))
                    run(dve.reciprocal(dev, dev))
                    run(tt(xc, xc, bc(dev, 2), MUL))
                    for j in range(2):
                        ins = ts(w(PT + (20 + j) * T, T), xc[:, j, :], par(f"cln_w{l}", j), par(f"cln_b{l}", j), MUL, ADD)
                        if j:
                            run(ins, CV_V, "affine", l)
                        else:
                            run(ins)

            def conv_input(l):
                u = w(PT + 18 * T, 512)
                dve.wait_ge(CV_A.sem, CV_A.at("sigmoid", l))
                run(tt(u, u, w(PT + 20 * T, 512), MUL))

            def conv_taps(l, taps):
                for back in taps:
                    for j in range(2):
                        u, acc = w(PT + (18 + j) * T, T), w(PT + (20 + j) * T, T)
                        tap = par(f"dw{l}", j * TAPS + TAPS - 1 - back)
                        if back == 0:
                            ins = ts(acc, u, tap, par(f"db{l}", j), MUL, ADD)
                        else:
                            ins = stt(acc[:, back:T], u[:, 0:T - back], tap, acc[:, back:T], MUL, ADD)
                        if back == TAPS - 1 and j:
                            run(ins, CV_V, "conv", l)
                        else:
                            run(ins)

            def merge(l, ns):
                for n in ns:
                    i, q = BRANCH_ORDER[n // 4], n % 4
                    dve.wait_ge(br_full, 16 * l + n + 1)
                    s, merged = w(SIG + 512 * (4 * i + q), 512), w(MERGED + 512 * q, 512)
                    ins = tt(s, s, banks[:, BRANCH_BANK[n % 4], :], MUL)
                    if n >= 4:
                        run(ins)
                        ins = tt(merged, merged, s, ADD)
                    chain.to(ins, br_out, 16 * l + n + 1)

            def mixers(l):
                rw_mix(l)
                rw_operands(l)
                sb_squares(l)
                for n in range(LEVELS):
                    side(l, SIDE[2 * n])
                    if n == 0:
                        conv_input(l)
                    rw_level(l, n)
                    side(l, SIDE[2 * n + 1])
                    conv_taps(l, range(TAPS * n // 5, TAPS * (n + 1) // 5) if n < 5 else ())
                rw_state(l)
                merge(l, (0, 1))
                rw_y(l)
                merge(l, (2, 3))
                centre(4, RW_P, RW_V, *RW_Y, l)
                merge(l, (4, 5))
                rw_done(l)
                merge(l, range(6, 16))

            def project(r):
                for c in range(2):
                    dve.wait_ge(proj_full, 2 * r + c + 1)
                    for a in range(TT):
                        xs = x[:, a, 512 * c:512 * c + 512]
                        ins = tt(xs, xs, banks[:, 2 * c + a, :], ADD)
                        if a:
                            chain.to(ins, proj_added, 2 * r + c + 1)
                        else:
                            run(ins)

            def route():
                dve.wait_ge(RT_P.sem, RT_P.at("logits"))
                lg = small[:, 64:64 + TT * NE].rearrange("p (a e) -> p a e", a=TT)
                top = small[:, 96:96 + TT * 8].rearrange("p (a e) -> p a e", a=TT)
                idx = small[:, 128:128 + TT * 8].rearrange("p (a e) -> p a e", a=TT)
                run(dve.tensor_copy(lg, bank(0)[:, 0:TT * NE].rearrange("p (a e) -> p a e", a=TT)))
                for a in range(TT):
                    run(dve.max(top[:, a, :], lg[:, a, :]))
                    run(dve.max_index(top_index[:, a, :], top[:, a, :], lg[:, a, :]))
                run(dve.tensor_copy(idx, top_index[:, :, :]))
                run(tt(small[:, 6:8], top[:, :, 1], top[:, :, 0], SUB), RT_V, "gap")
                dve.wait_ge(RT_A.sem, RT_A.at("exp"))
                run(ts(small[:, 8:10], small[:, 4:6], 1.0, None, ADD))
                run(dve.reciprocal(small[:, 8:10], small[:, 8:10]))
                run(tt(small[:, 10:12], small[:, 8:10], small[:, 4:6], MUL))
                run(dve.memset(w(5504, 96), 0.0))
                for a in range(TT):
                    tmp = small[:, 160:160 + NE]
                    run(ts(router_gates[:, a, :], const("experts"), idx[:, a, 0:1], small[:, 8 + a:9 + a],
                           ALU.is_equal, MUL))
                    run(ts(tmp, const("experts"), idx[:, a, 1:2], small[:, 10 + a:11 + a], ALU.is_equal, MUL))
                    run(tt(router_gates[:, a, :], router_gates[:, a, :], tmp, ADD))
                    run(ts(tmp, const("experts"), idx[:, a, 0:1], None, ALU.is_equal))
                    ins = stt(chosen[:, a, 0:NE], const("experts"), idx[:, a, 1:2], tmp, ALU.is_equal, ADD)
                    if a:
                        run(ins, RT_V, "chosen")
                    else:
                        run(ins)
                run(dve.tensor_copy(gate_of[:, :, 0:NE], router_gates[:, :, :]))
                dve.wait_ge(RT_P.sem, RT_P.at("slots"))
                run(dve.tensor_copy(slot[:, :, 0:NE], grid(bank(1)[:, 0:2 * NE], 2)))
                run(dve.tensor_reduce(small[:, 12:13], bank(1)[:, 2 * NE:3 * NE], AX, MAX))
                run(ts(crowded[:, :], small[:, 12:13], float(CAP), None, ALU.is_gt), RT_V, "flag")

            def select(dst, weight, e):
                for a in range(TT):
                    ins = ts(dst[:, a, :], const("slots"), slot[:, a, bass.ds(e, 1)], weight[:, a, bass.ds(e, 1)],
                             ALU.is_equal, MUL)
                return ins

            def take_inputs():
                src = banks[:, 4:6, 0:4 * CAP].rearrange("p b (k s) -> p b k s", k=4)
                gain = par("norm_ffn1", 0, KT).rearrange("p (b k) -> p b k", b=2).unsqueeze(3)
                tt(gathered.rearrange("p (b k) s -> p b k s", b=2), src, gain.to_broadcast([P, 2, 4, CAP]),
                   MUL).then_inc(sp_inputs, 1)

            def add_scattered(e):
                dve.wait_ge(sp_scattered, e + 1)
                dve.wait_ge(sp_added, 4 * e + 1)
                for b in range(4):
                    xs = x[:, b // 2, (b % 2) * 512:(b % 2) * 512 + 512]
                    tt(xs, xs, bank(b), ADD).then_inc(sp_added, 1)

            def experts_short():
                first = FIRST_EXPERT["moe"]
                dve.memset(result, 0.0).then_inc(sp_copied, 1)
                dve.memset(sel_turned, 0.0).then_inc(sp_turned, 1)
                dve.memset(small[:, 13:14], 0.0).then_inc(sp_added, 1)
                select(sel, chosen, 0).then_inc(sp_selected, 1)
                dve.wait_ge(sp_gathered, 1)
                take_inputs()
                with dve.Fori(0, NE) as e:
                    dve.wait_ge(sp_gathered, e + 1)
                    select(sel_gate, gate_of, e)
                    select(sel, chosen, e + 1).then_inc(sp_selected, 1)
                    for t in range(FT):
                        dve.wait_ge(glu_silu, (e + first) * FT + t + 1)
                        tt(w(t * CAP, CAP), glu[:, t % 2, 0:CAP], banks[:, 6 + t % 2, P:P + CAP], MUL)\
                            .then_inc(glu_done, 1)
                        if t == 6:
                            add_scattered(e)
                    dve.wait_ge(sp_gathered, e + 2)
                    take_inputs()
                add_scattered(NE)
                dve.wait_ge(sp_added, 4 * NE + 5)
                dve.sem_inc(ffn_added, 4 * NE)

            def ffn(name, gates_):
                first = FIRST_EXPERT[name]
                with dve.Fori(0, N_PARTS[name]) as e:
                    for t in range(FT):
                        dve.wait_ge(glu_silu, (e + first) * FT + t + 1)
                        tt(w(t * T, T), glu[:, t % 2, :], banks[:, 4 + t % 4, T:2 * T], MUL).then_inc(glu_done, 1)
                    dve.wait_ge(slab_used, e * EXPERT_SLABS + LAST_MOE_SLAB)
                    dve.wait_ge(ffn_added, (e + first) * 4 + 1)
                    for b in range(4):
                        xs = x[:, b // 2, (b % 2) * 512:(b % 2) * 512 + 512]
                        stt(xs, banks[:, b, :], gates_[:, b // 2, bass.ds(e, 1)], xs, MUL, ADD).then_inc(ffn_added, 1)
                dve.wait_ge(ffn_added, 4 * (first + N_PARTS[name]) + 1)

            def lru():
                lam = par("a_lambda", 0, KT)
                e, s, s2, acc, cl = (small[:, 16 + 8 * i:24 + 8 * i] for i in range(5))
                dve.wait_ge(LR_A.sem, LR_A.at("lambda"))
                run(ts(s, e, 2.0, None, ADD))
                run(dve.reciprocal(s, s))
                run(tt(s, s, e, MUL))
                run(tt(s2, s, s, MUL))
                run(ts(acc, s2, 1.0 / 17, 1.0 / 15, MUL, ADD))
                for n in (13, 11, 9, 7, 5, 3, 1):
                    run(tt(acc, acc, s2, MUL))
                    run(ts(acc, acc, 1.0 / n, None, ADD))
                run(tt(acc, acc, s, MUL))
                run(ts(cl, lam, -1.0, 0.0, MUL, MAX))
                run(stt(cl, acc, 2.0, cl, MUL, ADD))
                run(ts(cl, cl, -LRU_C, None, MUL))
                run(ts(small[:, 56:64], cl, -1.0, None, MUL), LR_V, "rate")
                z = w(2048, KT, T + 4)
                xr = w(6144, KT, T)
                run(dve.memset(z[:, :, 0:3], 0.0))
                for q in range(4):
                    dve.wait_ge(ain_out, 5 + q)
                    for i in range(TAPS2):
                        for k in range(2 * q, 2 * q + 2):
                            wk = par("a_conv_w", k * TAPS2 + i)
                            if i == 0:
                                ins = ts(xr[:, k, :], z[:, k, i:i + T], wk, par("a_conv_b", k), MUL, ADD)
                            else:
                                ins = stt(xr[:, k, :], z[:, k, i:i + T], wk, xr[:, k, :], MUL, ADD)
                        if i < TAPS2 - 1:
                            run(ins)
                        else:
                            chain.to(ins, lru_conv, q + 1)
                for i in range(2):
                    r2, gi, a, th, xr, y = (w(at + 1024 * i, 1024) for at in (8192, 10240, 12288, 14336, 6144, 0))
                    dve.wait_ge(ag_out, 4 * i + 4)
                    run(tt(gi, gi, xr, MUL))
                    dve.wait_ge(LR_A.sem, LR_A.at(f"exps{i}"))
                    run(tt(r2, a, a, MUL))
                    run(stt(th, r2, 1.0, th, ADD, MUL), LR_V, f"square{i}")
                    dve.wait_ge(LR_A.sem, LR_A.at(f"root{i}"))
                    run(tt(gi, gi, th, MUL))
                    for h in range(KT // 2):
                        s_ = slice(h * T, h * T + T)
                        ins = dve.tensor_tensor_scan(r2[:, s_], a[:, s_], gi[:, s_], 0.0, MUL, ADD)
                    run(ins)
                    run(tt(xr, r2, y, MUL), LR_V, f"done{i}")

            def query_squares(i):
                dve.wait_ge(Q_A.sem, Q_A.at(f"out{2 * i + 1}"))
                q = w(QR + 1024 * i, 1024)
                run(tt(w(QSQ + 1024 * i, 1024), q, q, MUL), Q_V, f"squares{i}")

            def query_norm(i):
                q, root = w(QR + 1024 * i, 1024), w(QSQ + 1024 * i, 1024)
                dve.wait_ge(Q_A.sem, Q_A.at(f"norm{i}"))
                run(dve.reciprocal(root, root))
                run(stt(q, q, par("q_norm"), root, MUL, MUL), Q_V, f"normed{i}")

            def query_rope(i):
                dve.wait_ge(Q_P.sem, Q_P.at(f"rot{i}"))
                rotate(w(QR + 1024 * i, 4, T), grid(bank(Q_BANK[2 * i], 2), 4), const("cos"), const("sin"),
                       w(QSQ + 1024 * i, 4, T), 4, Q_V, f"rope{i}")

            def keys_and_queries():
                dve.wait_ge(NORM_A.sem, NORM_A.at("hT", 6))
                for k in range(KT):
                    ins = ts(w(HB + k * T, T), bank(k // 2)[:, (k % 2) * T:(k % 2) * T + T], par("b_norm", k), None, MUL)
                run(ins, Q_V, "input")
                dve.wait_ge(kv_out, 2)
                for v in range(2):
                    src = w(KC + 1024 * v, G, T).rearrange("p g (n s) -> p s g n", s=CS)
                    for j in range(2):
                        pos = par("cmp_pos", 16 * v + 8 * j, 8).unsqueeze(2).unsqueeze(3).to_broadcast([P, 8, G, NC])
                        ins = tt(w(EXW + 960 * v + 480 * j, 8, G, NC), src[:, 0::2, :, j:j + NC], pos, ADD)
                run(ins, KV_V, "windows")
                dve.wait_ge(kv_out, 4)
                k, root = w(KR, 1024), w(KSQ, 1024)
                run(tt(root, k, k, MUL), KV_V, "k_squares")
                dve.wait_ge(KV_A.sem, KV_A.at("k_norm"))
                run(dve.reciprocal(root, root))
                for b in range(2):
                    kb = k[:, 512 * b:512 * b + 512]
                    ins = stt(kb, kb, par("k_norm", 1 + b), root[:, 512 * b:512 * b + 512], MUL, MUL)
                run(ins, KV_V, "k_normed")
                query_squares(0)
                dve.wait_ge(KV_P.sem, KV_P.at("k_rot"))
                rotate(w(KR, 4, T), grid(bank(2, 2), 4), const("cos"), const("sin"), w(KSQ, 4, T), 4,
                       KV_V, "k_rope")
                query_norm(0)
                dve.wait_ge(KV_A.sem, KV_A.at("k_cmp"))
                k, sq = w(KCM, G * NC), w(EXW, G * NC)
                run(tt(sq, k, k, MUL), KV_V, "cmp_squares")
                query_rope(0)
                query_squares(1)
                dve.wait_ge(KV_A.sem, KV_A.at("cmp_norm"))
                run(dve.reciprocal(sq, sq))
                run(stt(k, k, par("k_norm", 0), sq, MUL, MUL), KV_V, "cmp_normed")
                query_norm(1)
                dve.wait_ge(KV_P.sem, KV_P.at("cmp_rot"))
                rotate(w(KCM, G, NC), grid(bank(2)[:, 0:G * NC], G), const("cos_cmp"), const("sin_cmp"),
                       w(EXW, G, NC), G, KV_V, "cmp_rope")
                dve.wait_ge(KV_P.sem, KV_P.at("v_cmp"))
                r = slice(0, NC)
                run(dve.tensor_copy(w(VCM, G * HD, rows=r), bank(3, rows=r)[:, 0:G * HD]), KV_V, "v_cmp")
                query_rope(1)

            def at_mask(k):
                g, a, b = TASKS[k]
                n = P * (a + 1)
                at, _ = CONSTS["causal_add"]
                mask = consts[:, at + (1 - a) * P:at + 2 * P]
                dve.wait_ge(at_scores, k + 1)
                if k >= 3:
                    dve.wait_ge(at_turned, k - 2)
                s = at_s(k)
                for r in range(2):
                    ins = stt(s[:, 2 * r:2 * r + 2, :], grid(bank(2 * (k % 2) + r)[:, 0:2 * n], 2), HD ** -0.5,
                              bc(mask, 2), MUL, ADD)
                run(ins)
                c = 4 * (k % 3)
                dve.tensor_reduce(small[:, 32 + c:36 + c], s, AX, MAX, negate=True).then_inc(at_masked, 1)

            def at_norm(k):
                g, a, b = TASKS[k]
                c = 4 * (k % 3)
                dve.wait_ge(at_exps, k + 1)
                wt = small[:, 48 + c:52 + c]
                run(dve.reciprocal(wt, wt))
                ga = w(GA + 48 * a, 3, 16)[:, b + 1, 4 * g:4 * g + 4].rearrange("p (t r) -> p r t", t=2)
                run(tt(grid(wt, 2), grid(wt, 2), ga, MUL))
                s = at_s(k)
                tt(s, s, wt.unsqueeze(2).to_broadcast([P, 4, P * (a + 1)]), MUL).then_inc(at_probs, 1)

            def cmp_mask():
                dve.wait_ge(CA_P.sem, CA_P.at("scores"))
                for r in range(2):
                    for a in range(TT):
                        src = grid(bank(4 + r)[:, 8 * a * NC:8 * (a + 1) * NC], 8)
                        mask = bc(grid(const("cmp_add"), 2)[:, a, :], 8)
                        ins = stt(w(CMP_S + 240 * r + 120 * a, 8, NC), src, HD ** -0.5, mask, MUL, ADD)
                run(ins)
                s = w(CMP_S, 32, NC)
                run(dve.tensor_reduce(small[:, 64:96], s, AX, MAX))
                run(tt(s, s, small[:, 64:96].unsqueeze(2).to_broadcast([P, 32, NC]), SUB), CA_V, "shifted")

            def cmp_norm():
                dve.wait_ge(CA_A.sem, CA_A.at("exps"))
                s, wt = w(CMP_S, 32, NC), small[:, 96:128]
                run(dve.tensor_reduce(wt, s, AX, ADD))
                run(dve.reciprocal(wt, wt))
                for r in range(2):
                    wr = grid(wt, 2)[:, r, :]
                    ga = w(GA, 2, 3, 16)[:, :, 0, :].rearrange("p a (j r) -> p a j r", r=2)[:, :, :, r]
                    ins = tt(grid(wr, 2), grid(wr, 2), ga, MUL)
                run(ins)
                for r in range(2):
                    for a in range(TT):
                        sr = w(CMP_S + 240 * r + 120 * a, 8, NC)
                        ins = tt(sr, sr, bc(grid(const("cmp_keep"), 2)[:, a, :], 8), MUL)
                run(ins)
                run(tt(s, s, wt.unsqueeze(2).to_broadcast([P, 32, NC]), MUL), CA_V, "probs")

            def attention():
                at_mask(0)
                cmp_mask()
                at_mask(1)
                cmp_norm()
                for k in range(len(TASKS)):
                    if k:
                        if k + 1 < len(TASKS):
                            at_mask(k + 1)
                    at_norm(k)

            for l in range(2):
                norm(2 * l, f"norm_mix{l}")
                mixers(l)
                project(l)
                norm(2 * l + 1, f"norm_ffn{l}")
                if l == 0:
                    ffn_split("dense")
                else:
                    route()
                    with dve.If(dve.value_load(crowded[0:1, 0:1], min_val=0, max_val=1) == 0):
                        experts_short()
                    with dve.Else():
                        ffn("moe", router_gates)
            norm(4, "a_norm")
            lru()
            project(2)
            norm(5, "f_norm0")
            ffn_split("f0")
            norm(6, "kv_norm")
            keys_and_queries()
            attention()
            project(3)
            norm(7, "f_norm1")
            ffn_split("f1")


def kernel(**inputs):
    import concourse.bacc as bacc
    from concourse.bass_utils import run_bass_kernel_spmd

    a = {name: np.asarray(v) for name, v in inputs.items()}
    arrays = {"weights_in": weight_stream(a), "consts_in": constant_arrays(), "params_in": parameter_array(a),
              "x_in": np.ascontiguousarray(a["x"])}
    nc = bacc.Bacc("TRN2", target_bir_lowering=False, num_devices=1)
    aps = [nc.dram_tensor(name, v.shape, F32, kind="ExternalInput").ap() for name, v in arrays.items()]
    out = nc.dram_tensor("out", (1, T, D), F32, kind="ExternalOutput").ap()
    build(nc, *aps, out)
    return run_bass_kernel_spmd(nc, [arrays], core_ids=[0]).results[0]["out"]
```
